# Optimizing a Trainium2 kernel written in Bass

```python
import math
import jax, jax.numpy as jnp
from jax import lax
import numpy as np

D_MODEL = 1024
BATCH = 1
SEQ = 256
DEPTH = 2

D_MIX = D_MODEL
ATTN_HEADS = 8
HEAD_DIM = 64
ATTN_WIDTH = ATTN_HEADS * HEAD_DIM
SSD_HEADS = 8
SSD_HEAD_DIM = 64
SSD_WIDTH = SSD_HEADS * SSD_HEAD_DIM
SSD_GROUPS = 2
SSD_STATE = 128
CONV_K = 4
CHUNK = 128
Q_BLOCK = 128
CONV_DIM = SSD_WIDTH + 2 * SSD_GROUPS * SSD_STATE
D_IN_PROJ = 3 * ATTN_WIDTH + SSD_WIDTH + CONV_DIM + SSD_HEADS
D_FF = 2816
N_EXPERTS = 8
TOP_K = 2
D_FF_EXPERT = 3584
N_DENSE = (DEPTH + 1) // 2
N_MOE = DEPTH // 2
EPS = 1e-5

kernel_name = "hymba_sbattn_ssd_moe_block"

def rmsnorm(x, g):
    xf = x.astype(jnp.float32)
    var = jnp.mean(xf * xf, axis=-1, keepdims=True)
    return (xf * lax.rsqrt(var + EPS) * g.astype(jnp.float32)).astype(x.dtype)

def stick_breaking_attention(q, k, v):
    seq = q.shape[1]
    scale = HEAD_DIM ** -0.5
    outs = []
    for blk in range(seq // Q_BLOCK):
        q0 = blk * Q_BLOCK
        q1 = q0 + Q_BLOCK
        qb = q[:, q0:q1]
        kb = k[:, :q1]
        vb = v[:, :q1]
        z = jnp.einsum("bthd,bshd->bhts", qb, kb).astype(jnp.float32) * scale
        t_pos = q0 + jnp.arange(Q_BLOCK)[:, None]
        s_pos = jnp.arange(q1)[None, :]
        causal = s_pos < t_pos
        neg_log_1m_beta = jnp.where(causal, jax.nn.softplus(z), 0.0)
        later = lax.cumsum(neg_log_1m_beta, axis=3, reverse=True) - neg_log_1m_beta
        w = jnp.where(causal, jnp.exp(jax.nn.log_sigmoid(z) - later), 0.0)
        outs.append(jnp.einsum("bhts,bshd->bthd", w.astype(v.dtype), vb))
    return jnp.concatenate(outs, axis=1)

def segsum(a):
    t = a.shape[-1]
    ar = jnp.broadcast_to(a[..., :, None], a.shape + (t,))
    strict = jnp.tril(jnp.ones((t, t), dtype=bool), -1)
    cs = jnp.cumsum(jnp.where(strict, ar, 0.0), axis=-2)
    incl = jnp.tril(jnp.ones((t, t), dtype=bool), 0)
    return jnp.where(incl, cs, -jnp.inf)

def ssd_chunked(x, dt, a, b_in, c_in):
    bsz, seq = x.shape[0], x.shape[1]
    nc = seq // CHUNK
    r = SSD_HEADS // SSD_GROUPS
    xc = (x * dt[..., None]).reshape(bsz, nc, CHUNK, SSD_GROUPS, r, SSD_HEAD_DIM)
    ac = (dt * a).reshape(bsz, nc, CHUNK, SSD_GROUPS, r).transpose(0, 3, 4, 1, 2)
    bc = b_in.reshape(bsz, nc, CHUNK, SSD_GROUPS, SSD_STATE)
    cc = c_in.reshape(bsz, nc, CHUNK, SSD_GROUPS, SSD_STATE)
    a_cum = jnp.cumsum(ac, axis=-1)
    decay = jnp.exp(segsum(ac))
    cb = jnp.einsum("bclgn,bcsgn->bgcls", cc, bc)
    y_diag = jnp.einsum("bgcls,bgrcls,bcsgrp->bclgrp", cb, decay, xc)
    decay_states = jnp.exp(a_cum[..., -1:] - a_cum)
    states = jnp.einsum("bclgn,bgrcl,bclgrp->bcgrpn", bc, decay_states, xc)
    states = jnp.concatenate([jnp.zeros_like(states[:, :1]), states], axis=1)
    last = jnp.pad(a_cum[..., -1], ((0, 0), (0, 0), (0, 0), (1, 0)))
    chunk_decay = jnp.exp(segsum(last))
    new_states = jnp.einsum("bgrzc,bcgrpn->bzgrpn", chunk_decay, states)
    states = new_states[:, :-1]
    y_off = jnp.einsum("bclgn,bcgrpn,bgrcl->bclgrp", cc, states, jnp.exp(a_cum))
    return (y_diag + y_off).reshape(bsz, seq, SSD_HEADS, SSD_HEAD_DIM)

def causal_depthwise_conv(u, w, b):
    out = lax.conv_general_dilated(
        u, w[:, None, :].astype(u.dtype), window_strides=(1,), padding=[(CONV_K - 1, 0)],
        dimension_numbers=("NWC", "WIO", "NWC"), feature_group_count=CONV_DIM)
    return out + b.astype(u.dtype)

def hybrid_mixer(h, w_in, conv_w, conv_b, dt_bias, a_log, d_skip, attn_norm_g, ssd_norm_g, w_out):
    bsz, seq = h.shape[0], h.shape[1]
    proj = h @ w_in
    o1 = ATTN_WIDTH
    o2 = o1 + ATTN_WIDTH
    o3 = o2 + ATTN_WIDTH
    o4 = o3 + SSD_WIDTH
    o5 = o4 + CONV_DIM
    q, k, v, z, xbc, dt_raw = jnp.split(proj, [o1, o2, o3, o4, o5], axis=-1)
    hs = (bsz, seq, ATTN_HEADS, HEAD_DIM)
    attn = stick_breaking_attention(q.reshape(hs), k.reshape(hs), v.reshape(hs))
    attn = rmsnorm(attn.reshape(bsz, seq, ATTN_WIDTH), attn_norm_g)
    xbc = jax.nn.silu(causal_depthwise_conv(xbc, conv_w, conv_b))
    xs, bs, cs = jnp.split(xbc, [SSD_WIDTH, SSD_WIDTH + SSD_GROUPS * SSD_STATE], axis=-1)
    xs = xs.astype(jnp.float32).reshape(bsz, seq, SSD_HEADS, SSD_HEAD_DIM)
    bs = bs.astype(jnp.float32).reshape(bsz, seq, SSD_GROUPS, SSD_STATE)
    cs = cs.astype(jnp.float32).reshape(bsz, seq, SSD_GROUPS, SSD_STATE)
    dt = jax.nn.softplus(dt_raw.astype(jnp.float32) + dt_bias.astype(jnp.float32))
    a = -jnp.exp(a_log.astype(jnp.float32))
    y = ssd_chunked(xs, dt, a, bs, cs) + d_skip.astype(jnp.float32)[:, None] * xs
    y = y.reshape(bsz, seq, SSD_WIDTH) * jax.nn.silu(z.astype(jnp.float32))
    yg = y.reshape(bsz, seq, SSD_GROUPS, SSD_WIDTH // SSD_GROUPS)
    yg = yg * lax.rsqrt(jnp.mean(yg * yg, axis=-1, keepdims=True) + EPS)
    y = (yg.reshape(bsz, seq, SSD_WIDTH) * ssd_norm_g.astype(jnp.float32)).astype(h.dtype)
    return jnp.concatenate([attn, y], axis=-1) @ w_out

def swiglu(h, wg, wu, wd):
    return (jax.nn.silu(h @ wg) * (h @ wu)) @ wd

def moe_swiglu(h, router_w, wg, wu, wd):
    logits = (h @ router_w).astype(jnp.float32)
    top_vals, top_idx = lax.top_k(logits, TOP_K)
    top_w = jax.nn.softmax(top_vals, axis=-1)
    gates = jnp.sum(jax.nn.one_hot(top_idx, N_EXPERTS, dtype=jnp.float32) * top_w[..., None], axis=-2)
    gates = gates.astype(h.dtype)
    out = jnp.zeros_like(h)
    for e in range(N_EXPERTS):
        out = out + gates[..., e:e + 1] * swiglu(h, wg[e], wu[e], wd[e])
    return out

def setup_inputs(seed: int = 0) -> dict:
    key = jax.random.key(seed)
    ks = jax.random.split(key, 24)
    f32 = jnp.float32

    def nrm(k, shape, fan_in):
        return jax.random.normal(k, shape, f32) * (fan_in ** -0.5)

    def gain(k, shape):
        return 1.0 + 0.02 * jax.random.normal(k, shape, f32)

    dt0 = jnp.exp(jax.random.uniform(ks[5], (DEPTH, SSD_HEADS), f32, math.log(1e-3), math.log(1e-1)))
    dt_bias = dt0 + jnp.log(-jnp.expm1(-dt0))
    return {
        "x": jax.random.normal(ks[0], (BATCH, SEQ, D_MODEL), f32),
        "mix_norm_g": gain(ks[1], (DEPTH, D_MODEL)),
        "w_in": nrm(ks[2], (DEPTH, D_MODEL, D_IN_PROJ), D_MODEL),
        "conv_w": nrm(ks[3], (DEPTH, CONV_K, CONV_DIM), CONV_K),
        "conv_b": 0.01 * jax.random.normal(ks[4], (DEPTH, CONV_DIM), f32),
        "dt_bias": dt_bias,
        "a_log": jnp.log(jax.random.uniform(ks[6], (DEPTH, SSD_HEADS), f32, 1.0, 16.0)),
        "d_skip": gain(ks[7], (DEPTH, SSD_HEADS)),
        "attn_norm_g": gain(ks[8], (DEPTH, ATTN_WIDTH)),
        "ssd_norm_g": gain(ks[9], (DEPTH, SSD_WIDTH)),
        "w_out": nrm(ks[10], (DEPTH, D_MIX, D_MODEL), D_MIX),
        "ffn_norm_g": gain(ks[11], (DEPTH, D_MODEL)),
        "dense_w_gate": nrm(ks[12], (N_DENSE, D_MODEL, D_FF), D_MODEL),
        "dense_w_up": nrm(ks[13], (N_DENSE, D_MODEL, D_FF), D_MODEL),
        "dense_w_down": nrm(ks[14], (N_DENSE, D_FF, D_MODEL), D_FF),
        "router_w": nrm(ks[15], (N_MOE, D_MODEL, N_EXPERTS), D_MODEL),
        "moe_w_gate": nrm(ks[16], (N_MOE, N_EXPERTS, D_MODEL, D_FF_EXPERT), D_MODEL),
        "moe_w_up": nrm(ks[17], (N_MOE, N_EXPERTS, D_MODEL, D_FF_EXPERT), D_MODEL),
        "moe_w_down": nrm(ks[18], (N_MOE, N_EXPERTS, D_FF_EXPERT, D_MODEL), D_FF_EXPERT),
        "final_norm_g": gain(ks[19], (D_MODEL,)),
    }

def reference(x, mix_norm_g, w_in, conv_w, conv_b, dt_bias, a_log, d_skip, attn_norm_g, ssd_norm_g,
              w_out, ffn_norm_g, dense_w_gate, dense_w_up, dense_w_down, router_w, moe_w_gate,
              moe_w_up, moe_w_down, final_norm_g):
    for layer in range(DEPTH):
        h = rmsnorm(x, mix_norm_g[layer])
        x = x + hybrid_mixer(h, w_in[layer], conv_w[layer], conv_b[layer], dt_bias[layer], a_log[layer],
                             d_skip[layer], attn_norm_g[layer], ssd_norm_g[layer], w_out[layer])
        h = rmsnorm(x, ffn_norm_g[layer])
        i = layer // 2
        if layer % 2 == 0:
            x = x + swiglu(h, dense_w_gate[i], dense_w_up[i], dense_w_down[i])
        else:
            x = x + moe_swiglu(h, router_w[i], moe_w_gate[i], moe_w_up[i], moe_w_down[i])
    return rmsnorm(x, final_norm_g)


_drawn_inputs = setup_inputs


def setup_inputs(seed=0):
    import zlib

    import numpy as np

    out = dict(_drawn_inputs(seed))
    spreads = {}
    factors = {'conv_b': 3.819,
     'd_skip': 3.335,
     'ssd_norm_g': 2.74,
     'final_norm_g': 8.013,
     'attn_norm_g': 3.405,
     'ffn_norm_g': 3.325}
    for name, (base, spread) in spreads.items():
        noise = np.random.default_rng([zlib.crc32(name.encode()), seed]).standard_normal(out[name].shape)
        drawn = base * np.exp(spread * noise) if base else spread * noise
        out[name] = __import__('jax').numpy.asarray(drawn.astype(out[name].dtype))
    for name, factor in factors.items():
        out[name] = (out[name] * factor).astype(out[name].dtype)
    return out
```

```python
import numpy as np

import concourse.bass as bass
from concourse import mybir
from contextlib import ExitStack

ALU = mybir.AluOpType
ACT = mybir.ActivationFunctionType
AX = mybir.AxisListType
F32 = mybir.dt.float32
F32R = mybir.dt.float32r
I32 = mybir.dt.int32

P = 128
BANK = 512
EPS = 1e-5
RAW_RING = 14
PIECE = 1024
BLOCK = 2 * PIECE


def hybrid_trunk(nc, x, mix_norm_g, w_in, conv_w, conv_b, dt_bias, a_log, d_skip, attn_norm_g, ssd_norm_g,
                 w_out, ffn_norm_g, dense_w_gate, dense_w_up, dense_w_down, router_w, moe_w_gate,
                 moe_w_up, moe_w_down, final_norm_g, out):
    _, T, D = x.shape
    L = w_in.shape[0]
    TB, KT = T // P, D // P
    HEADS = dt_bias.shape[1]
    AW = attn_norm_g.shape[1]
    HD = AW // HEADS
    TAPS, CONV = conv_w.shape[1], conv_w.shape[2]
    CT = CONV // P
    XT = AW // P
    GROUPS = (CT - XT) // 2
    HG = HEADS // GROUPS
    GW = AW // GROUPS
    FF = dense_w_gate.shape[2]
    E, FE = moe_w_gate.shape[1], moe_w_gate.shape[3]
    TOPK = 2
    MORE = TOPK * T // (P + 1)
    ITEMS = E + MORE + 1
    OQ, OK_, OV, OZ = 0, AW, 2 * AW, 3 * AW
    OX, OBC = 4 * AW, 5 * AW
    ODT = OX + CONV
    assert (TB, KT, HEADS, HD, CT, XT, GROUPS, TAPS) == (2, 8, 8, 64, 8, 4, 2, 4) and L == 2 and AW == BANK

    DS = 256
    DSTEPS = FF // DS
    ES = 512
    ESTEPS = FE // ES

    def in_proj_blocks(l):
        w = w_in[l].rearrange("(c p) n -> p c n", p=P)
        return [w[:, 4 * h:4 * h + 4, o:o + BANK] for o in (OX, OBC, OQ, OK_, OV, OZ) for h in range(2)]

    def out_proj_blocks(l):
        w = w_out[l].rearrange("(c p) n -> p c n", p=P)
        return [w[:, 4 * h:4 * h + 4, o:o + BANK] for o in (0, BANK) for h in range(2)]

    def dense_blocks():
        wg = dense_w_gate[0].rearrange("(c p) n -> p c n", p=P)
        wu = dense_w_up[0].rearrange("(c p) n -> p c n", p=P)
        wd = dense_w_down[0].rearrange("(j p c) n -> j p c n", p=P, c=DS // P)
        blocks = []
        for j in range(DSTEPS):
            blocks += [wg[:, :, j * DS:j * DS + DS], wu[:, :, j * DS:j * DS + DS]]
            if j >= 1:
                blocks.append(wd[j - 1])
        return blocks + [wd[DSTEPS - 1]]

    def expert_blocks(e):
        pick = lambda w: w[0, bass.ds(e, 1)]
        wg = pick(moe_w_gate).rearrange("o (c p) n -> p (o c) n", p=P)
        wu = pick(moe_w_up).rearrange("o (c p) n -> p (o c) n", p=P)
        wd = pick(moe_w_down).rearrange("o (j p c) n -> j p (o c) n", p=P, c=ES // P)
        blocks = []
        for j in range(ESTEPS):
            blocks += [w[:, 4 * h:4 * h + 4, j * ES:j * ES + ES] for w in (wg, wu) for h in range(2)]
            if j >= 1:
                blocks += [wd[j - 1][:, 2 * h:2 * h + 2] for h in range(2)]
        return blocks + [wd[ESTEPS - 1][:, 2 * h:2 * h + 2] for h in range(2)]

    N_IN, N_OUT, N_DENSE, N_ITEM = 24, 8, 6 * DSTEPS, 12 * ESTEPS
    fixed_blocks = []
    seg = {}
    slot_of, prev_user = [], []

    def add_segment(name, blocks, ring):
        seg[name] = 2 * len(fixed_blocks)
        fixed_blocks.extend(blocks)
        for q in range(2 * len(blocks)):
            slot_of.append(q % ring)

    add_segment("in0", in_proj_blocks(0), 4)
    add_segment("out0", out_proj_blocks(0), 4)
    add_segment("dense", dense_blocks(), 6)
    add_segment("in1", in_proj_blocks(1), 4)
    add_segment("out1", out_proj_blocks(1), 4)
    last = {}
    for n, s in enumerate(slot_of):
        prev_user.append(last.get(s, -1))
        last[s] = n
    for q in range(4, 6):
        prev_user[seg["dense"] + q] = seg["dense"] - 1
    M0 = len(slot_of)
    assert M0 % 2 == 0 and (N_ITEM // 2) % RAW_RING == 0 and N_ITEM % 6 == 0

    with ExitStack() as ctx:
        BASE = (nc.sbuf_base + 31) // 32 * 32
        cursor = [BASE]

        def area(size):
            at = cursor[0]
            cursor[0] += (size + 31) // 32 * 32
            assert cursor[0] <= nc.sbuf_usable_end, (cursor[0], nc.sbuf_usable_end)
            return at

        def at(name, shape, offset, dt=F32):
            return nc.alloc_sbuf_tensor_at(name, shape, dt, offset=offset)

        def size(shape):
            return 4 * int(np.prod(shape[1:]))

        class Region:
            def __init__(self, start, limit):
                self.next, self.end = start, start + limit

            def __call__(self, name, shape, dt=F32):
                t = at(name, shape, self.next, dt)
                self.next += (size(shape) + 31) // 32 * 32
                assert self.next <= self.end, (name, self.next - self.end)
                return t

        raw = at("raw", [P, RAW_RING, BLOCK], area(4 * RAW_RING * BLOCK))
        RING_BYTES = 6 * 2 * 4 * PIECE
        ring_at = area(RING_BYTES)
        w_hi = [at(f"w_hi{s}", [P, PIECE], ring_at + s * 8 * PIECE, F32R) for s in range(6)]
        w_lo = [at(f"w_lo{s}", [P, PIECE], ring_at + s * 8 * PIECE + 4 * PIECE, F32R) for s in range(6)]
        mixer_hT = [at(f"mixer_hT{s}", [P, KT, T], ring_at + (4 + s) * 8 * PIECE, F32R) for s in range(2)]
        scratch = Region(ring_at, RING_BYTES)
        seg_rhs = scratch("seg_rhs", [P, TB, HEADS, P])
        decay = scratch("decay", [P, TB, HEADS, P])
        x_tok = scratch("x_tok", [P, TB, AW])
        x_dt = scratch("x_dt", [P, TB, AW])
        cb_m = scratch("cb_m", [P, TB, GROUPS, P])
        x_state = scratch("x_state", [P, AW])
        state = scratch("state", [P, AW])
        b_tok = scratch("b_tok", [P, GROUPS, P])
        y_off = scratch("y_off", [P, AW])
        W3 = P * 3
        soft = [scratch(f"soft{s}", [P, 2, W3]) for s in range(2)]
        attn = Region(ring_at, size(seg_rhs.shape))
        rest = [attn(f"rest{s}", [P, 2, W3]) for s in range(2)]
        after_dec = Region(ring_at + size(seg_rhs.shape), size(decay.shape))
        prob = [after_dec(f"prob{s}", [P, 2, W3]) for s in range(2)]

        x_sb = at("x_sb", [P, TB, D], area(4 * TB * D))
        gain_at = area(4 * D)
        gain = at("gain", [P, D], gain_at)
        z_act = at("z_act", [P, TB, AW], gain_at)
        ident = at("ident", [P, P], area(512))
        tri_le = at("tri_le", [P, P], area(512))
        tri_lt = at("tri_lt", [P, P], area(512))
        tri_gt = at("tri_gt", [P, P], area(512))
        neg_ge = at("neg_ge", [P, P], area(512))
        neg_one = at("neg_one", [P, P], area(512))
        ones = at("ones", [P, P], area(512))
        stat = at("stat", [P, 8], area(32))
        rstd = at("rstd", [P, 8], area(32))
        plan = at("plan", [P, 1 + MORE], area(32), I32)
        work_at = cursor[0]
        WORK = nc.sbuf_usable_end // 32 * 32 - work_at
        mixer = Region(work_at, WORK)
        xn = mixer("xn", [P, TB, D])
        conv = at("conv", [P, CT, T], work_at)
        qT = mixer("qT", [P, XT, T])
        kT = mixer("kT", [P, XT, T])
        v_tok = mixer("v_tok", [P, TB, AW])
        PAD = TAPS - 1
        xbc = mixer("xbc", [P, CT, PAD + T])
        mix = at("mix", [P, TB, D], xbc.manual_sbuf_range[0])
        NCP = TAPS * CT + CT
        PARAM_BYTES = 4 * (L * NCP + 2 * L * KT * HEADS + 3 * L * HEADS)
        params = Region(work_at + WORK - PARAM_BYTES, PARAM_BYTES)
        conv_par = params("conv_par", [P, L * NCP])
        w_dt = [params(f"w_dt_{s}", [P, L, KT, HEADS], F32R) for s in range(2)]
        dt_par = params("dt_par", [P, 3, L, HEADS])
        w_dt_raw = mixer("w_dt_raw", [P, L, KT, HEADS])
        dt_a = mixer("dt_a", [P, TB, HEADS])
        dt_b = mixer("dt_b", [P, TB, HEADS])
        dt_v = mixer("dt_v", [P, TB, HEADS])
        dA = mixer("dA", [P, TB, HEADS])
        e_cum = mixer("e_cum", [P, HEADS])
        assert mixer.next <= work_at + WORK - PARAM_BYTES
        conv_raw = at("conv_raw", [L * NCP, P], v_tok.manual_sbuf_range[0])

        after_xn = work_at + size(xn.shape)
        dense = Region(after_xn, WORK - size(xn.shape))
        dense_hT = [dense(f"dense_hT{s}", [P, KT, T], F32R) for s in range(2)]
        dense_h = dense("dense_h", [P, TB, DS])
        dense_aT = [dense(f"dense_aT{s}", [P, DS // P, T], F32R) for s in range(2)]
        assert dense.next <= work_at + WORK - PARAM_BYTES
        moe = Region(after_xn, WORK - size(xn.shape))
        g_hT = [moe(f"g_hT{s}", [P, KT, P], F32R) for s in range(2)]
        r_hT = at("r_hT", [P, KT, T], after_xn)
        sg = moe("sg", [P, ES])
        act_h = moe("act_h", [P, ES])
        aT = [moe(f"aT{s}", [P, ES // P, P], F32R) for s in range(2)]
        y_sb = moe("y_sb", [P, D])
        pick = moe("pick", [P, TB, P])
        pick_g = moe("pick_g", [P, TB, P])
        place = moe("place", [P, T])
        slot_t = moe("slot_t", [P, TB, ITEMS])
        gate_t = moe("gate_t", [P, TB, ITEMS])
        slots = moe("slots", [P, P])
        route = Region(y_sb.manual_sbuf_range[0], size(y_sb.shape))
        low8 = route("low8", [P, E, E])
        router = route("router", [P, KT, E])
        logit = route("logit", [P, TB, E])
        cmp_a = route("cmp_a", [P, TB, E, E])
        cmp_b = route("cmp_b", [P, TB, E, E])
        rank = route("rank", [P, TB, E])
        chosen = route("chosen", [P, TB, E])
        e_gate = route("e_gate", [P, TB, E])
        r_max = route("r_max", [P, TB])
        count = route("count", [P, E])
        over = route("over", [P, E])
        o_rank = route("o_rank", [P, E])
        pos1 = route("pos1", [P, TB, E])
        tmp_e = route("tmp_e", [P, TB, E])
        sel = route("sel", [P, E])
        e_ids = route("e_ids", [P, E])
        plan_f = route("plan_f", [P, 1 + MORE])

        psum = ctx.enter_context(nc.psum_tensor("psum", [P, 8, BANK], F32))

        def bank(b, n=1):
            return psum[:, b:b + n, :]

        sems = {}

        def sem(name):
            if name not in sems:
                sems[name] = ctx.enter_context(nc.semaphore(name))
            return sems[name]

        landed = [sem(f"landed{s}") for s in range(RAW_RING)]
        hi_done = sem("hi_done")
        split = sem("split")
        used = sem("used")

        def piece_src(n):
            b = (n // 2) % RAW_RING
            return raw[:, b, (n % 2) * PIECE:(n % 2) * PIECE + PIECE]

        ZB = (0, 2, 6)
        GATHER_BANK = (7, 1)
        COMBINE = ((1, 3), (6, 7))
        diag = lambda t: t.rearrange("p (a n) -> p a n", n=P)[:, 0:3:2, :]

        def slot_in(n):
            return slot_of[n] if n < M0 else (n - M0) % 6

        def mm3(ps, a_hi, a_lo, b_hi, b_lo, start, stop):
            nc.tensor.matmul(ps, a_hi, b_hi, start=start, stop=False, skip_group_check=True)
            nc.tensor.matmul(ps, a_lo, b_hi, start=False, stop=False, skip_group_check=True)
            return nc.tensor.matmul(ps, a_hi, b_lo, start=False, stop=stop, skip_group_check=True)

        def mm(ps, a, b, start=True, stop=True):
            return nc.tensor.matmul(ps, a, b, start=start, stop=stop, skip_group_check=True)

        block = ctx.enter_context(nc.Block())

        @block.sync
        def _(sp):
            sp.dma_start(x_sb[:], x[0].rearrange("(b p) d -> p b d", p=P)).then_inc(sem("x_landed"), 16)
            for n, src in enumerate(fixed_blocks):
                if n >= RAW_RING:
                    sp.wait_ge(split, 2 * (n - RAW_RING) + 2)
                dst = raw[:, n % RAW_RING, :].rearrange("p (c n) -> p c n", c=src.shape[1])
                sp.dma_start(dst, src).then_inc(landed[n % RAW_RING], 16)

            def item(i, e):
                for b, src in enumerate(expert_blocks(e)):
                    n = M0 // 2 + b
                    sp.wait_ge(split, 2 * (n - RAW_RING) + 2 + i * N_ITEM)
                    dst = raw[:, n % RAW_RING, :].rearrange("p (c n) -> p c n", c=src.shape[1])
                    sp.dma_start(dst, src).then_inc(landed[n % RAW_RING], 16)

            with sp.Fori(0, E) as e:
                item(e, e)
            sp.wait_ge(sem("planned"), 1)
            items = sp.value_load(plan[0:1, 0:1], min_val=E, max_val=E + MORE)
            for q in range(MORE):
                with sp.If(items > E + q):
                    e = sp.value_load(plan[0:1, 1 + q:2 + q], min_val=0, max_val=E - 1)
                    item(E + q, e)
                with sp.Else():
                    pass
            sp.wait_ge(sem("normed"), 2 * L + 3)
            sp.dma_start(out[0].rearrange("(b p) d -> p b d", p=P), xn[:]).then_inc(sem("stored"), 16)
            sp.wait_ge(sem("stored"), 16)

        @block.gpsimd
        def _(pool):
            g = nc.gpsimd
            par = sem("params")
            g.dma_start(gain[:], mix_norm_g[0:1, :].broadcast_to([P, D])).then_inc(sem("gain"), 16)
            for l in range(L):
                g.dma_start(conv_raw[l * NCP:l * NCP + TAPS * CT, :],
                            conv_w[l].rearrange("k (c p) -> (k c) p", p=P)).then_inc(par, 16)
                g.dma_start(conv_raw[l * NCP + TAPS * CT:(l + 1) * NCP, :],
                            conv_b[l].rearrange("(c p) -> c p", p=P)).then_inc(par, 16)
            for l in range(L):
                g.dma_start(w_dt_raw[:, l], w_in[l].rearrange("(c p) n -> p c n", p=P)[:, :, ODT:ODT + HEADS]
                            ).then_inc(par, 16)
            for s, v in enumerate((dt_bias, a_log, d_skip)):
                flat = v.rearrange("l (o h) -> o (l h)", o=1)
                g.dma_start(dt_par[:, s].rearrange("p l h -> p (l h)"),
                            flat.broadcast_to([P, L * HEADS])).then_inc(par, 16)
            cst = sem("consts")
            g.memset(ones[:], 1.0).then_inc(cst, 1)
            g.memset(neg_one[:], -1.0).then_inc(cst, 1)
            pool.wait_ge(cst, 2)
            tri = [(ident, ones, ALU.is_equal, [[-1, P]], 1, 0), (tri_le, ones, ALU.is_ge, [[1, P]], -1, 0),
                   (tri_lt, ones, ALU.is_gt, [[1, P]], -1, 0), (tri_gt, ones, ALU.is_gt, [[-1, P]], 1, 0),
                   (neg_ge, neg_one, ALU.is_ge, [[-1, P]], 1, 0)]
            for dst, src, op, pattern, mult, base in tri:
                g.affine_select(out=dst[:], in_=src[:], pattern=pattern, compare_op=op, fill=0.0, base=base,
                                channel_multiplier=mult).then_inc(cst, 1)

            def load_gain(u, parts):
                pool.wait_ge(sem("normed"), u)
                for lo, hi, src in parts:
                    g.dma_start(gain[:, lo:hi], src.broadcast_to([P, hi - lo])).then_inc(sem("gain"), 16)

            for l in range(L):
                if l:
                    load_gain(3 * l, [(0, D, mix_norm_g[l:l + 1, :])])
                pool.wait_ge(sem("y_done"), TB * (l + 1))
                load_gain(3 * l + 1, [(0, AW, attn_norm_g[l:l + 1, :]), (AW, D, ssd_norm_g[l:l + 1, :])])
                load_gain(3 * l + 2, [(0, D, ffn_norm_g[l:l + 1, :])])
                if l == L - 1:
                    pool.wait_ge(sem("normed"), 3 * l + 2)
                    g.dma_start(router[:], router_w[0].rearrange("(c p) e -> p c e", p=P)
                                ).then_inc(sem("router_in"), 16)
                    g.affine_select(out=low8[:], in_=ones[:, 0:E * E].rearrange("p (a b) -> p a b", a=E),
                                    pattern=[[1, E], [-1, E]], compare_op=ALU.is_gt, fill=0.0, base=0,
                                    channel_multiplier=0).then_inc(cst, 1)
                    g.iota(slots[:], [[1, P]], base=0, channel_multiplier=0,
                           allow_small_or_imprecise_dtypes=True).then_inc(cst, 1)
                    g.iota(e_ids[:], [[1, E]], base=0, channel_multiplier=0,
                           allow_small_or_imprecise_dtypes=True).then_inc(cst, 1)
            load_gain(3 * L, [(0, D, final_norm_g.rearrange("(o d) -> o d", o=1))])

        CONSTS, ROUTE_CONSTS = 7, 10
        GAINS = [1, 3, 4, 5, 7, 8, 9]
        PARAMS = 16 * (2 * L + L + 3)

        @block.scalar
        def _(act):
            a = nc.scalar
            own = [0]

            def link(ins):
                own[0] += 1
                ins.then_inc(sem("act_chain"), 1)
                act.wait_ge(sem("act_chain"), own[0])

            def hi(n):
                if n % 2 == 0:
                    act.wait_ge(landed[n // 2 % RAW_RING], 16 * (n // 2 // RAW_RING + 1))
                if prev_user[n] >= 0:
                    act.wait_ge(used, prev_user[n] + 1)
                a.copy(w_hi[slot_of[n]][:], piece_src(n)).then_inc(hi_done, 1)

            def sum_squares(src, u):
                for b in range(TB):
                    ins = a.activation(xn[:, b], src[:, b], ACT.Square, accum_out=stat[:, b:b + 1])
                ins.then_inc(sem("squares"), 1)

            def inv_root(u, n):
                act.wait_ge(sem("variance"), u + 1)
                link(a.activation(rstd[:, 0:n], stat[:, 0:n], ACT.Ln))
                a.activation(rstd[:, 0:n], rstd[:, 0:n], ACT.Exp, scale=-0.5).then_inc(sem("rstd"), 1)

            def turn_hi(w, dst):
                for c in range(4):
                    act.wait_ge(sem("turned"), 4 * w + c + 1)
                    a.copy(dst[:, 2 * c:2 * c + 2, :], bank(4 + c)).then_inc(sem("turn_hi"), 1)

            def mixer_act(l):
                n0, o0 = seg[f"in{l}"], seg[f"out{l}"]
                if l == 0:
                    act.wait_ge(sem("x_landed"), 16)
                sum_squares(x_sb, 3 * l)
                inv_root(3 * l, TB)
                if l == 0:
                    act.wait_ge(sem("params"), PARAMS)
                    a.copy(w_dt[0][:], w_dt_raw[:]).then_inc(sem("w_dt_hi"), 1)
                    a.activation(dt_par[:, 1], dt_par[:, 1], ACT.Exp).then_inc(sem("exp_a"), 1)
                    act.wait_ge(sem("par_turned"), 1)
                    a.copy(conv_par[:], bank(0)[:, 0, 0:L * NCP]).then_inc(sem("par_out"), 1)
                for q in range(4):
                    hi(n0 + q)
                turn_hi(3 * l, mixer_hT[0])
                for grp in range(1, 7):
                    if grp < 6:
                        for q in range(4):
                            hi(n0 + 4 * grp + q)
                    done = grp - 1
                    act.wait_ge(used, n0 + 4 * done + 4)
                    src = bank(2 * (done % 2), 2)
                    tiles = src.rearrange("p b (c t) -> p (b c) t", c=2)
                    if done < 2:
                        ins = a.copy(xbc[:, 4 * done:4 * done + 4, PAD:], tiles)
                    elif done == 2:
                        ins = a.mul(qT[:], tiles, float(HD) ** -0.5)
                    elif done == 3:
                        ins = a.copy(kT[:], tiles)
                    elif done == 4:
                        ins = a.copy(v_tok[:], src)
                    else:
                        ins = a.activation(z_act[:], src, ACT.Silu)
                    ins.then_inc(sem("moved"), 1)
                    if done in (3, 4):
                        h = done - 3
                        act.wait_ge(sem("convolved"), 2 * l + h + 1)
                        a.activation(conv[:, 4 * h:4 * h + 4], conv[:, 4 * h:4 * h + 4], ACT.Silu
                                     ).then_inc(sem("conv_act"), 1)
                act.wait_ge(sem("dt_raw"), l + 1)
                link(a.activation(dt_a[:], dt_v[:], ACT.Abs))
                link(a.activation(dt_a[:], dt_a[:], ACT.Exp, scale=-1.0))
                a.activation(dt_a[:], dt_a[:], ACT.Ln, bias=1.0).then_inc(sem("dt_rest"), 1)
                act.wait_ge(used, n0 + N_IN)
                act.wait_ge(sem("tokened"), l + 1)
                a.copy(x_tok[:], bank(4, 2)).then_inc(sem("x_tok"), 1)
                for c in range(TB):
                    act.wait_ge(sem("segsum"), TB * l + c + 1)
                    a.activation(decay[:, c].rearrange("p h t -> p (h t)"),
                                 bank(2 * c, 2).rearrange("p b t -> p (b t)"), ACT.Exp).then_inc(sem("decay"), 1)
                act.wait_ge(sem("cum"), l + 1)
                a.activation(e_cum[:], psum[:, 4, 0:HEADS], ACT.Exp).then_inc(sem("e_cum"), 1)
                act.wait_ge(sem("stated"), l + 1)
                a.copy(state[:], bank(6)[:, 0]).then_inc(sem("state_out"), 1)

                def rest_part(p):
                    act.wait_ge(sem("scores"), 4 * l + p + 1)
                    z = bank(ZB[p % 3], 2)[:, :, 0:W3]
                    r = rest[p % 2]
                    if p >= 2:
                        act.wait_ge(sem("soft"), 4 * l + p - 1)
                    link(a.activation(r[:], z, ACT.Abs))
                    link(a.activation(r[:], r[:], ACT.Exp, scale=-1.0))
                    a.activation(r[:], r[:], ACT.Ln, bias=1.0).then_inc(sem("rest"), 1)

                def prob_part(p):
                    act.wait_ge(sem("cummed"), 4 * l + p + 1)
                    if p >= 2:
                        act.wait_ge(sem("pv"), 4 * l + p - 1)
                    else:
                        act.wait_ge(sem("y_done"), TB * (l + 1))
                    a.activation(prob[p % 2][:], bank(ZB[p % 3], 2)[:, :, 0:W3], ACT.Exp
                                 ).then_inc(sem("prob"), 1)

                rest_part(0)
                for p in range(HEADS // 2):
                    if p + 1 < HEADS // 2:
                        rest_part(p + 1)
                    prob_part(p)
                act.wait_ge(sem("pv"), 4 * (l + 1))
                a.copy(mix[:, :, 0:AW], bank(4, 2)).then_inc(sem("attended"), 1)
                act.wait_ge(sem("attended"), l + 1)
                act.wait_ge(sem("y_done"), TB * (l + 1))
                for b in range(TB):
                    for lo, w, col in ((0, AW, 0), (AW, GW, 1), (AW + GW, GW, 2)):
                        ins = a.activation(xn[:, b, lo:lo + w], mix[:, b, lo:lo + w], ACT.Square,
                                           accum_out=stat[:, 3 * b + col:3 * b + col + 1])
                ins.then_inc(sem("squares"), 1)
                inv_root(3 * l + 1, 6)
                for q in range(4):
                    hi(o0 + q)
                turn_hi(1 + 3 * l, mixer_hT[0])
                for q in range(4, 8):
                    hi(o0 + q)

            mixer_act(0)

            act.wait_ge(sem("x_added"), 1 * 4)
            sum_squares(x_sb, 2)
            inv_root(2, TB)
            d0 = seg["dense"]
            for q in range(4):
                hi(d0 + q)
            turn_hi(2, dense_hT[0])

            def a_hi(k, src, dst):
                act.wait_ge(sem("hidden_turned"), k + 1)
                a.copy(dst, src).then_inc(sem("a_hi"), 1)

            def gate_silu(pieces, src, dst):
                act.wait_ge(used, pieces)
                a.activation(dst, src, ACT.Silu).then_inc(sem("silu"), 1)

            T_BANK = 2
            for j in range(DSTEPS):
                base = d0 + (0 if j == 0 else 4 + 6 * (j - 1))
                for q in range(4 if j == 0 else 6):
                    if j == 0:
                        continue
                    hi(base + q)
                if j >= 1:
                    a_hi(j - 1, bank(T_BANK)[:, 0].rearrange("p (c t) -> p c t", c=2), dense_aT[0][:])
                gate_silu(base + 2, bank(0 if j % 2 == 0 else 3)[:, 0].rearrange("p (b n) -> p b n", b=2), dense_h[:])
            for q in range(N_DENSE - 2, N_DENSE):
                hi(d0 + q)
            a_hi(DSTEPS - 1, bank(T_BANK)[:, 0].rearrange("p (c t) -> p c t", c=2), dense_aT[0][:])

            act.wait_ge(sem("x_added"), 2 * 4)
            mixer_act(1)

            act.wait_ge(sem("x_added"), 3 * 4)
            sum_squares(x_sb, 5)
            inv_root(5, TB)
            for c in range(4):
                act.wait_ge(sem("turned"), 4 * 5 + c + 1)
                a.copy(r_hT[:, 2 * c:2 * c + 2, :], bank(4 + c)).then_inc(sem("router_hT"), 1)
            act.wait_ge(sem("logit_rel"), 1)
            a.activation(e_gate[:], logit[:], ACT.Exp).then_inc(sem("e_gate"), 1)

            def gather_hi(k, half, i):
                act.wait_ge(sem("gathered"), k)
                a.copy(g_hT[0][:, 4 * half:4 * half + 4, :],
                       bank(GATHER_BANK[half])[:, 0].rearrange("p (c t) -> p c t", c=4)
                       ).then_inc(sem("gather_hi"), 1)

            gather_hi(1, 0, 0)
            act.wait_ge(sem("planned"), 1)
            act.wait_ge(sem("y_zero"), 2)
            n_items = act.value_load(plan[0:1, 0:1], min_val=E, max_val=E + MORE)
            with act.Fori(0, n_items) as i:
                def hi_m(q):
                    n = M0 + q
                    if n % 2 == 0:
                        act.wait_ge(landed[n // 2 % RAW_RING],
                                    16 * (n // 2 // RAW_RING + 1) + i * (16 * (N_ITEM // 2 // RAW_RING)))
                    act.wait_ge(used, n - 5 + i * N_ITEM)
                    a.copy(w_hi[q % 6][:], piece_src(n)).then_inc(hi_done, 1)

                KD = DSTEPS
                for q in range(N_ITEM):
                    hi_m(q)
                    if q == 3:
                        gather_hi(2 + i * 2, 1, i)
                    if q == 4:
                        act.wait_ge(used, M0 + i * N_ITEM)
                        a.copy(y_sb[:], bank(4, 2).rearrange("p b n -> p (b n)")).then_inc(sem("y_out"), 1)
                    if q == 8:
                        gate_silu(M0 + 4 + i * N_ITEM, bank(0)[:, 0], sg[:])
                    if q > 8 and (q - 16) % 12 == 0 and q < 80:
                        j = (q - 16) // 12 + 1
                        a_hi(KD + j - 1 + i * ESTEPS, bank(6)[:, 0].rearrange("p (c t) -> p c t", c=4), aT[0][:])
                        gate_silu(M0 + q - 4 + i * N_ITEM, bank(j % 2)[:, 0], sg[:])
                        if j == 3:
                            act.wait_ge(sem("place_ps"), 1 + i)
                            a.copy(place[:], bank(7)[:, 0, 0:T]).then_inc(sem("place"), 1)
                a_hi(KD + ESTEPS - 1 + i * ESTEPS, bank(6)[:, 0].rearrange("p (c t) -> p c t", c=4), aT[0][:])
                gather_hi(3 + i * 2, 0, i)
            act.wait_ge(used, M0 + n_items * N_ITEM)
            a.copy(y_sb[:], bank(4, 2).rearrange("p b n -> p (b n)")).then_inc(sem("y_out"), 1)
            act.wait_ge(sem("x_added"), 3 * 4 + 4 + 4 * n_items)
            sum_squares(x_sb, 6)
            inv_root(6, TB)

        @block.vector
        def _(dve):
            v = nc.vector
            own = [0]

            def link(ins):
                own[0] += 1
                ins.then_inc(sem("dve_chain"), 1)
                dve.wait_ge(sem("dve_chain"), own[0])

            def lo(n):
                dve.wait_ge(hi_done, n + 1)
                v.tensor_tensor(w_lo[slot_of[n]][:], piece_src(n), w_hi[slot_of[n]][:].bitcast(F32),
                                ALU.subtract).then_inc(split, 1)

            def variance(u, cols):
                dve.wait_ge(sem("squares"), u + 1)
                for sl, n in cols:
                    ins = v.tensor_scalar(sl, sl, 1.0 / n, EPS, ALU.mult, ALU.add)
                ins.then_inc(sem("variance"), 1)

            def scale(u, src, spans):
                dve.wait_ge(sem("rstd"), u + 1)
                dve.wait_ge(sem("gain"), 16 * GAINS[u])
                for b, lo_, w, col in spans:
                    ins = v.scalar_tensor_tensor(out=xn[:, b, lo_:lo_ + w], in0=src[:, b, lo_:lo_ + w],
                                                 scalar=rstd[:, col:col + 1], in1=gain[:, lo_:lo_ + w],
                                                 op0=ALU.mult, op1=ALU.mult)
                ins.then_inc(sem("normed"), 1)

            FULL = [(b, 0, D, b) for b in range(TB)]

            def turn_lo(w, src_hi, dst):
                for c in range(4):
                    dve.wait_ge(sem("turn_hi"), 4 * w + c + 1)
                    v.tensor_tensor(dst[:, 2 * c:2 * c + 2, :], bank(4 + c)[:, 0].rearrange("p (c t) -> p c t", c=2),
                                    src_hi[:, 2 * c:2 * c + 2, :].bitcast(F32), ALU.subtract
                                    ).then_inc(sem("turn_lo"), 1)

            def conv_half(l, h):
                dve.wait_ge(sem("moved"), 6 * l + h + 1)
                par = lambda k, c: conv_par[:, l * NCP + k * CT + c:l * NCP + k * CT + c + 1]
                for k in range(TAPS):
                    for c in range(4 * h, 4 * h + 4):
                        src = xbc[:, c, k:k + T]
                        if k == 0:
                            ins = v.tensor_scalar(conv[:, c], src, par(0, c), par(TAPS, c), ALU.mult, ALU.add)
                        else:
                            ins = v.scalar_tensor_tensor(out=conv[:, c], in0=src, scalar=par(k, c), in1=conv[:, c],
                                                         op0=ALU.mult, op1=ALU.add)
                    if k < TAPS - 1:
                        link(ins)
                ins.then_inc(sem("convolved"), 1)

            def mixer_dve(l):
                n0, o0 = seg[f"in{l}"], seg[f"out{l}"]
                if l == 0:
                    dve.wait_ge(sem("x_landed"), 16)
                variance(3 * l, [(stat[:, 0:TB], D)])
                scale(3 * l, x_sb, FULL)
                if l == 0:
                    dve.wait_ge(sem("w_dt_hi"), 1)
                    v.tensor_tensor(w_dt[1][:], w_dt_raw[:], w_dt[0][:].bitcast(F32), ALU.subtract
                                    ).then_inc(sem("w_dt_lo"), 1)
                v.memset(xbc[:, :, 0:PAD], 0.0).then_inc(sem("padded"), 1)
                for q in range(4):
                    lo(n0 + q)
                turn_lo(3 * l, mixer_hT[0], mixer_hT[1])
                for grp in range(1, 6):
                    for q in range(4):
                        lo(n0 + 4 * grp + q)
                    if grp == 2:
                        dve.wait_ge(sem("par_out"), 1)
                        dve.wait_ge(sem("padded"), l + 1)
                        conv_half(l, 0)
                    if grp == 3:
                        conv_half(l, 1)
                        dve.wait_ge(sem("dt_ps"), l + 1)
                        bias = dt_par[:, 0, l, :].unsqueeze(1).broadcast_to([P, TB, HEADS])
                        v.tensor_tensor(dt_v[:], psum[:, 4, 0:TB * HEADS].rearrange("p (b h) -> p b h", b=TB), bias,
                                        ALU.add).then_inc(sem("dt_raw"), 1)
                dve.wait_ge(sem("dt_rest"), l + 1)
                link(v.scalar_tensor_tensor(out=dt_b[:], in0=dt_v[:], scalar=0.0, in1=dt_a[:], op0=ALU.max,
                                            op1=ALU.add))
                dve.wait_ge(sem("exp_a"), 1)
                link(v.scalar_tensor_tensor(out=dA[:], in0=dt_b[:], scalar=-1.0,
                                            in1=dt_par[:, 1, l, :].unsqueeze(1).broadcast_to([P, TB, HEADS]),
                                            op0=ALU.mult, op1=ALU.mult))
                dve.wait_ge(used, n0 + N_IN)
                for c in range(TB):
                    v.tensor_tensor(seg_rhs[:, c], tri_le[:].unsqueeze(1).broadcast_to([P, HEADS, P]),
                                    dA[:, c].unsqueeze(2).broadcast_to([P, HEADS, P]), ALU.mult
                                    ).then_inc(sem("seg_rhs"), 1)
                dve.wait_ge(sem("tokened"), l + 1)
                v.tensor_copy(b_tok[:], bank(6)[:, 0, 0:GROUPS * P].rearrange("p (g n) -> p g n", g=GROUPS)
                              ).then_inc(sem("b_tok"), 1)
                dve.wait_ge(sem("cb_ps"), l + 1)
                link(v.tensor_tensor(cb_m[:].rearrange("p c g t -> p (c g) t"),
                                     bank(7)[:, 0].rearrange("p (c t) -> p c t", c=TB * GROUPS),
                                     tri_le[:].unsqueeze(1).broadcast_to([P, TB * GROUPS, P]), ALU.mult))
                dve.wait_ge(sem("x_tok"), l + 1)
                heads = lambda t: t.rearrange("p (h d) -> p h d", h=HEADS)
                for c in range(TB):
                    ins = v.tensor_tensor(heads(x_dt[:, c]), heads(x_tok[:, c]),
                                          dt_b[:, c].unsqueeze(2).broadcast_to([P, HEADS, HD]), ALU.mult)
                link(ins)
                dve.wait_ge(sem("decay"), TB * l + 1)
                v.tensor_tensor(heads(x_state[:]), heads(x_dt[:, 0]),
                                decay[:, 0, :, P - 1:P].broadcast_to([P, HEADS, HD]), ALU.mult
                                ).then_inc(sem("x_state"), 1)
                dve.wait_ge(sem("x_state"), l + 1)
                for c in range(TB):
                    dve.wait_ge(sem("decay"), TB * l + c + 1)
                    d4 = decay[:, c].rearrange("p (g r) t -> p g r t", g=GROUPS)
                    v.tensor_tensor(d4, d4, cb_m[:, c].unsqueeze(2).broadcast_to([P, GROUPS, HG, P]), ALU.mult
                                    ).then_inc(sem("masked_decay"), 1)
                for c in range(TB):
                    y = mix[:, c, AW:2 * AW]
                    link(v.tensor_tensor(heads(y), heads(x_tok[:, c]),
                                         dt_par[:, 2, l, :].unsqueeze(2).broadcast_to([P, HEADS, HD]), ALU.mult))
                    dve.wait_ge(sem("y_diag"), TB * l + c + 1)
                    link(v.tensor_tensor(y, y, bank(c)[:, 0], ALU.add))
                    if c == 1:
                        dve.wait_ge(sem("y_off"), l + 1)
                        dve.wait_ge(sem("e_cum"), l + 1)
                        link(v.tensor_tensor(heads(y_off[:]), heads(bank(2)[:, 0]),
                                             e_cum[:].unsqueeze(2).broadcast_to([P, HEADS, HD]), ALU.mult))
                        link(v.tensor_tensor(y, y, y_off[:], ALU.add))
                    dve.wait_ge(sem("moved"), 6 * l + 6)
                    v.tensor_tensor(y, y, z_act[:, c], ALU.mult).then_inc(sem("y_done"), 1)

                def soft_part(p):
                    dve.wait_ge(sem("rest"), 4 * l + p + 1)
                    if p >= 2:
                        dve.wait_ge(sem("cummed"), 4 * l + p - 1)
                    s = soft[p % 2]
                    link(v.scalar_tensor_tensor(out=s[:], in0=bank(ZB[p % 3], 2)[:, :, 0:W3], scalar=0.0,
                                                in1=rest[p % 2][:], op0=ALU.max, op1=ALU.add))
                    for h in range(2):
                        d = diag(s[:, h])
                        ins = v.tensor_tensor(d, d, tri_lt[:].unsqueeze(1).broadcast_to([P, 2, P]), ALU.mult)
                    ins.then_inc(sem("soft"), 1)

                def mask_part(p):
                    dve.wait_ge(sem("prob"), 4 * l + p + 1)
                    for h in range(2):
                        d = diag(prob[p % 2][:, h])
                        ins = v.scalar_tensor_tensor(out=d, in0=d, scalar=2.0,
                                                     in1=tri_lt[:].unsqueeze(1).broadcast_to([P, 2, P]),
                                                     op0=ALU.min, op1=ALU.mult)
                    ins.then_inc(sem("masked"), 1)

                soft_part(0)
                for p in range(HEADS // 2):
                    if p + 1 < HEADS // 2:
                        soft_part(p + 1)
                    mask_part(p)

                variance(3 * l + 1, [(stat[:, 0:6].rearrange("p (b c) -> p b c", b=2)[:, :, 0:1], AW),
                                     (stat[:, 0:6].rearrange("p (b c) -> p b c", b=2)[:, :, 1:3], GW)])
                scale(3 * l + 1, mix, [(b, f, w, 3 * b + c) for b in range(TB)
                                       for f, w, c in ((0, AW, 0), (AW, GW, 1), (AW + GW, GW, 2))])
                for q in range(4):
                    lo(o0 + q)
                turn_lo(1 + 3 * l, mixer_hT[0], mixer_hT[1])
                for q in range(4, 8):
                    lo(o0 + q)
                for h in range(2):
                    dve.wait_ge(used, o0 + 4 * h + 4)
                    for b in range(TB):
                        xs = x_sb[:, b, h * BANK:(h + 1) * BANK]
                        v.tensor_tensor(xs, xs, bank(2 * h + b)[:, 0], ALU.add).then_inc(sem("x_added"), 1)

            def a_lo(k, src, dst_hi, dst_lo):
                dve.wait_ge(sem("a_hi"), k + 1)
                v.tensor_tensor(dst_lo, src, dst_hi.bitcast(F32), ALU.subtract).then_inc(sem("hidden_split"), 1)

            def glu(k, pieces, sg_, up, dst):
                dve.wait_ge(sem("silu"), k + 1)
                dve.wait_ge(used, pieces)
                v.tensor_tensor(dst, sg_, up, ALU.mult).then_inc(sem("hidden"), 1)

            mixer_dve(0)

            dve.wait_ge(sem("x_added"), 4)
            variance(2, [(stat[:, 0:TB], D)])
            scale(2, x_sb, FULL)
            d0 = seg["dense"]
            for q in range(4):
                lo(d0 + q)
            turn_lo(2, dense_hT[0], dense_hT[1])
            two = lambda ap: ap.rearrange("p (b n) -> p b n", b=2)
            for j in range(DSTEPS):
                base = d0 + (0 if j == 0 else 4 + 6 * (j - 1))
                if j >= 1:
                    for q in range(2):
                        lo(base + q)
                    glu(j - 1, base - (0 if j == 1 else 2), dense_h[:], two(bank(1)[:, 0]), dense_h[:])
                    for q in range(2, 6):
                        lo(base + q)
                    a_lo(j - 1, two(bank(2)[:, 0]), dense_aT[0][:], dense_aT[1][:])
            for q in range(N_DENSE - 2, N_DENSE):
                lo(d0 + q)
            glu(DSTEPS - 1, d0 + N_DENSE - 4, dense_h[:], two(bank(1)[:, 0]), dense_h[:])
            a_lo(DSTEPS - 1, two(bank(2)[:, 0]), dense_aT[0][:], dense_aT[1][:])
            dve.wait_ge(used, d0 + N_DENSE)
            for b in range(TB):
                for h in range(2):
                    xs = x_sb[:, b, h * BANK:(h + 1) * BANK]
                    v.tensor_tensor(xs, xs, bank(4 + 2 * b + h)[:, 0], ALU.add).then_inc(sem("x_added"), 1)
            dve.wait_ge(sem("x_added"), 8)
            mixer_dve(1)

            dve.wait_ge(sem("x_added"), 12)
            variance(5, [(stat[:, 0:TB], D)])
            scale(5, x_sb, FULL)
            dve.wait_ge(sem("consts"), ROUTE_CONSTS)
            dve.wait_ge(sem("logits"), 1)
            wide = [P, TB, E, E]
            link(v.tensor_copy(logit[:], psum[:, 0, 0:TB * E].rearrange("p (b e) -> p b e", b=TB)))
            mine, other = logit[:].unsqueeze(3).broadcast_to(wide), logit[:].unsqueeze(2).broadcast_to(wide)
            v.tensor_tensor(cmp_a[:], mine, other, ALU.is_lt)
            link(v.tensor_tensor(cmp_b[:], mine, other, ALU.is_equal))
            link(v.tensor_tensor(cmp_b[:], cmp_b[:], low8[:].unsqueeze(1).broadcast_to(wide), ALU.mult))
            link(v.tensor_tensor(cmp_a[:], cmp_a[:], cmp_b[:], ALU.add))
            link(v.tensor_reduce(rank[:], cmp_a[:], AX.X, ALU.add))
            v.tensor_scalar(chosen[:], rank[:], TOPK - 0.5, None, ALU.is_lt).then_inc(sem("chosen"), 1)
            link(v.tensor_reduce(r_max[:], logit[:], AX.X, ALU.max))
            v.tensor_tensor(logit[:], logit[:], r_max[:].unsqueeze(2).broadcast_to([P, TB, E]), ALU.subtract
                            ).then_inc(sem("logit_rel"), 1)
            dve.wait_ge(sem("e_gate"), 1)
            dve.wait_ge(sem("chosen"), 1)
            link(v.tensor_tensor(e_gate[:], e_gate[:], chosen[:], ALU.mult))
            link(v.tensor_reduce(r_max[:], e_gate[:], AX.X, ALU.add))
            link(v.reciprocal(r_max[:], r_max[:]))
            v.memset(slot_t[:, :, E:], -1.0)
            link(v.memset(gate_t[:, :, E:], 0.0))
            link(v.tensor_tensor(gate_t[:, :, 0:E], e_gate[:], r_max[:].unsqueeze(2).broadcast_to([P, TB, E]),
                                 ALU.mult))
            dve.wait_ge(sem("positions"), 1)
            pos = psum[:, 1, 0:TB * E].rearrange("p (b e) -> p b e", b=TB)
            v.tensor_copy(count[:], psum[:, 1, TB * E:(TB + 1) * E])
            link(v.scalar_tensor_tensor(out=pos1[:], in0=pos, scalar=1.0, in1=chosen[:], op0=ALU.add, op1=ALU.mult))
            v.tensor_scalar(slot_t[:, :, 0:E], pos1[:], -1.0, None, ALU.add).then_inc(sem("slots_main"), 1)
            link(v.tensor_scalar(over[:], count[:], float(P), None, ALU.is_gt))
            link(v.tensor_tensor(cmp_a[:, 0], over[:].unsqueeze(1).broadcast_to([P, E, E]), low8[:], ALU.mult))
            link(v.tensor_reduce(o_rank[:], cmp_a[:, 0], AX.X, ALU.add))
            v.tensor_reduce(plan_f[:, 0:1], over[:], AX.X, ALU.add)
            link(v.tensor_scalar(pos1[:], pos1[:], -1.0 - P, None, ALU.add))
            for q in range(MORE):
                link(v.scalar_tensor_tensor(out=sel[:], in0=o_rank[:], scalar=float(q), in1=over[:],
                                            op0=ALU.is_equal, op1=ALU.mult))
                both = sel[:].unsqueeze(1).broadcast_to([P, TB, E])
                link(v.tensor_tensor(tmp_e[:], pos1[:], both, ALU.mult))
                link(v.tensor_reduce(slot_t[:, :, E + q:E + q + 1], tmp_e[:], AX.X, ALU.add))
                link(v.tensor_tensor(tmp_e[:], gate_t[:, :, 0:E], both, ALU.mult))
                link(v.tensor_reduce(gate_t[:, :, E + q:E + q + 1], tmp_e[:], AX.X, ALU.add))
                link(v.tensor_tensor(tmp_e[:, 0], e_ids[:], sel[:], ALU.mult))
                link(v.tensor_reduce(plan_f[:, 1 + q:2 + q], tmp_e[:, 0], AX.X, ALU.add))
            link(v.tensor_scalar(plan_f[:, 0:1], plan_f[:, 0:1], float(E), None, ALU.add))
            v.tensor_copy(plan[:], plan_f[:]).then_inc(sem("planned"), 1)

            def make_pick(i, cnt):
                for b in range(TB):
                    ins = v.tensor_scalar(pick[:, b], slots[:], slot_t[:, b, bass.ds(i, 1)], None, ALU.is_equal)
                ins.then_inc(sem("pick"), 1)

            def gather_lo(k, half):
                dve.wait_ge(sem("gather_hi"), k)
                h = slice(4 * half, 4 * half + 4)
                v.tensor_tensor(g_hT[1][:, h, :], bank(GATHER_BANK[half])[:, 0].rearrange("p (c t) -> p c t", c=4),
                                g_hT[0][:, h, :].bitcast(F32), ALU.subtract).then_inc(sem("gather_lo"), 1)

            dve.wait_ge(sem("planned"), 1)
            make_pick(0, 1)
            v.memset(bank(4, 2), 0.0).then_inc(sem("y_zero"), 1)
            v.memset(place[:], 0.0).then_inc(sem("y_zero"), 1)
            gather_lo(1, 0)
            n_items = dve.value_load(plan[0:1, 0:1], min_val=E, max_val=E + MORE)
            KD = DSTEPS
            four = lambda ap: ap.rearrange("p (c t) -> p c t", c=4)
            with dve.Fori(0, n_items) as i:
                def lo_m(q):
                    n = M0 + q
                    dve.wait_ge(hi_done, n + 1 + i * N_ITEM)
                    v.tensor_tensor(w_lo[q % 6][:], piece_src(n), w_hi[q % 6][:].bitcast(F32), ALU.subtract
                                    ).then_inc(split, 1)

                for q in range(N_ITEM):
                    lo_m(q)
                    if q == 3:
                        gather_lo(2 + i * 2, 1)
                    if q == 9:
                        for b in range(TB):
                            dve.wait_ge(sem("combined"), b + 1 + i * TB)
                            for h in range(2):
                                xs = x_sb[:, b, h * BANK:(h + 1) * BANK]
                                v.tensor_tensor(xs, xs, bank(COMBINE[b][h])[:, 0], ALU.add
                                                ).then_inc(sem("x_added"), 1)
                    if q == 13:
                        for b in range(TB):
                            ins = v.tensor_scalar(pick_g[:, b], slots[:], slot_t[:, b, bass.ds(i, 1)],
                                                  gate_t[:, b, bass.ds(i, 1)], ALU.is_equal, ALU.mult)
                        ins.then_inc(sem("pick_g"), 1)
                    if q == 12:
                        glu(KD + i * ESTEPS, M0 + 8 + i * N_ITEM, sg[:], bank(2)[:, 0], act_h[:])
                    if q >= 20 and q % 12 == 8:
                        j = (q - 20) // 12 + 1
                        glu(KD + j + i * ESTEPS, M0 + q - 4 + i * N_ITEM, sg[:], bank(2 + j % 2)[:, 0], act_h[:])
                    if q >= 16 and q % 12 == 4 and q < 80:
                        j = (q - 16) // 12 + 1
                        a_lo(KD + j - 1 + i * ESTEPS, four(bank(6)[:, 0]), aT[0][:], aT[1][:])
                    if q == 60:
                        make_pick(i + 1, 2 + i)
                a_lo(KD + ESTEPS - 1 + i * ESTEPS, four(bank(6)[:, 0]), aT[0][:], aT[1][:])
                gather_lo(3 + i * 2, 0)
            for b in range(TB):
                dve.wait_ge(sem("combined"), b + 1 + n_items * TB)
                for h in range(2):
                    xs = x_sb[:, b, h * BANK:(h + 1) * BANK]
                    v.tensor_tensor(xs, xs, bank(COMBINE[b][h])[:, 0], ALU.add).then_inc(sem("x_added"), 1)
            variance(6, [(stat[:, 0:TB], D)])
            scale(6, x_sb, FULL)

        @block.tensor
        def _(pe):
            def turn():
                for c in range(4):
                    for k in range(2):
                        for b in range(TB):
                            ins = nc.tensor.transpose(psum[:, 4 + c, k * T + b * P:k * T + b * P + P],
                                                      xn[:, b, (2 * c + k) * P:(2 * c + k + 1) * P], ident[:])
                    ins.then_inc(sem("turned"), 1)

            hi_lo = lambda n, c: [w[slot_in(n)][:].rearrange("p (k n) -> p k n", k=c) for w in (w_hi, w_lo)]

            def token_major(n, k0, kts, h, banks_of, first, last):
                wh, wl = hi_lo(n, kts)
                for kk in range(kts):
                    k = k0 + kk
                    for b in range(TB):
                        tok = slice(b * P, b * P + P)
                        ins = mm3(banks_of(b), h[0][:, k, tok], h[1][:, k, tok], wh[:, kk], wl[:, kk],
                                  first(k, b), last(k))
                ins.then_inc(used, 1)

            def mixer_pe(l):
                n0, o0, u = seg[f"in{l}"], seg[f"out{l}"], 3 * l
                if l == 0:
                    pe.wait_ge(sem("consts"), CONSTS)
                    pe.wait_ge(sem("params"), PARAMS)
                    nc.tensor.transpose(psum[:, 0, 0:L * NCP], conv_raw[:], ident[0:L * NCP, 0:L * NCP]
                                        ).then_inc(sem("par_turned"), 1)
                pe.wait_ge(sem("normed"), u + 1)
                turn()
                pe.wait_ge(sem("turn_lo"), 4 * u + 4)
                if l == 0:
                    pe.wait_ge(sem("par_out"), 1)
                hh, hl = mixer_hT
                for grp in range(6):
                    if grp >= 2:
                        pe.wait_ge(sem("moved"), 6 * l + grp - 1)
                    if grp == 2:
                        pe.wait_ge(sem("w_dt_lo"), 1)
                        for b in range(TB):
                            tok = slice(b * P, b * P + P)
                            for k in range(KT):
                                ins = mm3(psum[:, 4, b * HEADS:(b + 1) * HEADS], hh[:, k, tok], hl[:, k, tok],
                                          w_dt[0][:, l, k], w_dt[1][:, l, k], k == 0, k == KT - 1)
                        ins.then_inc(sem("dt_ps"), 1)
                    b0 = 2 * (grp % 2)
                    for q in range(4):
                        n = n0 + 4 * grp + q
                        pe.wait_ge(split, n + 1)
                        if grp >= 4:
                            token_major(n, 2 * q, 2, mixer_hT, lambda b: psum[:, b0 + b, :],
                                        lambda k, b: k == 0, lambda k: k == KT - 1)
                            continue
                        wh, wl = hi_lo(n, 2)
                        for kk in range(2):
                            k = 2 * q + kk
                            for c in range(4):
                                ch = slice(c * P, c * P + P)
                                ins = mm3(psum[:, b0 + c // 2, (c % 2) * T:(c % 2) * T + T], wh[:, kk, ch],
                                          wl[:, kk, ch], hh[:, k], hl[:, k], k == 0 and c % 2 == 0, k == KT - 1)
                        ins.then_inc(used, 1)

                pe.wait_ge(sem("conv_act"), 2 * l + 2)
                pe.wait_ge(sem("dt_raw"), l + 1)
                for b in range(TB):
                    for c in range(XT):
                        nc.tensor.transpose(psum[:, 4 + b, c * P:c * P + P], conv[:, c, b * P:b * P + P], ident[:])
                for g in range(GROUPS):
                    ins = nc.tensor.transpose(psum[:, 6, g * P:g * P + P], conv[:, XT + g, 0:P], ident[:])
                ins.then_inc(sem("tokened"), 1)
                for c in range(TB):
                    for g in range(GROUPS):
                        at_ = (c * GROUPS + g) * P
                        ins = mm(psum[:, 7, at_:at_ + P], conv[:, XT + g, c * P:c * P + P],
                                 conv[:, XT + GROUPS + g, c * P:c * P + P])
                ins.then_inc(sem("cb_ps"), 1)
                pe.wait_ge(sem("moved"), 6 * l + 6)
                for c in range(TB):
                    pe.wait_ge(sem("seg_rhs"), TB * l + c + 1)
                    for h in range(2):
                        ins = mm(psum[:, 2 * c + h, :], tri_gt[:],
                                 seg_rhs[:, c, 4 * h:4 * h + 4, :].rearrange("p h t -> p (h t)"))
                    ins.then_inc(sem("segsum"), 1)
                pe.wait_ge(sem("x_tok"), l + 1)
                mm(psum[:, 4, 0:HEADS], tri_le[:], dA[:, 1, :]).then_inc(sem("cum"), 1)
                pe.wait_ge(sem("b_tok"), l + 1)
                pe.wait_ge(sem("x_state"), l + 1)
                for g in range(GROUPS):
                    ins = mm(psum[:, 6, g * GW:(g + 1) * GW], b_tok[:, g, :], x_state[:, g * GW:(g + 1) * GW])
                ins.then_inc(sem("stated"), 1)
                for c in range(TB):
                    pe.wait_ge(sem("masked_decay"), TB * l + c + 1)
                    for h in range(HEADS):
                        ins = mm(psum[:, c, h * HD:(h + 1) * HD], decay[:, c, h, :], x_dt[:, c, h * HD:(h + 1) * HD])
                    ins.then_inc(sem("y_diag"), 1)
                pe.wait_ge(sem("state_out"), l + 1)
                for g in range(GROUPS):
                    ins = mm(psum[:, 2, g * GW:(g + 1) * GW], conv[:, XT + GROUPS + g, P:2 * P],
                             state[:, g * GW:(g + 1) * GW])
                ins.then_inc(sem("y_off"), 1)

                def scores(p):
                    if p < 3:
                        pe.wait_ge(sem("y_done"), TB * (l + 1))
                    else:
                        pe.wait_ge(sem("prob"), 4 * l + p - 2)
                    for s in range(2):
                        part = slice(s * HD, (s + 1) * HD)
                        ps = psum[:, ZB[p % 3] + s, :]
                        mm(ps[:, 0:T], kT[part, p, 0:P], qT[part, p, :])
                        ins = mm(ps[:, T:W3], kT[part, p, P:T], qT[part, p, P:T], start=False)
                    ins.then_inc(sem("scores"), 1)

                def cums(p):
                    pe.wait_ge(sem("soft"), 4 * l + p + 1)
                    for s in range(2):
                        ps, sf = psum[:, ZB[p % 3] + s, :], soft[p % 2][:, s]
                        mm(ps[:, 0:T], neg_ge[:], sf[:, 0:T], start=False)
                        mm(ps[:, P:T], neg_one[:], sf[:, T:W3], start=False)
                        ins = mm(ps[:, T:W3], neg_ge[:], sf[:, T:W3], start=False)
                    ins.then_inc(sem("cummed"), 1)

                def values(p):
                    pe.wait_ge(sem("masked"), 4 * l + p + 1)
                    for s in range(2):
                        h, w = 2 * p + s, prob[p % 2][:, s]
                        col = slice(h * HD, (h + 1) * HD)
                        mm(psum[:, 4, col], w[:, 0:P], v_tok[:, 0, col])
                        mm(psum[:, 5, col], w[:, P:T], v_tok[:, 0, col], stop=False)
                        ins = mm(psum[:, 5, col], w[:, T:W3], v_tok[:, 1, col], start=False)
                    ins.then_inc(sem("pv"), 1)

                PAIRS = HEADS // 2
                scores(0)
                scores(1)
                for p in range(PAIRS + 1):
                    if p < PAIRS:
                        cums(p)
                    if p >= 1:
                        values(p - 1)
                    if p + 2 < PAIRS:
                        scores(p + 2)

                pe.wait_ge(sem("normed"), u + 2)
                turn()
                pe.wait_ge(sem("turn_lo"), 4 * (u + 1) + 4)
                for h in range(2):
                    for q in range(4):
                        n = o0 + 4 * h + q
                        pe.wait_ge(split, n + 1)
                        token_major(n, 2 * q, 2, mixer_hT, lambda b: psum[:, 2 * h + b, :],
                                    lambda k, b: k == 0, lambda k: k == KT - 1)

            mixer_pe(0)

            pe.wait_ge(sem("normed"), 3)
            turn()
            pe.wait_ge(sem("turn_lo"), 4 * 2 + 4)
            d0 = seg["dense"]
            for j in range(DSTEPS + 1):
                base = d0 + (0 if j == 0 else 4 + 6 * (j - 1))
                for up in range(2):
                    if j < DSTEPS:
                        for q in range(2):
                            n = base + 2 * up + q
                            pe.wait_ge(split, n + 1)
                            ps = psum[:, 1 if up else (0, 3)[j % 2], :]
                            token_major(n, 4 * q, 4, dense_hT, lambda b: ps[:, b * DS:(b + 1) * DS],
                                        lambda k, b: k == 0 and b == 0, lambda k: k == KT - 1)
                    if up == 0 and j >= 1:
                        pe.wait_ge(sem("hidden"), j)
                        for c in range(2):
                            for b in range(TB):
                                ins = nc.tensor.transpose(
                                    psum[:, 2, c * T + b * P:c * T + b * P + P],
                                    dense_h[:, b].rearrange("p (f c) -> p c f", c=2)[:, c], ident[:])
                        ins.then_inc(sem("hidden_turned"), 1)
                if j >= 1:
                    pe.wait_ge(sem("hidden_split"), j)
                    for c in range(2):
                        n = base + (4 if j < DSTEPS else 0) + c
                        pe.wait_ge(split, n + 1)
                        wh, wl = hi_lo(n, 2)
                        for b in range(TB):
                            for h in range(2):
                                tok = slice(b * P, b * P + P)
                                ins = mm3(psum[:, 4 + 2 * b + h, :], dense_aT[0][:, c, tok], dense_aT[1][:, c, tok],
                                          wh[:, h], wl[:, h], j == 1 and c == 0, j == DSTEPS and c == 1)
                        ins.then_inc(used, 1)

            mixer_pe(1)

            pe.wait_ge(sem("normed"), 6)
            turn()
            pe.wait_ge(sem("router_hT"), 4)
            pe.wait_ge(sem("router_in"), 16)
            for b in range(TB):
                for k in range(KT):
                    ins = mm(psum[:, 0, b * E:(b + 1) * E], r_hT[:, k, b * P:b * P + P], router[:, k], k == 0,
                             k == KT - 1)
            ins.then_inc(sem("logits"), 1)
            pe.wait_ge(sem("chosen"), 1)
            mm(psum[:, 1, 0:E], tri_lt[:], chosen[:, 0])
            mm(psum[:, 1, E:2 * E], ones[:], chosen[:, 0], stop=False)
            mm(psum[:, 1, E:2 * E], tri_lt[:], chosen[:, 1], start=False)
            mm(psum[:, 1, 2 * E:3 * E], ones[:], chosen[:, 0], stop=False)
            mm(psum[:, 1, 2 * E:3 * E], ones[:], chosen[:, 1], start=False).then_inc(sem("positions"), 1)

            def gather(half):
                for kk in range(4):
                    k = 4 * half + kk
                    for b in range(TB):
                        ins = mm(psum[:, GATHER_BANK[half], kk * P:kk * P + P], xn[:, b, k * P:k * P + P],
                                 pick[:, b], b == 0, b == TB - 1)
                ins.then_inc(sem("gathered"), 1)

            pe.wait_ge(sem("pick"), 1)
            gather(0)
            gather(1)
            pe.wait_ge(sem("y_zero"), 2)
            n_items = pe.value_load(plan[0:1, 0:1], min_val=E, max_val=E + MORE)
            KD = DSTEPS

            def combine():
                for b in range(TB):
                    for h in range(2):
                        ins = mm(bank(COMBINE[b][h])[:, 0], place[:, b * P:b * P + P],
                                 y_sb[:, h * BANK:(h + 1) * BANK])
                    ins.then_inc(sem("combined"), 1)

            with pe.Fori(0, n_items) as i:
                def expert_up(q0, ps, wait_half):
                    for q in range(4):
                        n = M0 + q0 + q
                        if wait_half and q == 2:
                            pe.wait_ge(sem("gather_lo"), 2 + i * 2)
                        pe.wait_ge(split, n + 1 + i * N_ITEM)
                        wh, wl = hi_lo(n, 2)
                        for kk in range(2):
                            k = 2 * q + kk
                            ins = mm3(ps, g_hT[0][:, k], g_hT[1][:, k], wh[:, kk], wl[:, kk], k == 0, k == KT - 1)
                        ins.then_inc(used, 1)

                def turn_hidden(j):
                    pe.wait_ge(sem("hidden"), KD + j + 1 + i * ESTEPS)
                    for c in range(4):
                        ins = nc.tensor.transpose(psum[:, 6, c * P:c * P + P],
                                                  act_h[:].rearrange("p (f c) -> p c f", c=4)[:, c], ident[:])
                    ins.then_inc(sem("hidden_turned"), 1)

                def expert_down(q0, j):
                    pe.wait_ge(sem("hidden_split"), KD + j + 1 + i * ESTEPS)
                    for c in range(4):
                        n = M0 + q0 + c
                        pe.wait_ge(split, n + 1 + i * N_ITEM)
                        wh, wl = hi_lo(n, 2)
                        for h in range(2):
                            ins = mm3(psum[:, 4 + h, :], aT[0][:, c], aT[1][:, c], wh[:, h], wl[:, h],
                                      j == 0 and c == 0, j == ESTEPS - 1 and c == 3)
                        ins.then_inc(used, 1)

                for j in range(ESTEPS):
                    q0 = 0 if j == 0 else 8 + 12 * (j - 1)
                    if j == 0:
                        pe.wait_ge(sem("gather_lo"), 1 + i * 2)
                    if j == 1:
                        pe.wait_ge(sem("x_added"), 16 + i * 4)
                    expert_up(q0, psum[:, j % 2, :], j == 0)
                    if j == 0:
                        pe.wait_ge(sem("y_out"), 1 + i)
                        combine()
                    else:
                        turn_hidden(j - 1)
                    expert_up(q0 + 4, psum[:, 2 + j % 2, :], False)
                    if j >= 1:
                        expert_down(q0 + 8, j - 1)
                    if j == 2:
                        pe.wait_ge(sem("pick_g"), 1 + i)
                        for b in range(TB):
                            ins = nc.tensor.transpose(psum[:, 7, b * P:b * P + P], pick_g[:, b], ident[:])
                        ins.then_inc(sem("place_ps"), 1)
                turn_hidden(ESTEPS - 1)
                pe.wait_ge(sem("place"), 1 + i)
                pe.wait_ge(sem("pick"), 2 + i)
                gather(0)
                expert_down(N_ITEM - 4, ESTEPS - 1)
                gather(1)
            pe.wait_ge(sem("y_out"), 1 + n_items)
            pe.wait_ge(sem("gather_lo"), 1 + n_items * 2)
            combine()
    return nc


_INS = ["x", "mix_norm_g", "w_in", "conv_w", "conv_b", "dt_bias", "a_log", "d_skip", "attn_norm_g", "ssd_norm_g",
        "w_out", "ffn_norm_g", "dense_w_gate", "dense_w_up", "dense_w_down", "router_w", "moe_w_gate",
        "moe_w_up", "moe_w_down", "final_norm_g"]


def kernel(**inputs):
    import numpy as _np
    import concourse.bacc as _bacc
    from concourse import mybir as _mybir
    from concourse.bass_utils import run_bass_kernel_spmd as _run

    nc = _bacc.Bacc("TRN2", target_bir_lowering=False, num_devices=1)
    arrays, args = {}, []
    for name in _INS:
        a = _np.ascontiguousarray(inputs[name])
        arrays[f"in_{name}"] = a
        args.append(nc.dram_tensor(f"in_{name}", a.shape, _mybir.dt.from_np(a.dtype), kind="ExternalInput").ap())
    shape = inputs["x"].shape
    args.append(nc.dram_tensor("out_0", shape, _mybir.dt.float32, kind="ExternalOutput").ap())
    hybrid_trunk(nc, *args)
    r = _run(nc, [arrays], core_ids=[0])
    return r.results[0]["out_0"]
```

```python
import numpy as np

import concourse.bass as bass
from concourse import mybir
from contextlib import ExitStack

ALU = mybir.AluOpType
ACT = mybir.ActivationFunctionType
AX = mybir.AxisListType
F32 = mybir.dt.float32
F32R = mybir.dt.float32r
I32 = mybir.dt.int32

P = 128
BANK = 512
EPS = 1e-5
RAW_RING = 14
FRONT = 7
RING = 6
PIECE = 1024
BLOCK = 2 * PIECE


def hybrid_trunk(nc, x, mix_norm_g, w_in, conv_w, conv_b, dt_bias, a_log, d_skip, attn_norm_g, ssd_norm_g,
                 w_out, ffn_norm_g, dense_w_gate, dense_w_up, dense_w_down, router_w, moe_w_gate,
                 moe_w_up, moe_w_down, final_norm_g, out):
    _, T, D = x.shape
    L = w_in.shape[0]
    TB, KT = T // P, D // P
    HEADS = dt_bias.shape[1]
    AW = attn_norm_g.shape[1]
    HD = AW // HEADS
    TAPS, CONV = conv_w.shape[1], conv_w.shape[2]
    CT = CONV // P
    XT = AW // P
    GROUPS = (CT - XT) // 2
    HG = HEADS // GROUPS
    GW = AW // GROUPS
    FF = dense_w_gate.shape[2]
    E, FE = moe_w_gate.shape[1], moe_w_gate.shape[3]
    TOPK = 2
    MORE = TOPK * T // (P + 1)
    ITEMS = E + MORE + 1
    OQ, OK_, OV, OZ = 0, AW, 2 * AW, 3 * AW
    OX, OBC = 4 * AW, 5 * AW
    ODT = OX + CONV
    assert (TB, KT, HEADS, HD, CT, XT, GROUPS, TAPS) == (2, 8, 8, 64, 8, 4, 2, 4) and L == 2 and AW == BANK

    DS = 256
    DSTEPS = FF // DS
    ES = 512
    ESTEPS = FE // ES

    def in_proj_blocks(l):
        w = w_in[l].rearrange("(c p) n -> p c n", p=P)
        return [w[:, 4 * h:4 * h + 4, o:o + BANK] for o in (OX, OBC, OZ, OQ, OK_, OV) for h in range(2)]

    def out_proj_blocks(l):
        w = w_out[l].rearrange("(c p) n -> p c n", p=P)
        return [w[:, 4 * h:4 * h + 4, o:o + BANK] for h in (1, 0) for o in (0, BANK)]

    def dense_blocks():
        wg = dense_w_gate[0].rearrange("(c p) n -> p c n", p=P)
        wu = dense_w_up[0].rearrange("(c p) n -> p c n", p=P)
        wd = dense_w_down[0].rearrange("(j p c) n -> j p c n", p=P, c=DS // P)
        blocks = []
        for j in range(DSTEPS):
            blocks += [wg[:, :, j * DS:j * DS + DS], wu[:, :, j * DS:j * DS + DS]]
            if j >= 1:
                blocks.append(wd[j - 1])
        return blocks + [wd[DSTEPS - 1]]

    def expert_blocks(e):
        pick = lambda w: w[0, bass.ds(e, 1)]
        wg = pick(moe_w_gate).rearrange("o (c p) n -> p (o c) n", p=P)
        wu = pick(moe_w_up).rearrange("o (c p) n -> p (o c) n", p=P)
        wd = pick(moe_w_down).rearrange("o (j p c) n -> j p (o c) n", p=P, c=ES // P)
        blocks = []
        for j in range(ESTEPS):
            blocks += [w[:, 4 * h:4 * h + 4, j * ES:j * ES + ES] for w in (wg, wu) for h in range(2)]
            if j >= 1:
                blocks += [wd[j - 1][:, 2 * h:2 * h + 2] for h in range(2)]
        return blocks + [wd[ESTEPS - 1][:, 2 * h:2 * h + 2] for h in range(2)]

    N_IN, N_OUT, N_DENSE, N_ITEM = 24, 8, 6 * DSTEPS, 12 * ESTEPS
    fixed_blocks, seg = [], {}

    def add_part(name, blocks):
        seg[name] = 2 * len(fixed_blocks)
        fixed_blocks.extend(blocks)

    add_part("in0", in_proj_blocks(0))
    add_part("out0", out_proj_blocks(0))
    add_part("dense", dense_blocks())
    add_part("in1", in_proj_blocks(1))
    add_part("out1", out_proj_blocks(1))
    B0 = len(fixed_blocks)
    M0 = 2 * B0
    ITEM_BLOCKS = N_ITEM // 2
    assert ITEM_BLOCKS % RAW_RING == 0 and N_ITEM % RING == 0

    def raw_slot(n):
        return (n - B0) % (FRONT if n < B0 else RAW_RING)

    def raw_uses(n):
        return sum(raw_slot(m) == raw_slot(n) for m in range(n + 1))

    with ExitStack() as ctx:
        BASE = (nc.sbuf_base + 31) // 32 * 32
        cursor = [BASE]

        def area(size):
            at = cursor[0]
            cursor[0] += (size + 31) // 32 * 32
            assert cursor[0] <= nc.sbuf_usable_end, (cursor[0], nc.sbuf_usable_end)
            return at

        def at(name, shape, offset, dt=F32):
            return nc.alloc_sbuf_tensor_at(name, shape, dt, offset=offset)

        def size(shape):
            return 4 * int(np.prod(shape[1:]))

        class Region:
            def __init__(self, start, limit):
                self.next, self.end = start, start + limit

            def __call__(self, name, shape, dt=F32):
                t = at(name, shape, self.next, dt)
                self.next += (size(shape) + 31) // 32 * 32
                assert self.next <= self.end, (name, self.next - self.end)
                return t

        raw = at("raw", [P, RAW_RING, BLOCK], area(4 * RAW_RING * BLOCK))
        ring_at = area(RING * 2 * 4 * PIECE)
        w_hi = [at(f"w_hi{s}", [P, PIECE], ring_at + s * 8 * PIECE, F32R) for s in range(RING)]
        w_lo = [at(f"w_lo{s}", [P, PIECE], ring_at + s * 8 * PIECE + 4 * PIECE, F32R) for s in range(RING)]
        back_at = raw.manual_sbuf_range[0] + 4 * FRONT * BLOCK
        hT_at = raw.manual_sbuf_range[0] + 4 * (RAW_RING - 2) * BLOCK
        mixer_hT = [at(f"mixer_hT{s}", [P, KT, T], hT_at + s * 4 * BLOCK, F32R) for s in range(2)]
        scratch = Region(back_at, hT_at - back_at)
        seg_rhs = scratch("seg_rhs", [P, TB, HEADS, P])
        decay = scratch("decay", [P, TB, HEADS, P])
        x_tok = scratch("x_tok", [P, TB, AW])
        x_dt = scratch("x_dt", [P, TB, AW])
        z_act = scratch("z_act", [P, TB, AW])
        x_state = scratch("x_state", [P, AW])
        state = scratch("state", [P, AW])
        b_tok = scratch("b_tok", [P, GROUPS, P])
        W3 = P * 3
        soft = [scratch(f"soft{s}", [P, 2, W3]) for s in range(2)]
        after_seg = Region(seg_rhs.manual_sbuf_range[0], size(seg_rhs.shape))
        rest = [after_seg(f"rest{s}", [P, 2, W3]) for s in range(2)]
        y_off = after_seg("y_off", [P, AW])
        after_dec = Region(decay.manual_sbuf_range[0], size(decay.shape))
        prob = [after_dec(f"prob{s}", [P, 2, W3]) for s in range(2)]

        x_sb = at("x_sb", [P, TB, D], area(4 * TB * D))
        gain = at("gain", [P, D], area(4 * D))
        ident = at("ident", [P, P], area(512))
        tri_le = at("tri_le", [P, P], area(512))
        tri_lt = at("tri_lt", [P, P], area(512))
        tri_gt = at("tri_gt", [P, P], area(512))
        neg_ge = at("neg_ge", [P, P], area(512))
        neg_one = at("neg_one", [P, P], area(512))
        ones = at("ones", [P, P], area(512))
        stat = at("stat", [P, 8], area(32))
        rstd = at("rstd", [P, 8], area(32))
        plan = at("plan", [P, 1 + MORE], area(32), I32)
        work_at = cursor[0]
        WORK = nc.sbuf_usable_end // 32 * 32 - work_at
        mixer = Region(work_at, WORK)
        xn = mixer("xn", [P, TB, D])
        conv = at("conv", [P, CT, T], work_at)
        qT = mixer("qT", [P, XT, T])
        kT = mixer("kT", [P, XT, T])
        v_tok = mixer("v_tok", [P, TB, AW])
        PAD = TAPS - 1
        xbc = mixer("xbc", [P, CT, PAD + T])
        mix = at("mix", [P, TB, D], xbc.manual_sbuf_range[0])
        NCP = TAPS * CT + CT
        PARAM_BYTES = 4 * (L * NCP + 2 * L * KT * HEADS + 3 * L * HEADS)
        params = Region(work_at + WORK - PARAM_BYTES, PARAM_BYTES)
        conv_par = params("conv_par", [P, L * NCP])
        w_dt = [params(f"w_dt_{s}", [P, L, KT, HEADS], F32R) for s in range(2)]
        dt_par = params("dt_par", [P, 3, L, HEADS])
        cb_m = mixer("cb_m", [P, TB, GROUPS, P])
        w_dt_raw = at("w_dt_raw", [P, L, KT, HEADS], v_tok.manual_sbuf_range[0] + 512)
        dt_a = mixer("dt_a", [P, TB, HEADS])
        dt_b = mixer("dt_b", [P, TB, HEADS])
        dt_v = mixer("dt_v", [P, TB, HEADS])
        dA = mixer("dA", [P, TB, HEADS])
        e_cum = mixer("e_cum", [P, HEADS])
        assert mixer.next <= work_at + WORK - PARAM_BYTES
        conv_raw = at("conv_raw", [L * NCP, P], v_tok.manual_sbuf_range[0])

        after_xn = work_at + size(xn.shape)
        dense = Region(after_xn, WORK - size(xn.shape))
        dense_hT = [dense(f"dense_hT{s}", [P, KT, T], F32R) for s in range(2)]
        dense_h = dense("dense_h", [P, TB, DS])
        dense_aT = [dense(f"dense_aT{s}", [P, DS // P, T], F32R) for s in range(2)]
        assert dense.next <= work_at + WORK - PARAM_BYTES
        moe = Region(after_xn, WORK - size(xn.shape))
        g_hT = [moe(f"g_hT{s}", [P, KT, P], F32R) for s in range(2)]
        r_hT = at("r_hT", [P, KT, T], after_xn)
        sg = moe("sg", [P, ES])
        act_h = moe("act_h", [P, ES])
        aT = [moe(f"aT{s}", [P, ES // P, P], F32R) for s in range(2)]
        y_sb = moe("y_sb", [P, D])
        pick = moe("pick", [P, TB, P])
        pick_g = moe("pick_g", [P, TB, P])
        place = moe("place", [P, T])
        slot_t = moe("slot_t", [P, TB, ITEMS])
        gate_t = moe("gate_t", [P, TB, ITEMS])
        slots = moe("slots", [P, P])
        route = Region(y_sb.manual_sbuf_range[0], size(y_sb.shape))
        low8 = route("low8", [P, E, E])
        router = route("router", [P, KT, E])
        logit = route("logit", [P, TB, E])
        cmp_a = route("cmp_a", [P, TB, E, E])
        cmp_b = route("cmp_b", [P, TB, E, E])
        rank = route("rank", [P, TB, E])
        chosen = route("chosen", [P, TB, E])
        e_gate = route("e_gate", [P, TB, E])
        r_max = route("r_max", [P, TB])
        count = route("count", [P, E])
        over = route("over", [P, E])
        o_rank = route("o_rank", [P, E])
        pos1 = route("pos1", [P, TB, E])
        tmp_e = route("tmp_e", [P, TB, E])
        sel = route("sel", [P, E])
        e_ids = route("e_ids", [P, E])
        plan_f = route("plan_f", [P, 1 + MORE])

        psum = ctx.enter_context(nc.psum_tensor("psum", [P, 8, BANK], F32))

        def bank(b, n=1):
            return psum[:, b:b + n, :]

        sems = {}

        def sem(name):
            if name not in sems:
                sems[name] = ctx.enter_context(nc.semaphore(name))
            return sems[name]

        landed = [sem(f"landed{s}") for s in range(RAW_RING)]
        hi_done = sem("hi_done")
        split = sem("split")
        used = sem("used")

        def piece_src(n):
            b = raw_slot(n // 2)
            return raw[:, b, (n % 2) * PIECE:(n % 2) * PIECE + PIECE]

        ZB = (0, 6)
        OUT_BANK = (0, 6)
        GATHER_BANK = (7, 1)
        COMBINE = ((1, 3), (6, 7))
        diag = lambda t: t.rearrange("p (a n) -> p a n", n=P)[:, 0:3:2, :]

        def slot_in(n):
            return (n - M0) % RING

        STAGE = lambda l, name: 4 * l + {"mix": 1, "ssd": 2, "attn": 3, "ffn": 4}[name]
        TURNS = lambda l, name: 12 * l + {"mix": 4, "ssd": 6, "attn": 8, "ffn": 12}[name]
        FINAL = 4 * L + 1
        COLS = {"mix": (0, TB), "ffn": (0, TB), "ssd": (2, 2 + TB * GROUPS), "attn": (6, 6 + TB)}

        def mm3(ps, a_hi, a_lo, b_hi, b_lo, start, stop):
            nc.tensor.matmul(ps, a_hi, b_hi, start=start, stop=False, skip_group_check=True)
            nc.tensor.matmul(ps, a_lo, b_hi, start=False, stop=False, skip_group_check=True)
            return nc.tensor.matmul(ps, a_hi, b_lo, start=False, stop=stop, skip_group_check=True)

        def mm(ps, a, b, start=True, stop=True):
            return nc.tensor.matmul(ps, a, b, start=start, stop=stop, skip_group_check=True)

        block = ctx.enter_context(nc.Block())

        @block.sync
        def _(sp):
            par = sem("params")
            sp.dma_start(x_sb[:], x[0].rearrange("(b p) d -> p b d", p=P)).then_inc(sem("x_landed"), 16)
            sp.dma_start(gain[:], mix_norm_g[0:1, :].broadcast_to([P, D])).then_inc(sem("first_gain"), 16)

            def load(n, src):
                dst = raw[:, raw_slot(n), :].rearrange("p (c n) -> p c n", c=src.shape[1])
                sp.dma_start(dst, src).then_inc(landed[raw_slot(n)], 16)

            for n, src in enumerate(fixed_blocks):
                if n == 2:
                    for l in range(L):
                        sp.dma_start(conv_raw[l * NCP:l * NCP + TAPS * CT, :],
                                     conv_w[l].rearrange("k (c p) -> (k c) p", p=P)).then_inc(par, 16)
                        sp.dma_start(conv_raw[l * NCP + TAPS * CT:(l + 1) * NCP, :],
                                     conv_b[l].rearrange("(c p) -> c p", p=P)).then_inc(par, 16)
                        sp.dma_start(w_dt_raw[:, l], w_in[l].rearrange("(c p) n -> p c n", p=P)[:, :, ODT:ODT + HEADS]
                                     ).then_inc(par, 16)
                    for k, v in enumerate((dt_bias, a_log, d_skip)):
                        flat = v.rearrange("l (o h) -> o (l h)", o=1)
                        sp.dma_start(dt_par[:, k].rearrange("p l h -> p (l h)"),
                                     flat.broadcast_to([P, L * HEADS])).then_inc(par, 16)
                if n >= FRONT:
                    sp.wait_ge(split, 2 * (n - FRONT) + 2)
                load(n, src)

            first = expert_blocks(0)
            for b in range(RAW_RING):
                if b < FRONT:
                    sp.wait_ge(split, 2 * (B0 + b - FRONT) + 2)
                if b == FRONT:
                    sp.wait_ge(sem("normed"), STAGE(L - 1, "attn"))
                if b == RAW_RING - 2:
                    sp.wait_ge(used, M0)
                load(B0 + b, first[b])

            def load_item(i, e, lo_, hi_):
                for b, src in enumerate(expert_blocks(e)):
                    if lo_ <= b < hi_:
                        sp.wait_ge(split, 2 * (B0 + b - RAW_RING) + 2 + i * N_ITEM)
                        load(B0 + b, src)

            with sp.Fori(0, E - 1) as e:
                load_item(e, e, RAW_RING, ITEM_BLOCKS)
                load_item(e + 1, e + 1, 0, RAW_RING)
            load_item(E - 1, E - 1, RAW_RING, ITEM_BLOCKS)
            sp.wait_ge(sem("planned"), 1)
            items = sp.value_load(plan[0:1, 0:1], min_val=E, max_val=E + MORE)
            for q in range(MORE):
                with sp.If(items > E + q):
                    e = sp.value_load(plan[0:1, 1 + q:2 + q], min_val=0, max_val=E - 1)
                    load_item(E + q, e, 0, ITEM_BLOCKS)
                with sp.Else():
                    pass
            sp.wait_ge(sem("normed"), FINAL)
            sp.dma_start(out[0].rearrange("(b p) d -> p b d", p=P), xn[:]).then_inc(sem("stored"), 16)
            sp.wait_ge(sem("stored"), 16)

        @block.gpsimd
        def _(pool):
            g = nc.gpsimd
            cst = sem("consts")
            g.memset(ones[:], 1.0).then_inc(cst, 1)
            g.memset(neg_one[:], -1.0).then_inc(cst, 1)
            pool.wait_ge(cst, 2)
            tri = [(ident, ones, ALU.is_equal, [[-1, P]], 1, 0), (tri_le, ones, ALU.is_ge, [[1, P]], -1, 0),
                   (tri_lt, ones, ALU.is_gt, [[1, P]], -1, 0), (tri_gt, ones, ALU.is_gt, [[-1, P]], 1, 0),
                   (neg_ge, neg_one, ALU.is_ge, [[-1, P]], 1, 0)]
            for dst, src, op, pattern, mult, base in tri:
                g.affine_select(out=dst[:], in_=src[:], pattern=pattern, compare_op=op, fill=0.0, base=base,
                                channel_multiplier=mult).then_inc(cst, 1)

            def load_gain(count, parts):
                pool.wait_ge(sem("normed"), count)
                for lo_, hi_, src in parts:
                    g.dma_start(gain[:, lo_:hi_], src.broadcast_to([P, hi_ - lo_])).then_inc(sem("gain"), 16)

            for l in range(L):
                if l:
                    load_gain(STAGE(l - 1, "ffn"), [(0, D, mix_norm_g[l:l + 1, :])])
                load_gain(STAGE(l, "mix"), [(0, AW, attn_norm_g[l:l + 1, :]), (AW, D, ssd_norm_g[l:l + 1, :])])
                load_gain(STAGE(l, "attn"), [(0, D, ffn_norm_g[l:l + 1, :])])
            g.dma_start(router[:], router_w[0].rearrange("(c p) e -> p c e", p=P)).then_inc(sem("router_in"), 16)
            g.affine_select(out=low8[:], in_=ones[:, 0:E * E].rearrange("p (a b) -> p a b", a=E),
                            pattern=[[1, E], [-1, E]], compare_op=ALU.is_gt, fill=0.0, base=0,
                            channel_multiplier=0).then_inc(cst, 1)
            g.iota(slots[:], [[1, P]], base=0, channel_multiplier=0,
                   allow_small_or_imprecise_dtypes=True).then_inc(cst, 1)
            g.iota(e_ids[:], [[1, E]], base=0, channel_multiplier=0,
                   allow_small_or_imprecise_dtypes=True).then_inc(cst, 1)
            load_gain(STAGE(L - 1, "ffn"), [(0, D, final_norm_g.rearrange("(o d) -> o d", o=1))])

        CONSTS, ROUTE_CONSTS = 7, 10
        GAINS = lambda l, name: 4 * l + {"mix": 0, "ssd": 2, "attn": 2, "ffn": 3}[name]
        PARAMS = 16 * (2 * L + L + 3)

        @block.scalar
        def _(act):
            a = nc.scalar
            own = [0]

            def link(ins):
                own[0] += 1
                ins.then_inc(sem("act_chain"), 1)
                act.wait_ge(sem("act_chain"), own[0])

            def hi(first, count=1):
                for n in range(first, first + count):
                    if n % 2 == 0:
                        act.wait_ge(landed[raw_slot(n // 2)], 16 * raw_uses(n // 2))
                    if n >= RING:
                        act.wait_ge(used, n - RING + 1)
                    a.copy(w_hi[slot_in(n)][:], piece_src(n)).then_inc(hi_done, 1)

            def sum_squares(src):
                for b in range(TB):
                    ins = a.activation(xn[:, b], src[:, b], ACT.Square, accum_out=stat[:, b:b + 1])
                ins.then_inc(sem("squares"), 1)

            def inv_root(stage, name):
                c = slice(*COLS[name])
                act.wait_ge(sem("variance"), stage)
                link(a.activation(rstd[:, c], stat[:, c], ACT.Ln))
                a.activation(rstd[:, c], rstd[:, c], ACT.Exp, scale=-0.5).then_inc(sem("rstd"), 1)

            def turn_hi(done, dst, tiles, first_bank):
                for c in range(tiles // 2):
                    act.wait_ge(sem("turned"), done + c + 1)
                    a.copy(dst[:, 2 * c:2 * c + 2, :], bank(first_bank + c)).then_inc(sem("turn_hi"), 1)

            def mixer_act(l):
                n0, o0 = seg[f"in{l}"], seg[f"out{l}"]
                assert o0 == n0 + N_IN
                if l == 0:
                    act.wait_ge(sem("x_landed"), 16)
                    a.preload_act_table_set("natural_log_exp_and_others")
                sum_squares(x_sb)
                inv_root(STAGE(l, "mix"), "mix")
                if l == 0:
                    act.wait_ge(sem("params"), PARAMS)
                    a.activation(dt_par[:, 1], dt_par[:, 1], ACT.Exp).then_inc(sem("exp_a"), 1)
                hi(n0, 4)
                turn_hi(TURNS(l, "mix") - 4, mixer_hT[0], KT, 4)
                a.preload_act_table_set("silu_and_others")
                if l == 0:
                    a.copy(w_dt[0][:], w_dt_raw[:]).then_inc(sem("w_dt_hi"), 1)
                    act.wait_ge(sem("par_turned"), 1)
                    a.copy(conv_par[:], bank(5)[:, 0, 0:L * NCP]).then_inc(sem("par_out"), 1)

                def move(grp):
                    act.wait_ge(used, n0 + 4 * grp + 4)
                    src = bank(2 * (grp % 2), 2)
                    tiles = src.rearrange("p b (c t) -> p (b c) t", c=2)
                    if grp < 2:
                        ins = a.copy(xbc[:, 4 * grp:4 * grp + 4, PAD:], tiles)
                    elif grp == 2:
                        ins = a.activation(z_act[:], src, ACT.Silu)
                    elif grp == 3:
                        ins = a.mul(qT[:], tiles, float(HD) ** -0.5)
                    elif grp == 4:
                        ins = a.copy(kT[:], tiles)
                    else:
                        ins = a.copy(v_tok[:], src)
                    ins.then_inc(sem("moved"), 1)

                def silu_conv(h):
                    act.wait_ge(sem("convolved"), 2 * l + h + 1)
                    a.activation(conv[:, 4 * h:4 * h + 4], conv[:, 4 * h:4 * h + 4], ACT.Silu
                                 ).then_inc(sem("conv_act"), 1)

                hi(n0 + 4, 4)
                move(0)
                hi(n0 + 8, 3)
                silu_conv(0)
                hi(n0 + 11)
                move(1)
                hi(n0 + 12, 4)
                silu_conv(1)
                move(2)
                a.preload_act_table_set("natural_log_exp_and_others")
                act.wait_ge(sem("dt_raw"), l + 1)
                link(a.activation(dt_a[:], dt_v[:], ACT.Abs))
                link(a.activation(dt_a[:], dt_a[:], ACT.Exp, scale=-1.0))
                a.activation(dt_a[:], dt_a[:], ACT.Ln, bias=1.0).then_inc(sem("dt_rest"), 1)
                hi(n0 + 16, 2)
                act.wait_ge(sem("tokened"), l + 1)
                a.copy(x_tok[:], bank(4, 2)).then_inc(sem("x_tok"), 1)
                hi(n0 + 18, 2)
                move(3)
                hi(n0 + 20, 2)
                for c in range(TB):
                    act.wait_ge(sem("segsum"), TB * l + c + 1)
                    a.activation(decay[:, c].rearrange("p h t -> p (h t)"),
                                 bank(4 + 2 * c, 2).rearrange("p b t -> p (b t)"), ACT.Exp).then_inc(sem("decay"), 1)
                hi(n0 + 22, 2)
                act.wait_ge(sem("stated"), l + 1)
                a.copy(state[:], bank(7)[:, 0]).then_inc(sem("state_out"), 1)
                a.activation(e_cum[:], psum[:, 4, 0:HEADS], ACT.Exp).then_inc(sem("e_cum"), 1)
                move(4)

                def rest_part(p):
                    act.wait_ge(sem("scores"), 4 * l + p + 1)
                    z = bank(ZB[p % 2], 2)[:, :, 0:W3]
                    r = rest[p % 2]
                    if p >= 2:
                        act.wait_ge(sem("soft"), 4 * l + p - 1)
                    link(a.activation(r[:], z, ACT.Abs))
                    link(a.activation(r[:], r[:], ACT.Exp, scale=-1.0))
                    a.activation(r[:], r[:], ACT.Ln, bias=1.0).then_inc(sem("rest"), 1)

                def prob_part(p):
                    act.wait_ge(sem("cummed"), 4 * l + p + 1)
                    if p >= 2:
                        act.wait_ge(sem("pv"), 4 * l + p - 1)
                    a.activation(prob[p % 2][:], bank(ZB[p % 2], 2)[:, :, 0:W3], ACT.Exp
                                 ).then_inc(sem("prob"), 1)

                def part_squares(lo_, w, name):
                    col = COLS[name][0]
                    for b in range(TB):
                        for f in range(AW // w):
                            at_ = lo_ + f * w
                            ins = a.activation(xn[:, b, at_:at_ + w], mix[:, b, at_:at_ + w], ACT.Square,
                                               accum_out=stat[:, col:col + 1])
                            col += 1
                    ins.then_inc(sem("squares"), 1)

                rest_part(0)
                hi(n0 + 24, 2)
                rest_part(1)
                prob_part(0)
                hi(n0 + 26, 2)
                rest_part(2)
                move(5)
                act.wait_ge(sem("y_done"), TB * (l + 1))
                part_squares(AW, GW, "ssd")
                prob_part(1)
                inv_root(STAGE(l, "ssd"), "ssd")
                rest_part(3)
                prob_part(2)
                turn_hi(TURNS(l, "ssd") - 2, mixer_hT[0][:, XT:], XT, 2)
                hi(n0 + 28)
                prob_part(3)
                hi(n0 + 29)
                act.wait_ge(sem("pv"), 4 * (l + 1))
                link(a.copy(mix[:, :, 0:AW], bank(4, 2)))
                part_squares(0, AW, "attn")
                inv_root(STAGE(l, "attn"), "attn")
                hi(n0 + 30)
                turn_hi(TURNS(l, "attn") - 2, mixer_hT[0][:, 0:XT], XT, 4)
                hi(n0 + 31)

            mixer_act(0)

            act.wait_ge(sem("x_added"), 1 * 4)
            sum_squares(x_sb)
            inv_root(STAGE(0, "ffn"), "ffn")
            a.preload_act_table_set("silu_and_others")
            d0 = seg["dense"]
            hi(d0, 4)
            turn_hi(TURNS(0, "ffn") - 4, dense_hT[0], KT, 4)

            def a_hi(k, src, dst):
                act.wait_ge(sem("hidden_turned"), k + 1)
                a.copy(dst, src).then_inc(sem("a_hi"), 1)

            def gate_silu(pieces, src, dst):
                act.wait_ge(used, pieces)
                a.activation(dst, src, ACT.Silu).then_inc(sem("silu"), 1)

            T_BANK = 2
            for j in range(DSTEPS):
                base = d0 + (0 if j == 0 else 4 + 6 * (j - 1))
                for q in range(4 if j == 0 else 6):
                    if j == 0:
                        continue
                    hi(base + q)
                if j >= 1:
                    a_hi(j - 1, bank(T_BANK)[:, 0].rearrange("p (c t) -> p c t", c=2), dense_aT[0][:])
                gate_silu(base + 2, bank(0 if j % 2 == 0 else 3)[:, 0].rearrange("p (b n) -> p b n", b=2), dense_h[:])
            for q in range(N_DENSE - 2, N_DENSE):
                hi(d0 + q)
            a_hi(DSTEPS - 1, bank(T_BANK)[:, 0].rearrange("p (c t) -> p c t", c=2), dense_aT[0][:])

            a.preload_act_table_set("natural_log_exp_and_others")
            act.wait_ge(sem("x_added"), 2 * 4)
            mixer_act(1)

            act.wait_ge(sem("x_added"), 3 * 4)
            sum_squares(x_sb)
            inv_root(STAGE(1, "ffn"), "ffn")
            for c in range(4):
                act.wait_ge(sem("turned"), TURNS(1, "ffn") - 4 + c + 1)
                a.copy(r_hT[:, 2 * c:2 * c + 2, :], bank(4 + c)).then_inc(sem("router_hT"), 1)
            act.wait_ge(sem("logit_rel"), 1)
            a.activation(e_gate[:], logit[:], ACT.Exp).then_inc(sem("e_gate"), 1)

            def gather_hi(k, half, i):
                act.wait_ge(sem("gathered"), k)
                a.copy(g_hT[0][:, 4 * half:4 * half + 4, :],
                       bank(GATHER_BANK[half])[:, 0].rearrange("p (c t) -> p c t", c=4)
                       ).then_inc(sem("gather_hi"), 1)

            gather_hi(1, 0, 0)
            act.wait_ge(sem("planned"), 1)
            act.wait_ge(sem("y_zero"), 2)
            a.preload_act_table_set("silu_and_others")
            n_items = act.value_load(plan[0:1, 0:1], min_val=E, max_val=E + MORE)
            with act.Fori(0, n_items) as i:
                def hi_m(q):
                    n = M0 + q
                    if n % 2 == 0:
                        act.wait_ge(landed[raw_slot(n // 2)],
                                    16 * raw_uses(n // 2) + i * (16 * (ITEM_BLOCKS // RAW_RING)))
                    act.wait_ge(used, n - 5 + i * N_ITEM)
                    a.copy(w_hi[q % RING][:], piece_src(n)).then_inc(hi_done, 1)

                KD = DSTEPS
                for q in range(N_ITEM):
                    hi_m(q)
                    if q == 3:
                        gather_hi(2 + i * 2, 1, i)
                    if q == 4:
                        act.wait_ge(used, M0 + i * N_ITEM)
                        a.copy(y_sb[:], bank(4, 2).rearrange("p b n -> p (b n)")).then_inc(sem("y_out"), 1)
                    if q == 8:
                        gate_silu(M0 + 4 + i * N_ITEM, bank(0)[:, 0], sg[:])
                    if q > 8 and (q - 16) % 12 == 0 and q < 80:
                        j = (q - 16) // 12 + 1
                        a_hi(KD + j - 1 + i * ESTEPS, bank(6)[:, 0].rearrange("p (c t) -> p c t", c=4), aT[0][:])
                        gate_silu(M0 + q - 4 + i * N_ITEM, bank(j % 2)[:, 0], sg[:])
                        if j == 3:
                            act.wait_ge(sem("place_ps"), 1 + i)
                            a.copy(place[:], bank(7)[:, 0, 0:T]).then_inc(sem("place"), 1)
                a_hi(KD + ESTEPS - 1 + i * ESTEPS, bank(6)[:, 0].rearrange("p (c t) -> p c t", c=4), aT[0][:])
                gather_hi(3 + i * 2, 0, i)
            act.wait_ge(used, M0 + n_items * N_ITEM)
            a.copy(y_sb[:], bank(4, 2).rearrange("p b n -> p (b n)")).then_inc(sem("y_out"), 1)
            act.wait_ge(sem("x_added"), 3 * 4 + 4 + 4 * n_items)
            sum_squares(x_sb)
            inv_root(FINAL, "mix")

        @block.vector
        def _(dve):
            v = nc.vector
            own = [0]

            def link(ins):
                own[0] += 1
                ins.then_inc(sem("dve_chain"), 1)
                dve.wait_ge(sem("dve_chain"), own[0])

            def lo(first, count=1):
                for n in range(first, first + count):
                    dve.wait_ge(hi_done, n + 1)
                    v.tensor_tensor(w_lo[slot_in(n)][:], piece_src(n), w_hi[slot_in(n)][:].bitcast(F32),
                                    ALU.subtract).then_inc(split, 1)

            def variance(stage, name, n):
                c = slice(*COLS[name])
                dve.wait_ge(sem("squares"), stage)
                v.tensor_scalar(stat[:, c], stat[:, c], 1.0 / n, EPS, ALU.mult, ALU.add).then_inc(sem("variance"), 1)

            def scale(stage, gains, src, name, lo_, w, width):
                dve.wait_ge(sem("rstd"), stage)
                if gains:
                    dve.wait_ge(sem("gain"), 16 * gains)
                else:
                    dve.wait_ge(sem("first_gain"), 16)
                col = COLS[name][0]
                for b in range(TB):
                    for f in range(width // w):
                        c = slice(lo_ + f * w, lo_ + (f + 1) * w)
                        ins = v.scalar_tensor_tensor(out=xn[:, b, c], in0=src[:, b, c], scalar=rstd[:, col:col + 1],
                                                     in1=gain[:, c], op0=ALU.mult, op1=ALU.mult)
                        col += 1
                ins.then_inc(sem("normed"), 1)

            def turn_lo(done, h, k0, tiles, first_bank):
                for c in range(tiles // 2):
                    k = slice(k0 + 2 * c, k0 + 2 * c + 2)
                    dve.wait_ge(sem("turn_hi"), done + c + 1)
                    v.tensor_tensor(h[1][:, k, :], bank(first_bank + c)[:, 0].rearrange("p (c t) -> p c t", c=2),
                                    h[0][:, k, :].bitcast(F32), ALU.subtract).then_inc(sem("turn_lo"), 1)

            def conv_half(l, h):
                dve.wait_ge(sem("moved"), 6 * l + h + 1)
                par = lambda k, c: conv_par[:, l * NCP + k * CT + c:l * NCP + k * CT + c + 1]
                for k in range(TAPS):
                    for c in range(4 * h, 4 * h + 4):
                        src = xbc[:, c, k:k + T]
                        if k == 0:
                            ins = v.tensor_scalar(conv[:, c], src, par(0, c), par(TAPS, c), ALU.mult, ALU.add)
                        else:
                            ins = v.scalar_tensor_tensor(out=conv[:, c], in0=src, scalar=par(k, c), in1=conv[:, c],
                                                         op0=ALU.mult, op1=ALU.add)
                    if k < TAPS - 1:
                        link(ins)
                ins.then_inc(sem("convolved"), 1)

            def mixer_dve(l):
                n0, o0 = seg[f"in{l}"], seg[f"out{l}"]
                heads = lambda t: t.rearrange("p (h d) -> p h d", h=HEADS)
                if l == 0:
                    dve.wait_ge(sem("x_landed"), 16)
                variance(STAGE(l, "mix"), "mix", D)
                scale(STAGE(l, "mix"), GAINS(l, "mix"), x_sb, "mix", 0, D, D)
                v.memset(xbc[:, :, 0:PAD], 0.0).then_inc(sem("padded"), 1)
                lo(n0, 4)
                turn_lo(TURNS(l, "mix") - 4, mixer_hT, 0, KT, 4)
                if l == 0:
                    dve.wait_ge(sem("w_dt_hi"), 1)
                    v.tensor_tensor(w_dt[1][:], w_dt_raw[:], w_dt[0][:].bitcast(F32), ALU.subtract
                                    ).then_inc(sem("w_dt_lo"), 1)
                lo(n0 + 4, 4)
                dve.wait_ge(sem("par_out"), 1)
                dve.wait_ge(sem("padded"), l + 1)
                conv_half(l, 0)
                lo(n0 + 8, 4)
                conv_half(l, 1)
                dve.wait_ge(sem("dt_ps"), l + 1)
                bias = dt_par[:, 0, l, :].unsqueeze(1).broadcast_to([P, TB, HEADS])
                v.tensor_tensor(dt_v[:], psum[:, 4, 0:TB * HEADS].rearrange("p (b h) -> p b h", b=TB), bias,
                                ALU.add).then_inc(sem("dt_raw"), 1)
                lo(n0 + 12, 4)
                dve.wait_ge(sem("dt_rest"), l + 1)
                link(v.scalar_tensor_tensor(out=dt_b[:], in0=dt_v[:], scalar=0.0, in1=dt_a[:], op0=ALU.max,
                                            op1=ALU.add))
                dve.wait_ge(sem("exp_a"), 1)
                link(v.scalar_tensor_tensor(out=dA[:], in0=dt_b[:], scalar=-1.0,
                                            in1=dt_par[:, 1, l, :].unsqueeze(1).broadcast_to([P, TB, HEADS]),
                                            op0=ALU.mult, op1=ALU.mult))
                for c in range(TB):
                    v.tensor_tensor(seg_rhs[:, c], tri_le[:].unsqueeze(1).broadcast_to([P, HEADS, P]),
                                    dA[:, c].unsqueeze(2).broadcast_to([P, HEADS, P]), ALU.mult
                                    ).then_inc(sem("seg_rhs"), 1)
                lo(n0 + 16, 2)
                dve.wait_ge(sem("tokened"), l + 1)
                v.tensor_copy(b_tok[:], bank(6)[:, 0, 0:GROUPS * P].rearrange("p (g n) -> p g n", g=GROUPS)
                              ).then_inc(sem("b_tok"), 1)
                dve.wait_ge(sem("cb_ps"), l + 1)
                link(v.tensor_tensor(cb_m[:].rearrange("p c g t -> p (c g) t"),
                                     bank(7)[:, 0].rearrange("p (c t) -> p c t", c=TB * GROUPS),
                                     tri_le[:].unsqueeze(1).broadcast_to([P, TB * GROUPS, P]), ALU.mult))
                dve.wait_ge(sem("x_tok"), l + 1)
                for c in range(TB):
                    ins = v.tensor_tensor(heads(x_dt[:, c]), heads(x_tok[:, c]),
                                          dt_b[:, c].unsqueeze(2).broadcast_to([P, HEADS, HD]), ALU.mult)
                ins.then_inc(sem("x_dt"), 1)
                lo(n0 + 18, 4)
                dve.wait_ge(sem("decay"), TB * l + 1)
                dve.wait_ge(sem("x_dt"), l + 1)
                v.tensor_tensor(heads(x_state[:]), heads(x_dt[:, 0]),
                                decay[:, 0, :, P - 1:P].broadcast_to([P, HEADS, HD]), ALU.mult
                                ).then_inc(sem("x_state"), 1)
                dve.wait_ge(sem("x_state"), l + 1)
                for c in range(TB):
                    dve.wait_ge(sem("decay"), TB * l + c + 1)
                    d4 = decay[:, c].rearrange("p (g r) t -> p g r t", g=GROUPS)
                    v.tensor_tensor(d4, d4, cb_m[:, c].unsqueeze(2).broadcast_to([P, GROUPS, HG, P]), ALU.mult
                                    ).then_inc(sem("masked_decay"), 1)
                lo(n0 + 22, 2)
                for c in range(TB):
                    y = mix[:, c, AW:2 * AW]
                    link(v.tensor_tensor(heads(y), heads(x_tok[:, c]),
                                         dt_par[:, 2, l, :].unsqueeze(2).broadcast_to([P, HEADS, HD]), ALU.mult))
                    dve.wait_ge(sem("y_diag"), TB * l + c + 1)
                    link(v.tensor_tensor(y, y, bank(5 + c)[:, 0], ALU.add))
                    if c == 1:
                        dve.wait_ge(sem("y_off"), l + 1)
                        dve.wait_ge(sem("e_cum"), l + 1)
                        link(v.tensor_tensor(heads(y_off[:]), heads(bank(7)[:, 0]),
                                             e_cum[:].unsqueeze(2).broadcast_to([P, HEADS, HD]), ALU.mult))
                        link(v.tensor_tensor(y, y, y_off[:], ALU.add))
                    dve.wait_ge(sem("moved"), 6 * l + 3)
                    v.tensor_tensor(y, y, z_act[:, c], ALU.mult).then_inc(sem("y_done"), 1)

                def soft_part(p):
                    dve.wait_ge(sem("rest"), 4 * l + p + 1)
                    if p >= 2:
                        dve.wait_ge(sem("cummed"), 4 * l + p - 1)
                    s = soft[p % 2]
                    link(v.scalar_tensor_tensor(out=s[:], in0=bank(ZB[p % 2], 2)[:, :, 0:W3], scalar=0.0,
                                                in1=rest[p % 2][:], op0=ALU.max, op1=ALU.add))
                    for h in range(2):
                        d = diag(s[:, h])
                        ins = v.tensor_tensor(d, d, tri_lt[:].unsqueeze(1).broadcast_to([P, 2, P]), ALU.mult)
                    ins.then_inc(sem("soft"), 1)

                def mask_part(p):
                    dve.wait_ge(sem("prob"), 4 * l + p + 1)
                    for h in range(2):
                        d = diag(prob[p % 2][:, h])
                        ins = v.scalar_tensor_tensor(out=d, in0=d, scalar=2.0,
                                                     in1=tri_lt[:].unsqueeze(1).broadcast_to([P, 2, P]),
                                                     op0=ALU.min, op1=ALU.mult)
                    ins.then_inc(sem("masked"), 1)

                soft_part(0)
                lo(n0 + 24, 2)
                soft_part(1)
                mask_part(0)
                lo(n0 + 26, 2)
                soft_part(2)
                variance(STAGE(l, "ssd"), "ssd", GW)
                mask_part(1)
                scale(STAGE(l, "ssd"), GAINS(l, "ssd"), mix, "ssd", AW, GW, AW)
                soft_part(3)
                mask_part(2)
                turn_lo(TURNS(l, "ssd") - 2, mixer_hT, XT, XT, 2)
                lo(n0 + 28)
                mask_part(3)
                lo(n0 + 29)
                variance(STAGE(l, "attn"), "attn", AW)
                scale(STAGE(l, "attn"), GAINS(l, "attn"), mix, "attn", 0, AW, AW)
                lo(n0 + 30)
                turn_lo(TURNS(l, "attn") - 2, mixer_hT, 0, XT, 4)
                lo(n0 + 31)
                for h in range(2):
                    dve.wait_ge(used, o0 + 6 + 2 * h)
                    for b in range(TB):
                        xs = x_sb[:, b, h * BANK:(h + 1) * BANK]
                        v.tensor_tensor(xs, xs, bank(OUT_BANK[h] + b)[:, 0], ALU.add).then_inc(sem("x_added"), 1)

            def a_lo(k, src, dst_hi, dst_lo):
                dve.wait_ge(sem("a_hi"), k + 1)
                v.tensor_tensor(dst_lo, src, dst_hi.bitcast(F32), ALU.subtract).then_inc(sem("hidden_split"), 1)

            def glu(k, pieces, sg_, up, dst):
                dve.wait_ge(sem("silu"), k + 1)
                dve.wait_ge(used, pieces)
                v.tensor_tensor(dst, sg_, up, ALU.mult).then_inc(sem("hidden"), 1)

            mixer_dve(0)

            dve.wait_ge(sem("x_added"), 4)
            variance(STAGE(0, "ffn"), "ffn", D)
            scale(STAGE(0, "ffn"), GAINS(0, "ffn"), x_sb, "ffn", 0, D, D)
            d0 = seg["dense"]
            lo(d0, 4)
            turn_lo(TURNS(0, "ffn") - 4, dense_hT, 0, KT, 4)
            two = lambda ap: ap.rearrange("p (b n) -> p b n", b=2)
            for j in range(DSTEPS):
                base = d0 + (0 if j == 0 else 4 + 6 * (j - 1))
                if j >= 1:
                    for q in range(2):
                        lo(base + q)
                    glu(j - 1, base - (0 if j == 1 else 2), dense_h[:], two(bank(1)[:, 0]), dense_h[:])
                    for q in range(2, 6):
                        lo(base + q)
                    a_lo(j - 1, two(bank(2)[:, 0]), dense_aT[0][:], dense_aT[1][:])
            for q in range(N_DENSE - 2, N_DENSE):
                lo(d0 + q)
            glu(DSTEPS - 1, d0 + N_DENSE - 4, dense_h[:], two(bank(1)[:, 0]), dense_h[:])
            a_lo(DSTEPS - 1, two(bank(2)[:, 0]), dense_aT[0][:], dense_aT[1][:])
            dve.wait_ge(used, d0 + N_DENSE)
            for b in range(TB):
                for h in range(2):
                    xs = x_sb[:, b, h * BANK:(h + 1) * BANK]
                    v.tensor_tensor(xs, xs, bank(4 + 2 * b + h)[:, 0], ALU.add).then_inc(sem("x_added"), 1)
            dve.wait_ge(sem("x_added"), 8)
            mixer_dve(1)

            dve.wait_ge(sem("x_added"), 12)
            variance(STAGE(1, "ffn"), "ffn", D)
            scale(STAGE(1, "ffn"), GAINS(1, "ffn"), x_sb, "ffn", 0, D, D)
            dve.wait_ge(sem("consts"), ROUTE_CONSTS)
            dve.wait_ge(sem("logits"), 1)
            wide = [P, TB, E, E]
            link(v.tensor_copy(logit[:], psum[:, 0, 0:TB * E].rearrange("p (b e) -> p b e", b=TB)))
            mine, other = logit[:].unsqueeze(3).broadcast_to(wide), logit[:].unsqueeze(2).broadcast_to(wide)
            v.tensor_tensor(cmp_a[:], mine, other, ALU.is_lt)
            link(v.tensor_tensor(cmp_b[:], mine, other, ALU.is_equal))
            link(v.tensor_tensor(cmp_b[:], cmp_b[:], low8[:].unsqueeze(1).broadcast_to(wide), ALU.mult))
            link(v.tensor_tensor(cmp_a[:], cmp_a[:], cmp_b[:], ALU.add))
            link(v.tensor_reduce(rank[:], cmp_a[:], AX.X, ALU.add))
            v.tensor_scalar(chosen[:], rank[:], TOPK - 0.5, None, ALU.is_lt).then_inc(sem("chosen"), 1)
            link(v.tensor_reduce(r_max[:], logit[:], AX.X, ALU.max))
            v.tensor_tensor(logit[:], logit[:], r_max[:].unsqueeze(2).broadcast_to([P, TB, E]), ALU.subtract
                            ).then_inc(sem("logit_rel"), 1)
            dve.wait_ge(sem("e_gate"), 1)
            dve.wait_ge(sem("chosen"), 1)
            link(v.tensor_tensor(e_gate[:], e_gate[:], chosen[:], ALU.mult))
            link(v.tensor_reduce(r_max[:], e_gate[:], AX.X, ALU.add))
            link(v.reciprocal(r_max[:], r_max[:]))
            v.memset(slot_t[:, :, E:], -1.0)
            link(v.memset(gate_t[:, :, E:], 0.0))
            link(v.tensor_tensor(gate_t[:, :, 0:E], e_gate[:], r_max[:].unsqueeze(2).broadcast_to([P, TB, E]),
                                 ALU.mult))
            dve.wait_ge(sem("positions"), 1)
            pos = psum[:, 1, 0:TB * E].rearrange("p (b e) -> p b e", b=TB)
            v.tensor_copy(count[:], psum[:, 1, TB * E:(TB + 1) * E])
            link(v.scalar_tensor_tensor(out=pos1[:], in0=pos, scalar=1.0, in1=chosen[:], op0=ALU.add, op1=ALU.mult))
            v.tensor_scalar(slot_t[:, :, 0:E], pos1[:], -1.0, None, ALU.add).then_inc(sem("slots_main"), 1)
            link(v.tensor_scalar(over[:], count[:], float(P), None, ALU.is_gt))
            link(v.tensor_tensor(cmp_a[:, 0], over[:].unsqueeze(1).broadcast_to([P, E, E]), low8[:], ALU.mult))
            link(v.tensor_reduce(o_rank[:], cmp_a[:, 0], AX.X, ALU.add))
            v.tensor_reduce(plan_f[:, 0:1], over[:], AX.X, ALU.add)
            link(v.tensor_scalar(pos1[:], pos1[:], -1.0 - P, None, ALU.add))
            for q in range(MORE):
                link(v.scalar_tensor_tensor(out=sel[:], in0=o_rank[:], scalar=float(q), in1=over[:],
                                            op0=ALU.is_equal, op1=ALU.mult))
                both = sel[:].unsqueeze(1).broadcast_to([P, TB, E])
                link(v.tensor_tensor(tmp_e[:], pos1[:], both, ALU.mult))
                link(v.tensor_reduce(slot_t[:, :, E + q:E + q + 1], tmp_e[:], AX.X, ALU.add))
                link(v.tensor_tensor(tmp_e[:], gate_t[:, :, 0:E], both, ALU.mult))
                link(v.tensor_reduce(gate_t[:, :, E + q:E + q + 1], tmp_e[:], AX.X, ALU.add))
                link(v.tensor_tensor(tmp_e[:, 0], e_ids[:], sel[:], ALU.mult))
                link(v.tensor_reduce(plan_f[:, 1 + q:2 + q], tmp_e[:, 0], AX.X, ALU.add))
            link(v.tensor_scalar(plan_f[:, 0:1], plan_f[:, 0:1], float(E), None, ALU.add))
            v.tensor_copy(plan[:], plan_f[:]).then_inc(sem("planned"), 1)

            def make_pick(i, cnt):
                for b in range(TB):
                    ins = v.tensor_scalar(pick[:, b], slots[:], slot_t[:, b, bass.ds(i, 1)], None, ALU.is_equal)
                ins.then_inc(sem("pick"), 1)

            def gather_lo(k, half):
                dve.wait_ge(sem("gather_hi"), k)
                h = slice(4 * half, 4 * half + 4)
                v.tensor_tensor(g_hT[1][:, h, :], bank(GATHER_BANK[half])[:, 0].rearrange("p (c t) -> p c t", c=4),
                                g_hT[0][:, h, :].bitcast(F32), ALU.subtract).then_inc(sem("gather_lo"), 1)

            dve.wait_ge(sem("planned"), 1)
            make_pick(0, 1)
            v.memset(bank(4, 2), 0.0).then_inc(sem("y_zero"), 1)
            v.memset(place[:], 0.0).then_inc(sem("y_zero"), 1)
            gather_lo(1, 0)
            n_items = dve.value_load(plan[0:1, 0:1], min_val=E, max_val=E + MORE)
            KD = DSTEPS
            four = lambda ap: ap.rearrange("p (c t) -> p c t", c=4)
            with dve.Fori(0, n_items) as i:
                def lo_m(q):
                    n = M0 + q
                    dve.wait_ge(hi_done, n + 1 + i * N_ITEM)
                    v.tensor_tensor(w_lo[q % RING][:], piece_src(n), w_hi[q % RING][:].bitcast(F32), ALU.subtract
                                    ).then_inc(split, 1)

                for q in range(N_ITEM):
                    lo_m(q)
                    if q == 3:
                        gather_lo(2 + i * 2, 1)
                    if q == 9:
                        for b in range(TB):
                            dve.wait_ge(sem("combined"), b + 1 + i * TB)
                            for h in range(2):
                                xs = x_sb[:, b, h * BANK:(h + 1) * BANK]
                                v.tensor_tensor(xs, xs, bank(COMBINE[b][h])[:, 0], ALU.add
                                                ).then_inc(sem("x_added"), 1)
                    if q == 13:
                        for b in range(TB):
                            ins = v.tensor_scalar(pick_g[:, b], slots[:], slot_t[:, b, bass.ds(i, 1)],
                                                  gate_t[:, b, bass.ds(i, 1)], ALU.is_equal, ALU.mult)
                        ins.then_inc(sem("pick_g"), 1)
                    if q == 12:
                        glu(KD + i * ESTEPS, M0 + 8 + i * N_ITEM, sg[:], bank(2)[:, 0], act_h[:])
                    if q >= 20 and q % 12 == 8:
                        j = (q - 20) // 12 + 1
                        glu(KD + j + i * ESTEPS, M0 + q - 4 + i * N_ITEM, sg[:], bank(2 + j % 2)[:, 0], act_h[:])
                    if q >= 16 and q % 12 == 4 and q < 80:
                        j = (q - 16) // 12 + 1
                        a_lo(KD + j - 1 + i * ESTEPS, four(bank(6)[:, 0]), aT[0][:], aT[1][:])
                    if q == 60:
                        make_pick(i + 1, 2 + i)
                a_lo(KD + ESTEPS - 1 + i * ESTEPS, four(bank(6)[:, 0]), aT[0][:], aT[1][:])
                gather_lo(3 + i * 2, 0)
            for b in range(TB):
                dve.wait_ge(sem("combined"), b + 1 + n_items * TB)
                for h in range(2):
                    xs = x_sb[:, b, h * BANK:(h + 1) * BANK]
                    v.tensor_tensor(xs, xs, bank(COMBINE[b][h])[:, 0], ALU.add).then_inc(sem("x_added"), 1)
            variance(FINAL, "mix", D)
            scale(FINAL, GAINS(L, "mix"), x_sb, "mix", 0, D, D)

        @block.tensor
        def _(pe):
            def turn(k0, tiles, first_bank):
                for c in range(tiles // 2):
                    for k in range(2):
                        for b in range(TB):
                            at_ = (k0 + 2 * c + k) * P
                            ins = nc.tensor.transpose(psum[:, first_bank + c, k * T + b * P:k * T + b * P + P],
                                                      xn[:, b, at_:at_ + P], ident[:])
                    ins.then_inc(sem("turned"), 1)

            hi_lo = lambda n, c: [w[slot_in(n)][:].rearrange("p (k n) -> p k n", k=c) for w in (w_hi, w_lo)]

            def token_major(n, k0, kts, h, banks_of, first, last):
                wh, wl = hi_lo(n, kts)
                for kk in range(kts):
                    k = k0 + kk
                    for b in range(TB):
                        tok = slice(b * P, b * P + P)
                        ins = mm3(banks_of(b), h[0][:, k, tok], h[1][:, k, tok], wh[:, kk], wl[:, kk],
                                  first(k, b), last(k))
                ins.then_inc(used, 1)

            def mixer_pe(l):
                n0, o0 = seg[f"in{l}"], seg[f"out{l}"]
                if l == 0:
                    pe.wait_ge(sem("consts"), CONSTS)
                pe.wait_ge(sem("normed"), STAGE(l, "mix"))
                turn(0, KT, 4)
                pe.wait_ge(sem("turn_lo"), TURNS(l, "mix"))
                hh, hl = mixer_hT

                def project(grp, q):
                    if q == 0 and grp >= 2:
                        pe.wait_ge(sem("moved"), 6 * l + grp - 1)
                    b0, n = 2 * (grp % 2), n0 + 4 * grp + q
                    pe.wait_ge(split, n + 1)
                    if grp in (2, 5):
                        token_major(n, 2 * q, 2, mixer_hT, lambda b: psum[:, b0 + b, :],
                                    lambda k, b: k == 0, lambda k: k == KT - 1)
                        return
                    wh, wl = hi_lo(n, 2)
                    for kk in range(2):
                        k = 2 * q + kk
                        for c in range(4):
                            ch = slice(c * P, c * P + P)
                            ins = mm3(psum[:, b0 + c // 2, (c % 2) * T:(c % 2) * T + T], wh[:, kk, ch],
                                      wl[:, kk, ch], hh[:, k], hl[:, k], k == 0 and c % 2 == 0, k == KT - 1)
                    ins.then_inc(used, 1)

                def project_group(grp):
                    for q in range(4):
                        project(grp, q)

                def scores(p):
                    if p == 0:
                        pe.wait_ge(sem("moved"), 6 * l + 5)
                    elif p == 1:
                        pe.wait_ge(sem("y_done"), TB * (l + 1))
                    else:
                        pe.wait_ge(sem("prob"), 4 * l + p - 1)
                    for s in range(2):
                        part = slice(s * HD, (s + 1) * HD)
                        ps = psum[:, ZB[p % 2] + s, :]
                        mm(ps[:, 0:T], kT[part, p, 0:P], qT[part, p, :])
                        ins = mm(ps[:, T:W3], kT[part, p, P:T], qT[part, p, P:T], start=False)
                    ins.then_inc(sem("scores"), 1)

                def cums(p):
                    pe.wait_ge(sem("soft"), 4 * l + p + 1)
                    for s in range(2):
                        ps, sf = psum[:, ZB[p % 2] + s, :], soft[p % 2][:, s]
                        mm(ps[:, 0:T], neg_ge[:], sf[:, 0:T], start=False)
                        mm(ps[:, P:T], neg_one[:], sf[:, T:W3], start=False)
                        ins = mm(ps[:, T:W3], neg_ge[:], sf[:, T:W3], start=False)
                    ins.then_inc(sem("cummed"), 1)

                def values(p):
                    if p == 0:
                        pe.wait_ge(sem("moved"), 6 * l + 6)
                    pe.wait_ge(sem("masked"), 4 * l + p + 1)
                    for s in range(2):
                        h, w = 2 * p + s, prob[p % 2][:, s]
                        col = slice(h * HD, (h + 1) * HD)
                        mm(psum[:, 4, col], w[:, 0:P], v_tok[:, 0, col])
                        mm(psum[:, 5, col], w[:, P:T], v_tok[:, 0, col], stop=False)
                        ins = mm(psum[:, 5, col], w[:, T:W3], v_tok[:, 1, col], start=False)
                    ins.then_inc(sem("pv"), 1)

                def out_piece(m):
                    n, h = o0 + m, m // 2 % 2
                    k0 = (XT if m < 4 else 0) + 2 * (m % 2)
                    pe.wait_ge(split, n + 1)
                    token_major(n, k0, 2, mixer_hT, lambda b: psum[:, OUT_BANK[h] + b, :],
                                lambda k, b: k == XT, lambda k: k == XT - 1)

                project_group(0)
                if l == 0:
                    pe.wait_ge(sem("params"), PARAMS)
                    nc.tensor.transpose(psum[:, 5, 0:L * NCP], conv_raw[:], ident[0:L * NCP, 0:L * NCP]
                                        ).then_inc(sem("par_turned"), 1)
                project_group(1)
                pe.wait_ge(sem("w_dt_lo"), 1)
                for b in range(TB):
                    tok = slice(b * P, b * P + P)
                    for k in range(KT):
                        ins = mm3(psum[:, 4, b * HEADS:(b + 1) * HEADS], hh[:, k, tok], hl[:, k, tok],
                                  w_dt[0][:, l, k], w_dt[1][:, l, k], k == 0, k == KT - 1)
                ins.then_inc(sem("dt_ps"), 1)
                project_group(2)
                pe.wait_ge(sem("conv_act"), 2 * l + 2)
                pe.wait_ge(sem("dt_raw"), l + 1)
                pe.wait_ge(sem("par_out"), 1)
                for b in range(TB):
                    for c in range(XT):
                        nc.tensor.transpose(psum[:, 4 + b, c * P:c * P + P], conv[:, c, b * P:b * P + P], ident[:])
                for g in range(GROUPS):
                    ins = nc.tensor.transpose(psum[:, 6, g * P:g * P + P], conv[:, XT + g, 0:P], ident[:])
                ins.then_inc(sem("tokened"), 1)
                for c in range(TB):
                    for g in range(GROUPS):
                        at_ = (c * GROUPS + g) * P
                        ins = mm(psum[:, 7, at_:at_ + P], conv[:, XT + g, c * P:c * P + P],
                                 conv[:, XT + GROUPS + g, c * P:c * P + P])
                ins.then_inc(sem("cb_ps"), 1)
                project_group(3)
                pe.wait_ge(sem("x_tok"), l + 1)
                pe.wait_ge(sem("x_dt"), l + 1)
                for c in range(TB):
                    pe.wait_ge(sem("seg_rhs"), TB * l + c + 1)
                    for h in range(2):
                        ins = mm(psum[:, 4 + 2 * c + h, :], tri_gt[:],
                                 seg_rhs[:, c, 4 * h:4 * h + 4, :].rearrange("p h t -> p (h t)"))
                    ins.then_inc(sem("segsum"), 1)
                project_group(4)
                pe.wait_ge(sem("decay"), TB * (l + 1))
                mm(psum[:, 4, 0:HEADS], tri_le[:], dA[:, 1, :])
                pe.wait_ge(sem("b_tok"), l + 1)
                pe.wait_ge(sem("x_state"), l + 1)
                for g in range(GROUPS):
                    ins = mm(psum[:, 7, g * GW:(g + 1) * GW], b_tok[:, g, :], x_state[:, g * GW:(g + 1) * GW])
                ins.then_inc(sem("stated"), 1)
                for c in range(TB):
                    pe.wait_ge(sem("masked_decay"), TB * l + c + 1)
                    for h in range(HEADS):
                        ins = mm(psum[:, 5 + c, h * HD:(h + 1) * HD], decay[:, c, h, :],
                                 x_dt[:, c, h * HD:(h + 1) * HD])
                    ins.then_inc(sem("y_diag"), 1)
                project(5, 0)
                pe.wait_ge(sem("state_out"), l + 1)
                for g in range(GROUPS):
                    ins = mm(psum[:, 7, g * GW:(g + 1) * GW], conv[:, XT + GROUPS + g, P:2 * P],
                             state[:, g * GW:(g + 1) * GW])
                ins.then_inc(sem("y_off"), 1)
                scores(0)
                project(5, 1)
                scores(1)
                cums(0)
                project(5, 2)
                scores(2)
                project(5, 3)
                cums(1)
                values(0)
                scores(3)
                cums(2)
                pe.wait_ge(sem("normed"), STAGE(l, "ssd"))
                turn(XT, XT, 2)
                values(1)
                cums(3)
                values(2)
                pe.wait_ge(sem("turn_lo"), TURNS(l, "ssd"))
                pe.wait_ge(sem("prob"), 4 * l + 3)
                out_piece(0)
                values(3)
                out_piece(1)
                out_piece(2)
                out_piece(3)
                pe.wait_ge(sem("normed"), STAGE(l, "attn"))
                turn(0, XT, 4)
                pe.wait_ge(sem("turn_lo"), TURNS(l, "attn"))
                for m in range(4, 8):
                    out_piece(m)

            mixer_pe(0)

            pe.wait_ge(sem("normed"), STAGE(0, "ffn"))
            turn(0, KT, 4)
            pe.wait_ge(sem("turn_lo"), TURNS(0, "ffn"))
            d0 = seg["dense"]
            for j in range(DSTEPS + 1):
                base = d0 + (0 if j == 0 else 4 + 6 * (j - 1))
                for up in range(2):
                    if j < DSTEPS:
                        for q in range(2):
                            n = base + 2 * up + q
                            pe.wait_ge(split, n + 1)
                            ps = psum[:, 1 if up else (0, 3)[j % 2], :]
                            token_major(n, 4 * q, 4, dense_hT, lambda b: ps[:, b * DS:(b + 1) * DS],
                                        lambda k, b: k == 0 and b == 0, lambda k: k == KT - 1)
                    if up == 0 and j >= 1:
                        pe.wait_ge(sem("hidden"), j)
                        for c in range(2):
                            for b in range(TB):
                                ins = nc.tensor.transpose(
                                    psum[:, 2, c * T + b * P:c * T + b * P + P],
                                    dense_h[:, b].rearrange("p (f c) -> p c f", c=2)[:, c], ident[:])
                        ins.then_inc(sem("hidden_turned"), 1)
                if j >= 1:
                    pe.wait_ge(sem("hidden_split"), j)
                    for c in range(2):
                        n = base + (4 if j < DSTEPS else 0) + c
                        pe.wait_ge(split, n + 1)
                        wh, wl = hi_lo(n, 2)
                        for b in range(TB):
                            for h in range(2):
                                tok = slice(b * P, b * P + P)
                                ins = mm3(psum[:, 4 + 2 * b + h, :], dense_aT[0][:, c, tok], dense_aT[1][:, c, tok],
                                          wh[:, h], wl[:, h], j == 1 and c == 0, j == DSTEPS and c == 1)
                        ins.then_inc(used, 1)

            mixer_pe(1)

            pe.wait_ge(sem("normed"), STAGE(1, "ffn"))
            turn(0, KT, 4)
            pe.wait_ge(sem("router_hT"), 4)
            pe.wait_ge(sem("router_in"), 16)
            for b in range(TB):
                for k in range(KT):
                    ins = mm(psum[:, 0, b * E:(b + 1) * E], r_hT[:, k, b * P:b * P + P], router[:, k], k == 0,
                             k == KT - 1)
            ins.then_inc(sem("logits"), 1)
            pe.wait_ge(sem("chosen"), 1)
            mm(psum[:, 1, 0:E], tri_lt[:], chosen[:, 0])
            mm(psum[:, 1, E:2 * E], ones[:], chosen[:, 0], stop=False)
            mm(psum[:, 1, E:2 * E], tri_lt[:], chosen[:, 1], start=False)
            mm(psum[:, 1, 2 * E:3 * E], ones[:], chosen[:, 0], stop=False)
            mm(psum[:, 1, 2 * E:3 * E], ones[:], chosen[:, 1], start=False).then_inc(sem("positions"), 1)

            def gather(half):
                for kk in range(4):
                    k = 4 * half + kk
                    for b in range(TB):
                        ins = mm(psum[:, GATHER_BANK[half], kk * P:kk * P + P], xn[:, b, k * P:k * P + P],
                                 pick[:, b], b == 0, b == TB - 1)
                ins.then_inc(sem("gathered"), 1)

            pe.wait_ge(sem("pick"), 1)
            gather(0)
            gather(1)
            pe.wait_ge(sem("y_zero"), 2)
            n_items = pe.value_load(plan[0:1, 0:1], min_val=E, max_val=E + MORE)
            KD = DSTEPS

            def combine():
                for b in range(TB):
                    for h in range(2):
                        ins = mm(bank(COMBINE[b][h])[:, 0], place[:, b * P:b * P + P],
                                 y_sb[:, h * BANK:(h + 1) * BANK])
                    ins.then_inc(sem("combined"), 1)

            with pe.Fori(0, n_items) as i:
                def expert_up(q0, ps, wait_half):
                    for q in range(4):
                        n = M0 + q0 + q
                        if wait_half and q == 2:
                            pe.wait_ge(sem("gather_lo"), 2 + i * 2)
                        pe.wait_ge(split, n + 1 + i * N_ITEM)
                        wh, wl = hi_lo(n, 2)
                        for kk in range(2):
                            k = 2 * q + kk
                            ins = mm3(ps, g_hT[0][:, k], g_hT[1][:, k], wh[:, kk], wl[:, kk], k == 0, k == KT - 1)
                        ins.then_inc(used, 1)

                def turn_hidden(j):
                    pe.wait_ge(sem("hidden"), KD + j + 1 + i * ESTEPS)
                    for c in range(4):
                        ins = nc.tensor.transpose(psum[:, 6, c * P:c * P + P],
                                                  act_h[:].rearrange("p (f c) -> p c f", c=4)[:, c], ident[:])
                    ins.then_inc(sem("hidden_turned"), 1)

                def expert_down(q0, j):
                    pe.wait_ge(sem("hidden_split"), KD + j + 1 + i * ESTEPS)
                    for c in range(4):
                        n = M0 + q0 + c
                        pe.wait_ge(split, n + 1 + i * N_ITEM)
                        wh, wl = hi_lo(n, 2)
                        for h in range(2):
                            ins = mm3(psum[:, 4 + h, :], aT[0][:, c], aT[1][:, c], wh[:, h], wl[:, h],
                                      j == 0 and c == 0, j == ESTEPS - 1 and c == 3)
                        ins.then_inc(used, 1)

                for j in range(ESTEPS):
                    q0 = 0 if j == 0 else 8 + 12 * (j - 1)
                    if j == 0:
                        pe.wait_ge(sem("gather_lo"), 1 + i * 2)
                    if j == 1:
                        pe.wait_ge(sem("x_added"), 16 + i * 4)
                    expert_up(q0, psum[:, j % 2, :], j == 0)
                    if j == 0:
                        pe.wait_ge(sem("y_out"), 1 + i)
                        combine()
                    else:
                        turn_hidden(j - 1)
                    expert_up(q0 + 4, psum[:, 2 + j % 2, :], False)
                    if j >= 1:
                        expert_down(q0 + 8, j - 1)
                    if j == 2:
                        pe.wait_ge(sem("pick_g"), 1 + i)
                        for b in range(TB):
                            ins = nc.tensor.transpose(psum[:, 7, b * P:b * P + P], pick_g[:, b], ident[:])
                        ins.then_inc(sem("place_ps"), 1)
                turn_hidden(ESTEPS - 1)
                pe.wait_ge(sem("place"), 1 + i)
                pe.wait_ge(sem("pick"), 2 + i)
                gather(0)
                expert_down(N_ITEM - 4, ESTEPS - 1)
                gather(1)
            pe.wait_ge(sem("y_out"), 1 + n_items)
            pe.wait_ge(sem("gather_lo"), 1 + n_items * 2)
            combine()
    return nc


_INS = ["x", "mix_norm_g", "w_in", "conv_w", "conv_b", "dt_bias", "a_log", "d_skip", "attn_norm_g", "ssd_norm_g",
        "w_out", "ffn_norm_g", "dense_w_gate", "dense_w_up", "dense_w_down", "router_w", "moe_w_gate",
        "moe_w_up", "moe_w_down", "final_norm_g"]


def kernel(**inputs):
    import numpy as _np
    import concourse.bacc as _bacc
    from concourse import mybir as _mybir
    from concourse.bass_utils import run_bass_kernel_spmd as _run

    nc = _bacc.Bacc("TRN2", target_bir_lowering=False, num_devices=1)
    arrays, args = {}, []
    for name in _INS:
        a = _np.ascontiguousarray(inputs[name])
        arrays[f"in_{name}"] = a
        args.append(nc.dram_tensor(f"in_{name}", a.shape, _mybir.dt.from_np(a.dtype), kind="ExternalInput").ap())
    shape = inputs["x"].shape
    args.append(nc.dram_tensor("out_0", shape, _mybir.dt.float32, kind="ExternalOutput").ap())
    hybrid_trunk(nc, *args)
    r = _run(nc, [arrays], core_ids=[0])
    return r.results[0]["out_0"]
```

```python
import numpy as np

import concourse.bass as bass
from concourse import mybir
from contextlib import ExitStack

ALU = mybir.AluOpType
ACT = mybir.ActivationFunctionType
AX = mybir.AxisListType
F32 = mybir.dt.float32
F32R = mybir.dt.float32r
I32 = mybir.dt.int32

P = 128
BANK = 512
EPS = 1e-5
RAW_RING = 14
FRONT = 7
RING = 6
PIECE = 1024
BLOCK = 2 * PIECE


def hybrid_trunk(nc, x, mix_norm_g, w_in, conv_w, conv_b, dt_bias, a_log, d_skip, attn_norm_g, ssd_norm_g,
                 w_out, ffn_norm_g, dense_w_gate, dense_w_up, dense_w_down, router_w, moe_w_gate,
                 moe_w_up, moe_w_down, final_norm_g, out):
    _, T, D = x.shape
    L = w_in.shape[0]
    TB, KT = T // P, D // P
    HEADS = dt_bias.shape[1]
    AW = attn_norm_g.shape[1]
    HD = AW // HEADS
    TAPS, CONV = conv_w.shape[1], conv_w.shape[2]
    CT = CONV // P
    XT = AW // P
    GROUPS = (CT - XT) // 2
    HG = HEADS // GROUPS
    GW = AW // GROUPS
    FF = dense_w_gate.shape[2]
    E, FE = moe_w_gate.shape[1], moe_w_gate.shape[3]
    TOPK = 2
    MORE = TOPK * T // (P + 1)
    ITEMS = E + MORE + 1
    OQ, OK_, OV, OZ = 0, AW, 2 * AW, 3 * AW
    OX, OBC = 4 * AW, 5 * AW
    ODT = OX + CONV
    assert (TB, KT, HEADS, HD, CT, XT, GROUPS, TAPS) == (2, 8, 8, 64, 8, 4, 2, 4) and L == 2 and AW == BANK

    DS = 256
    DSTEPS = FF // DS
    ES = 512
    ESTEPS = FE // ES

    def in_proj_blocks(l):
        w = w_in[l].rearrange("(c p) n -> p c n", p=P)
        return [w[:, 4 * h:4 * h + 4, o:o + BANK] for o in (OX, OBC, OZ, OQ, OK_, OV) for h in range(2)]

    def out_proj_blocks(l):
        w = w_out[l].rearrange("(c p) n -> p c n", p=P)
        return [w[:, 4 * h:4 * h + 4, o:o + BANK] for h in (1, 0) for o in (0, BANK)]

    def dense_blocks():
        wg = dense_w_gate[0].rearrange("(c p) n -> p c n", p=P)
        wu = dense_w_up[0].rearrange("(c p) n -> p c n", p=P)
        wd = dense_w_down[0].rearrange("(j p c) n -> j p c n", p=P, c=DS // P)
        blocks = []
        for j in range(DSTEPS):
            blocks += [wg[:, :, j * DS:j * DS + DS], wu[:, :, j * DS:j * DS + DS]]
            if j >= 1:
                blocks.append(wd[j - 1])
        return blocks + [wd[DSTEPS - 1]]

    def expert_blocks(e):
        pick = lambda w: w[0, bass.ds(e, 1)]
        wg = pick(moe_w_gate).rearrange("o (c p) n -> p (o c) n", p=P)
        wu = pick(moe_w_up).rearrange("o (c p) n -> p (o c) n", p=P)
        wd = pick(moe_w_down).rearrange("o (j p c) n -> j p (o c) n", p=P, c=ES // P)
        blocks = []
        for j in range(ESTEPS):
            blocks += [w[:, 4 * h:4 * h + 4, j * ES:j * ES + ES] for w in (wg, wu) for h in range(2)]
            if j >= 1:
                blocks += [wd[j - 1][:, 2 * h:2 * h + 2] for h in range(2)]
        return blocks + [wd[ESTEPS - 1][:, 2 * h:2 * h + 2] for h in range(2)]

    N_IN, N_DENSE, N_ITEM = 24, 6 * DSTEPS, 12 * ESTEPS
    fixed_blocks, seg = [], {}

    def add_part(name, blocks):
        seg[name] = 2 * len(fixed_blocks)
        fixed_blocks.extend(blocks)

    add_part("in0", in_proj_blocks(0))
    add_part("out0", out_proj_blocks(0))
    add_part("dense", dense_blocks())
    add_part("in1", in_proj_blocks(1))
    add_part("out1", out_proj_blocks(1))
    B0 = len(fixed_blocks)
    M0 = 2 * B0
    ITEM_BLOCKS = N_ITEM // 2
    assert ITEM_BLOCKS % RAW_RING == 0 and N_ITEM % RING == 0

    def raw_slot(n):
        return (n - B0) % (FRONT if n < B0 else RAW_RING)

    def raw_uses(n):
        return sum(raw_slot(m) == raw_slot(n) for m in range(n + 1))

    with ExitStack() as ctx:
        BASE = (nc.sbuf_base + 31) // 32 * 32
        cursor = [BASE]

        def area(size):
            at = cursor[0]
            cursor[0] += (size + 31) // 32 * 32
            assert cursor[0] <= nc.sbuf_usable_end, (cursor[0], nc.sbuf_usable_end)
            return at

        def at(name, shape, offset, dt=F32):
            return nc.alloc_sbuf_tensor_at(name, shape, dt, offset=offset)

        def size(shape):
            return 4 * int(np.prod(shape[1:]))

        class Region:
            def __init__(self, start, limit):
                self.next, self.end = start, start + limit

            def __call__(self, name, shape, dt=F32):
                t = at(name, shape, self.next, dt)
                self.next += (size(shape) + 31) // 32 * 32
                assert self.next <= self.end, (name, self.next - self.end)
                return t

        raw = at("raw", [P, RAW_RING, BLOCK], area(4 * RAW_RING * BLOCK))
        ring_at = area(RING * 2 * 4 * PIECE)
        w_hi = [at(f"w_hi{s}", [P, PIECE], ring_at + s * 8 * PIECE, F32R) for s in range(RING)]
        w_lo = [at(f"w_lo{s}", [P, PIECE], ring_at + s * 8 * PIECE + 4 * PIECE, F32R) for s in range(RING)]
        back_at = raw.manual_sbuf_range[0] + 4 * FRONT * BLOCK
        hT_at = raw.manual_sbuf_range[0] + 4 * (RAW_RING - 2) * BLOCK
        mixer_hT = [at(f"mixer_hT{s}", [P, KT, T], hT_at + s * 4 * BLOCK, F32R) for s in range(2)]
        scratch = Region(back_at, hT_at - back_at)
        x_tok = scratch("x_tok", [P, TB, AW])
        x_dt = scratch("x_dt", [P, TB, AW])
        z_act = scratch("z_act", [P, TB, AW])
        x_state = scratch("x_state", [P, AW])
        state = scratch("state", [P, AW])
        seg_rhs = scratch("seg_rhs", [P, TB, HEADS, P])
        decay = scratch("decay", [P, TB, HEADS, P])
        b_tok = scratch("b_tok", [P, GROUPS, P])
        dt_t = scratch("dt_t", [P, T])
        W3 = P * 3
        soft = [scratch(f"soft{s}", [P, 2, W3]) for s in range(2)]
        after_seg = Region(seg_rhs.manual_sbuf_range[0], size(seg_rhs.shape))
        rest = [after_seg(f"rest{s}", [P, 2, W3]) for s in range(2)]
        y_off = after_seg("y_off", [P, AW])
        after_dec = Region(decay.manual_sbuf_range[0], size(decay.shape))
        prob = [after_dec(f"prob{s}", [P, 2, W3]) for s in range(2)]

        x_sb = at("x_sb", [P, TB, D], area(4 * TB * D))
        gain = at("gain", [P, D], area(4 * D))
        ident = at("ident", [P, P], area(512))
        tri_le = at("tri_le", [P, P], area(512))
        tri_lt = at("tri_lt", [P, P], area(512))
        tri_gt = at("tri_gt", [P, P], area(512))
        neg_ge = at("neg_ge", [P, P], area(512))
        neg_one = at("neg_one", [P, P], area(512))
        ones = at("ones", [P, P], area(512))
        stat = at("stat", [P, 8], area(32))
        rstd = at("rstd", [P, 8], area(32))
        plan = at("plan", [P, 1 + MORE], area(32), I32)
        work_at = cursor[0]
        WORK = nc.sbuf_usable_end // 32 * 32 - work_at
        mixer = Region(work_at, WORK)
        xn = mixer("xn", [P, TB, D])
        conv = at("conv", [P, CT, T], work_at)
        qT = mixer("qT", [P, XT, T])
        kT = mixer("kT", [P, XT, T])
        v_tok = mixer("v_tok", [P, TB, AW])
        PAD = TAPS - 1
        xbc = mixer("xbc", [P, CT, PAD + T])
        mix = at("mix", [P, TB, D], xbc.manual_sbuf_range[0])
        NCP = TAPS * CT + CT
        ROWS = L * (NCP + KT)
        PARAM_BYTES = 4 * (ROWS + 2 * L * KT * HEADS + 3 * L * HEADS)
        params = Region(work_at + WORK - PARAM_BYTES, PARAM_BYTES)
        conv_par = params("conv_par", [P, ROWS])
        ffn_gain = lambda l, k: conv_par[:, L * NCP + l * KT + k:L * NCP + l * KT + k + 1]
        w_dt = [params(f"w_dt_{s}", [P, L, KT, HEADS], F32R) for s in range(2)]
        dt_par = params("dt_par", [P, 3, L, HEADS])
        cb_m = mixer("cb_m", [P, TB, GROUPS, P])
        w_dt_raw = at("w_dt_raw", [P, L, KT, HEADS], v_tok.manual_sbuf_range[0] + 512)
        dt_a = mixer("dt_a", [P, TB, HEADS])
        dt_b = mixer("dt_b", [P, TB, HEADS])
        dt_v = mixer("dt_v", [P, TB, HEADS])
        dA = mixer("dA", [P, TB, HEADS])
        e_cum = mixer("e_cum", [P, HEADS])
        assert mixer.next <= work_at + WORK - PARAM_BYTES
        conv_raw = at("conv_raw", [ROWS, P], v_tok.manual_sbuf_range[0])

        after_xn = work_at + size(xn.shape)
        dense = Region(after_xn, WORK - size(xn.shape))
        dense_hT = [dense(f"dense_hT{s}", [P, KT, T], F32R) for s in range(2)]
        dense_h = dense("dense_h", [P, TB, DS])
        dense_aT = [dense(f"dense_aT{s}", [P, DS // P, T], F32R) for s in range(2)]
        assert dense.next <= work_at + WORK - PARAM_BYTES
        moe = Region(after_xn, WORK - size(xn.shape))
        g_hT = [moe(f"g_hT{s}", [P, KT, P], F32R) for s in range(2)]
        r_hT = at("r_hT", [P, KT, T], after_xn)
        act_h = moe("act_h", [P, ES])
        aT = [moe(f"aT{s}", [P, ES // P, P], F32R) for s in range(2)]
        y = [moe(f"y{s}", [P, D], F32R) for s in range(2)]
        pick = moe("pick", [P, TB, P])
        place = at("place", [P, T], neg_ge.manual_sbuf_range[0], F32R)
        slot_gate = moe("slot_gate", [P, 1])
        slot_t = moe("slot_t", [P, TB, ITEMS])
        gate_t = moe("gate_t", [P, TB, ITEMS])
        slots = moe("slots", [P, P])
        route = Region(y[0].manual_sbuf_range[0], 2 * size(y[0].shape))
        low8 = route("low8", [P, E, E])
        router = route("router", [P, KT, E])
        logit_t = route("logit_t", [P, T])
        logit = route("logit", [P, TB, E])
        cmp_a = route("cmp_a", [P, TB, E, E])
        cmp_b = route("cmp_b", [P, TB, E, E])
        rank = route("rank", [P, TB, E])
        chosen = route("chosen", [P, TB, E])
        e_gate = route("e_gate", [P, TB, E])
        r_max = route("r_max", [P, TB])
        over = route("over", [P, E])
        o_rank = route("o_rank", [P, E])
        pos1 = route("pos1", [P, TB, E])
        tmp_e = route("tmp_e", [P, TB, MORE, E])
        sel = route("sel", [P, MORE, E])
        e_ids = route("e_ids", [P, E])
        plan_f = route("plan_f", [P, 1 + MORE])

        psum = ctx.enter_context(nc.psum_tensor("psum", [P, 8, BANK], F32))

        def bank(b, n=1):
            return psum[:, b:b + n, :]

        sems = {}

        def sem(name):
            if name not in sems:
                sems[name] = ctx.enter_context(nc.semaphore(name))
            return sems[name]

        landed = [sem(f"landed{s}") for s in range(RAW_RING)]
        hi_done = sem("hi_done")
        split = sem("split")
        used = sem("used")

        def piece_src(n):
            b = raw_slot(n // 2)
            return raw[:, b, (n % 2) * PIECE:(n % 2) * PIECE + PIECE]

        ZB = (0, 6)
        OUT_BANK = (0, 6)
        GATHER_BANK = (7, 2)
        COMBINE = ((1, 3), (6, 7))
        diag = lambda t: t.rearrange("p (a n) -> p a n", n=P)[:, 0:3:2, :]

        def slot_in(n):
            return (n - M0) % RING

        STAGE = lambda l, name: 4 * l + {"mix": 1, "ssd": 2, "attn": 3, "ffn": 4}[name]
        TURNS = lambda l, name: 12 * l + {"mix": 4, "ssd": 6, "attn": 8, "ffn": 12}[name]
        FINAL = 4 * L + 1
        Y_SPLIT, COMBINED = TURNS(L - 1, "attn"), TURNS(L - 1, "ffn")
        NORMED = lambda stage: stage - (stage >= STAGE(0, "ffn"))
        COLS = {"mix": (0, TB), "ffn": (0, TB), "ssd": (2, 2 + TB * GROUPS), "attn": (6, 6 + TB)}
        HALVES = [slice(0, BANK), slice(BANK, D)]

        def mm3(ps, a_hi, a_lo, b_hi, b_lo, start, stop):
            nc.tensor.matmul(ps, a_hi, b_hi, start=start, stop=False, skip_group_check=True)
            nc.tensor.matmul(ps, a_lo, b_hi, start=False, stop=False, skip_group_check=True)
            return nc.tensor.matmul(ps, a_hi, b_lo, start=False, stop=stop, skip_group_check=True)

        def mm(ps, a, b, start=True, stop=True):
            return nc.tensor.matmul(ps, a, b, start=start, stop=stop, skip_group_check=True)

        block = ctx.enter_context(nc.Block())

        @block.sync
        def _(sp):
            par = sem("params")
            x_in = x[0].rearrange("(b p) d -> p b d", p=P)
            for h in range(2):
                sp.dma_start(x_sb[:, :, HALVES[h]], x_in[:, :, HALVES[h]]).then_inc(sem(f"x_landed{h}"), 16)
            sp.dma_start(gain[:], mix_norm_g[0:1, :].broadcast_to([P, D])).then_inc(sem("first_gain"), 16)

            def load(n, src):
                dst = raw[:, raw_slot(n), :].rearrange("p (c n) -> p c n", c=src.shape[1])
                sp.dma_start(dst, src).then_inc(landed[raw_slot(n)], 16)

            for n, src in enumerate(fixed_blocks):
                if n == 2:
                    for l in range(L):
                        sp.dma_start(conv_raw[l * NCP:l * NCP + TAPS * CT, :],
                                     conv_w[l].rearrange("k (c p) -> (k c) p", p=P)).then_inc(par, 16)
                        sp.dma_start(conv_raw[l * NCP + TAPS * CT:(l + 1) * NCP, :],
                                     conv_b[l].rearrange("(c p) -> c p", p=P)).then_inc(par, 16)
                        sp.dma_start(w_dt_raw[:, l], w_in[l].rearrange("(c p) n -> p c n", p=P)[:, :, ODT:ODT + HEADS]
                                     ).then_inc(par, 16)
                        sp.dma_start(conv_raw[L * NCP + l * KT:L * NCP + (l + 1) * KT, :],
                                     ffn_norm_g[l].rearrange("(c p) -> c p", p=P)).then_inc(par, 16)
                    for k, v in enumerate((dt_bias, a_log, d_skip)):
                        flat = v.rearrange("l (o h) -> o (l h)", o=1)
                        sp.dma_start(dt_par[:, k].rearrange("p l h -> p (l h)"),
                                     flat.broadcast_to([P, L * HEADS])).then_inc(par, 16)
                if n >= FRONT:
                    sp.wait_ge(split, 2 * (n - FRONT) + 2)
                load(n, src)

            first = expert_blocks(0)
            early, scratch_slots = [FRONT, FRONT + 1], list(range(FRONT + 2, RAW_RING - 2))
            hT_slots = [RAW_RING - 2, RAW_RING - 1]
            for b in early + list(range(FRONT)) + scratch_slots + hT_slots:
                if b < FRONT:
                    sp.wait_ge(split, 2 * (B0 + b - FRONT) + 2)
                elif b == early[0]:
                    sp.wait_ge(sem("y_done"), TB * L)
                elif b == scratch_slots[0]:
                    sp.wait_ge(sem("normed"), NORMED(STAGE(L - 1, "attn")))
                elif b == hT_slots[0]:
                    sp.wait_ge(used, M0)
                load(B0 + b, first[b])

            def load_item(i, e, lo_, hi_):
                for b, src in enumerate(expert_blocks(e)):
                    if lo_ <= b < hi_:
                        sp.wait_ge(split, 2 * (B0 + b - RAW_RING) + 2 + i * N_ITEM)
                        load(B0 + b, src)

            with sp.Fori(0, E - 1) as e:
                load_item(e, e, RAW_RING, ITEM_BLOCKS)
                load_item(e + 1, e + 1, 0, RAW_RING)
            load_item(E - 1, E - 1, RAW_RING, ITEM_BLOCKS)
            sp.wait_ge(sem("planned"), 1)
            items = sp.value_load(plan[0:1, 0:1], min_val=E, max_val=E + MORE)
            for q in range(MORE):
                with sp.If(items > E + q):
                    e = sp.value_load(plan[0:1, 1 + q:2 + q], min_val=0, max_val=E - 1)
                    load_item(E + q, e, 0, ITEM_BLOCKS)
                with sp.Else():
                    pass
            final = out[0].rearrange("(b p) d -> p b d", p=P)
            sp.wait_ge(sem("half_normed"), L + 2)
            sp.dma_start(final[:, :, HALVES[0]], xn[:, :, HALVES[0]]).then_inc(sem("stored"), 16)
            sp.wait_ge(sem("normed"), NORMED(FINAL))
            sp.dma_start(final[:, :, HALVES[1]], xn[:, :, HALVES[1]]).then_inc(sem("stored"), 16)
            sp.wait_ge(sem("stored"), 32)

        @block.gpsimd
        def _(pool):
            g = nc.gpsimd
            cst = sem("consts")
            g.memset(ones[:], 1.0).then_inc(cst, 1)
            g.memset(neg_one[:], -1.0).then_inc(cst, 1)
            pool.wait_ge(cst, 2)
            tri = [(ident, ones, ALU.is_equal, [[-1, P]], 1, 0), (tri_le, ones, ALU.is_ge, [[1, P]], -1, 0),
                   (tri_lt, ones, ALU.is_gt, [[1, P]], -1, 0), (tri_gt, ones, ALU.is_gt, [[-1, P]], 1, 0),
                   (neg_ge, neg_one, ALU.is_ge, [[-1, P]], 1, 0)]
            for dst, src, op, pattern, mult, base in tri:
                g.affine_select(out=dst[:], in_=src[:], pattern=pattern, compare_op=op, fill=0.0, base=base,
                                channel_multiplier=mult).then_inc(cst, 1)

            def load_gain(stage, parts):
                pool.wait_ge(sem("normed"), NORMED(stage))
                for lo_, hi_, src in parts:
                    g.dma_start(gain[:, lo_:hi_], src.broadcast_to([P, hi_ - lo_])).then_inc(sem("gain"), 16)

            for l in range(L):
                load_gain(STAGE(l, "mix"), [(0, AW, attn_norm_g[l:l + 1, :]), (AW, D, ssd_norm_g[l:l + 1, :])])
                load_gain(STAGE(l, "attn"), [(0, D, (mix_norm_g if l == 0 else ffn_norm_g)[1:2, :])])
            g.dma_start(router[:], router_w[0].rearrange("(c p) e -> p c e", p=P)).then_inc(sem("router_in"), 16)
            g.affine_select(out=low8[:], in_=ones[:, 0:E * E].rearrange("p (a b) -> p a b", a=E),
                            pattern=[[1, E], [-1, E]], compare_op=ALU.is_gt, fill=0.0, base=0,
                            channel_multiplier=0).then_inc(cst, 1)
            g.iota(slots[:], [[1, P]], base=0, channel_multiplier=0,
                   allow_small_or_imprecise_dtypes=True).then_inc(cst, 1)
            g.iota(e_ids[:], [[1, E]], base=0, channel_multiplier=0,
                   allow_small_or_imprecise_dtypes=True).then_inc(cst, 1)
            load_gain(STAGE(L - 1, "ffn"), [(0, D, final_norm_g.rearrange("(o d) -> o d", o=1))])

        CONSTS, ROUTE_CONSTS = 7, 10
        GAINS = lambda l, name: 4 * l + {"mix": 0, "ssd": 2, "attn": 2, "ffn": 3}[name] - (l > 0)
        PARAMS = 16 * (4 * L + 3)

        @block.scalar
        def _(act):
            a = nc.scalar
            own = [0]

            def link(ins):
                own[0] += 1
                ins.then_inc(sem("act_chain"), 1)
                act.wait_ge(sem("act_chain"), own[0])

            def hi(first, count=1):
                for n in range(first, first + count):
                    if n % 2 == 0:
                        act.wait_ge(landed[raw_slot(n // 2)], 16 * raw_uses(n // 2))
                    if n >= RING:
                        act.wait_ge(used, n - RING + 1)
                    a.copy(w_hi[slot_in(n)][:], piece_src(n)).then_inc(hi_done, 1)

            def sum_squares(h):
                for b in range(TB):
                    ins = a.activation(xn[:, b, HALVES[h]], x_sb[:, b, HALVES[h]], ACT.Square,
                                       accum_out=stat[:, 2 * h + b:2 * h + b + 1])
                if h == 1:
                    ins.then_inc(sem("squares"), 1)

            def inv_root(stage, name):
                c = slice(*COLS[name])
                act.wait_ge(sem("variance"), stage)
                link(a.activation(rstd[:, c], stat[:, c], ACT.Ln))
                a.activation(rstd[:, c], rstd[:, c], ACT.Exp, scale=-0.5).then_inc(sem("rstd"), 1)

            def turn_hi(done, dst, c, bank_):
                act.wait_ge(sem("turned"), done + 1)
                a.copy(dst[:, 2 * c:2 * c + 2, :], bank(bank_)).then_inc(sem("turn_hi"), 1)

            def mixer_act(l):
                n0, o0 = seg[f"in{l}"], seg[f"out{l}"]
                assert o0 == n0 + N_IN
                a.preload_act_table_set("natural_log_exp_and_others")
                if l:
                    hi(n0, 3)
                for h in range(2):
                    if l == 0:
                        act.wait_ge(sem(f"x_landed{h}"), 16)
                    else:
                        act.wait_ge(sem("x_added"), 4 * 2 * l - 2 + 2 * h)
                    sum_squares(h)
                inv_root(STAGE(l, "mix"), "mix")
                if l == 0:
                    hi(n0)
                for c in range(4):
                    turn_hi(TURNS(l, "mix") - 4 + c, mixer_hT[0], c, 4 + c)
                    if l == 0 and c == 0:
                        hi(n0 + 1)
                if l == 0:
                    hi(n0 + 2)
                hi(n0 + 3, 3)
                if l == 0:
                    act.wait_ge(sem("params"), PARAMS)
                    a.activation(dt_par[:, 1], dt_par[:, 1], ACT.Exp).then_inc(sem("exp_a"), 1)
                    a.copy(w_dt[0][:], w_dt_raw[:]).then_inc(sem("w_dt_hi"), 1)
                    act.wait_ge(sem("par_turned"), 1)
                    a.copy(conv_par[:], bank(5)[:, 0, 0:ROWS]).then_inc(sem("par_out"), 1)
                a.preload_act_table_set("silu_and_others")

                def move(grp):
                    act.wait_ge(used, n0 + 4 * grp + 4)
                    src = bank(2 * (grp % 2), 2)
                    tiles = src.rearrange("p b (c t) -> p (b c) t", c=2)
                    if grp < 2:
                        ins = a.copy(xbc[:, 4 * grp:4 * grp + 4, PAD:], tiles)
                    elif grp == 2:
                        ins = a.activation(z_act[:], src, ACT.Silu)
                    elif grp == 3:
                        ins = a.mul(qT[:], tiles, float(HD) ** -0.5)
                    elif grp == 4:
                        ins = a.copy(kT[:], tiles)
                    else:
                        ins = a.copy(v_tok[:], src)
                    ins.then_inc(sem("moved"), 1)

                def silu_conv(h):
                    act.wait_ge(sem("convolved"), 2 * l + h + 1)
                    a.activation(conv[:, 4 * h:4 * h + 4], conv[:, 4 * h:4 * h + 4], ACT.Silu
                                 ).then_inc(sem("conv_act"), 1)

                hi(n0 + 6, 2)
                move(0)
                hi(n0 + 8, 3)
                silu_conv(0)
                hi(n0 + 11)
                move(1)
                hi(n0 + 12)
                act.wait_ge(sem("dt_mm"), l + 1)
                a.copy(dt_t[0:HEADS, :], psum[0:HEADS, 4, 0:T]).then_inc(sem("dt_t"), 1)
                hi(n0 + 13, 3)
                silu_conv(1)
                move(2)
                a.preload_act_table_set("natural_log_exp_and_others")
                act.wait_ge(sem("dt_raw"), l + 1)
                link(a.activation(dt_a[:], dt_v[:], ACT.Abs))
                link(a.activation(dt_a[:], dt_a[:], ACT.Exp, scale=-1.0))
                a.activation(dt_a[:], dt_a[:], ACT.Ln, bias=1.0).then_inc(sem("dt_rest"), 1)
                hi(n0 + 16, 2)
                act.wait_ge(sem("tokened"), l + 1)
                a.copy(x_tok[:], bank(4, 2)).then_inc(sem("x_tok"), 1)
                hi(n0 + 18, 2)
                move(3)
                hi(n0 + 20, 2)
                for c in range(TB):
                    act.wait_ge(sem("segsum"), TB * l + c + 1)
                    a.activation(decay[:, c].rearrange("p h t -> p (h t)"),
                                 bank(4 + 2 * c, 2).rearrange("p b t -> p (b t)"), ACT.Exp).then_inc(sem("decay"), 1)
                hi(n0 + 22, 2)
                act.wait_ge(sem("stated"), l + 1)
                a.copy(state[:], bank(7)[:, 0]).then_inc(sem("state_out"), 1)
                a.activation(e_cum[:], psum[:, 4, 0:HEADS], ACT.Exp).then_inc(sem("e_cum"), 1)
                move(4)

                def rest_part(p):
                    act.wait_ge(sem("scores"), 4 * l + p + 1)
                    z = bank(ZB[p % 2], 2)[:, :, 0:W3]
                    r = rest[p % 2]
                    if p >= 2:
                        act.wait_ge(sem("soft"), 4 * l + p - 1)
                    link(a.activation(r[:], z, ACT.Abs))
                    link(a.activation(r[:], r[:], ACT.Exp, scale=-1.0))
                    a.activation(r[:], r[:], ACT.Ln, bias=1.0).then_inc(sem("rest"), 1)

                def prob_part(p):
                    act.wait_ge(sem("cummed"), 4 * l + p + 1)
                    if p >= 2:
                        act.wait_ge(sem("pv"), 4 * l + p - 1)
                    a.activation(prob[p % 2][:], bank(ZB[p % 2], 2)[:, :, 0:W3], ACT.Exp
                                 ).then_inc(sem("prob"), 1)

                def part_squares(lo_, w, name):
                    col = COLS[name][0]
                    for b in range(TB):
                        for f in range(AW // w):
                            at_ = lo_ + f * w
                            ins = a.activation(xn[:, b, at_:at_ + w], mix[:, b, at_:at_ + w], ACT.Square,
                                               accum_out=stat[:, col:col + 1])
                            col += 1
                    ins.then_inc(sem("squares"), 1)

                rest_part(0)
                hi(n0 + 24, 2)
                rest_part(1)
                prob_part(0)
                hi(n0 + 26, 2)
                rest_part(2)
                move(5)
                act.wait_ge(sem("y_done"), TB * (l + 1))
                part_squares(AW, GW, "ssd")
                prob_part(1)
                inv_root(STAGE(l, "ssd"), "ssd")
                rest_part(3)
                prob_part(2)
                for c in range(2):
                    turn_hi(TURNS(l, "ssd") - 2 + c, mixer_hT[0], 2 + c, 2 + c)
                hi(n0 + 28)
                prob_part(3)
                hi(n0 + 29)
                act.wait_ge(sem("pv"), 4 * (l + 1))
                link(a.copy(mix[:, :, 0:AW], bank(4, 2)))
                part_squares(0, AW, "attn")
                inv_root(STAGE(l, "attn"), "attn")
                hi(n0 + 30)
                for c in range(2):
                    turn_hi(TURNS(l, "attn") - 2 + c, mixer_hT[0], c, 4 + c)
                hi(n0 + 31)

            mixer_act(0)

            d0 = seg["dense"]

            def turn_gain_hi(c):
                act.wait_ge(sem("turned"), TURNS(0, "ffn") - 4 + c + 1)
                for k in range(2 * c, 2 * c + 2):
                    ins = a.activation(dense_hT[0][:, k, :], psum[:, 2 + c, k % 2 * T:k % 2 * T + T], ACT.Copy,
                                       scale=ffn_gain(0, k))
                ins.then_inc(sem("turn_hi"), 1)

            hi(d0, 2)
            for h in range(2):
                turn_gain_hi(2 * h)
                turn_gain_hi(2 * h + 1)
                act.wait_ge(sem("x_added"), 2 * h + 2)
                sum_squares(h)
                if h == 0:
                    hi(d0 + 2)
            inv_root(STAGE(0, "ffn"), "ffn")
            act.wait_ge(sem("rstd"), STAGE(0, "ffn"))
            a.preload_act_table_set("silu_and_others")
            hi(d0 + 3)

            def a_hi(k, src, dst):
                act.wait_ge(sem("hidden_turned"), k + 1)
                a.copy(dst, src).then_inc(sem("a_hi"), 1)

            def gate_silu(pieces, src):
                act.wait_ge(used, pieces)
                a.activation(act_h[:], src, ACT.Silu).then_inc(sem("silu"), 1)

            for j in range(DSTEPS):
                base = d0 + (0 if j == 0 else 4 + 6 * (j - 1))
                if j >= 1:
                    hi(base, 6)
                    a_hi(j - 1, bank(2)[:, 0].rearrange("p (c t) -> p c t", c=2), dense_aT[0][:])
                act.wait_ge(used, base + 2)
                for b in range(TB):
                    ins = a.activation(dense_h[:, b], psum[:, (0, 3)[j % 2], b * DS:(b + 1) * DS], ACT.Silu,
                                       scale=rstd[:, b:b + 1])
                ins.then_inc(sem("silu"), 1)
            hi(d0 + N_DENSE - 2, 2)
            a_hi(DSTEPS - 1, bank(2)[:, 0].rearrange("p (c t) -> p c t", c=2), dense_aT[0][:])

            mixer_act(1)

            for h in range(2):
                for c in range(2 * h, 2 * h + 2):
                    act.wait_ge(sem("turned"), TURNS(1, "ffn") - 4 + c + 1)
                    a.copy(r_hT[:, 2 * c:2 * c + 2, :], bank(2 + c)).then_inc(sem("router_hT"), 1)
                act.wait_ge(sem("x_added"), 10 + 2 * h)
                sum_squares(h)
                if h == 0:
                    hi(M0, 3)
            inv_root(STAGE(1, "ffn"), "ffn")
            act.wait_ge(sem("logits_t"), 1)
            a.copy(logit_t[0:E, :], psum[0:E, 0, 0:T]).then_inc(sem("logit_t"), 1)
            hi(M0 + 3, RING - 3)
            act.wait_ge(sem("logit_rel"), 1)
            a.activation(e_gate[:], logit[:], ACT.Exp).then_inc(sem("e_gate"), 1)
            a.preload_act_table_set("silu_and_others")

            def gather_hi(k, half):
                act.wait_ge(sem("gathered"), k)
                a.copy(g_hT[0][:, 4 * half:4 * half + 4, :],
                       bank(GATHER_BANK[half])[:, 0].rearrange("p (c t) -> p c t", c=4)
                       ).then_inc(sem("gather_hi"), 1)

            for half in range(2):
                gather_hi(1 + half, half)
            act.wait_ge(sem("planned"), 1)
            act.wait_ge(sem("routed"), 2)
            n_items = act.value_load(plan[0:1, 0:1], min_val=E, max_val=E + MORE)

            def y_hi(i):
                act.wait_ge(used, M0 + i * N_ITEM)
                act.wait_ge(sem("slot_gate"), i)
                for h in range(2):
                    a.activation(y[0][:, HALVES[h]], bank(4 + h)[:, 0], ACT.Copy, scale=slot_gate[:, 0:1]
                                 ).then_inc(sem("turn_hi"), 1)

            with act.Fori(0, n_items) as i:
                def hi_m(q):
                    n = M0 + q
                    if n % 2 == 0:
                        first = M0 + q % N_ITEM
                        act.wait_ge(landed[raw_slot(n // 2)], 16 * raw_uses(first // 2)
                                    + (i + q // N_ITEM) * (16 * (ITEM_BLOCKS // RAW_RING)))
                    act.wait_ge(used, n - 5 + i * N_ITEM)
                    a.copy(w_hi[q % RING][:], piece_src(n)).then_inc(hi_done, 1)

                KD = DSTEPS
                for q in range(RING, N_ITEM):
                    hi_m(q)
                    if q == RING:
                        with act.If(i > 0):
                            y_hi(i)
                        with act.Else():
                            pass
                    if q == 8:
                        gate_silu(M0 + 4 + i * N_ITEM, bank(0)[:, 0])
                    if q > 8 and q % 12 == 2 and q < N_ITEM - 8:
                        j = (q - 14) // 12 + 1
                        a_hi(KD + j - 1 + i * ESTEPS, bank(6)[:, 0].rearrange("p (c t) -> p c t", c=4), aT[0][:])
                        gate_silu(M0 + q - 2 + i * N_ITEM, bank(j % 2)[:, 0])
                        if j == 3:
                            act.wait_ge(sem("place_ps"), 1 + i)
                            a.copy(place[:], bank(7)[:, 0, 0:T]).then_inc(sem("place"), 1)
                    if q == N_ITEM - 3:
                        a_hi(KD + ESTEPS - 1 + i * ESTEPS, bank(6)[:, 0].rearrange("p (c t) -> p c t", c=4),
                             aT[0][:])
                with act.If(n_items > i + 1):
                    for half in range(2):
                        gather_hi(3 + half + i * 2, half)
                    for q in range(N_ITEM, N_ITEM + RING):
                        hi_m(q)
                with act.Else():
                    pass
            a.preload_act_table_set("natural_log_exp_and_others")
            y_hi(n_items)
            for h in range(2):
                act.wait_ge(sem("x_added"), 10 + 2 * h + 4 * n_items)
                sum_squares(h)
            inv_root(FINAL, "mix")

        @block.vector
        def _(dve):
            v = nc.vector
            own = [0]

            def link(ins):
                own[0] += 1
                ins.then_inc(sem("dve_chain"), 1)
                dve.wait_ge(sem("dve_chain"), own[0])

            def lo(first, count=1):
                for n in range(first, first + count):
                    dve.wait_ge(hi_done, n + 1)
                    v.tensor_tensor(w_lo[slot_in(n)][:], piece_src(n), w_hi[slot_in(n)][:].bitcast(F32),
                                    ALU.subtract).then_inc(split, 1)

            def variance(stage, name, n):
                c = slice(*COLS[name])
                dve.wait_ge(sem("squares"), stage)
                if n == D:
                    link(v.tensor_tensor(stat[:, c], stat[:, c], stat[:, TB:2 * TB], ALU.add))
                v.tensor_scalar(stat[:, c], stat[:, c], 1.0 / n, EPS, ALU.mult, ALU.add).then_inc(sem("variance"), 1)

            def scale(stage, gains, src, name, lo_, w):
                dve.wait_ge(sem("rstd"), stage)
                if gains:
                    dve.wait_ge(sem("gain"), 16 * gains)
                else:
                    dve.wait_ge(sem("first_gain"), 16)
                first, end = COLS[name]
                parts = (end - first) // TB
                for b in range(TB):
                    for f in range(parts):
                        c = slice(lo_ + f * w, lo_ + (f + 1) * w)
                        col = first + b * parts + f
                        ins = v.scalar_tensor_tensor(out=xn[:, b, c], in0=src[:, b, c], scalar=rstd[:, col:col + 1],
                                                     in1=gain[:, c], op0=ALU.mult, op1=ALU.mult)
                ins.then_inc(sem("normed"), 1)

            def scale_half(stage, gains, h):
                dve.wait_ge(sem("rstd"), stage)
                if gains:
                    dve.wait_ge(sem("gain"), 16 * gains)
                else:
                    dve.wait_ge(sem("first_gain"), 16)
                for b in range(TB):
                    c = HALVES[h]
                    ins = v.scalar_tensor_tensor(out=xn[:, b, c], in0=x_sb[:, b, c], scalar=rstd[:, b:b + 1],
                                                 in1=gain[:, c], op0=ALU.mult, op1=ALU.mult)
                ins.then_inc(sem("normed" if h else "half_normed"), 1)

            def add_to_x(h, banks):
                for b in range(TB):
                    xs = x_sb[:, b, HALVES[h]]
                    v.tensor_tensor(xs, xs, bank(banks[b])[:, 0], ALU.add).then_inc(sem("x_added"), 1)

            def turn_lo(done, c, bank_):
                k = slice(2 * c, 2 * c + 2)
                dve.wait_ge(sem("turn_hi"), done + 1)
                v.tensor_tensor(mixer_hT[1][:, k, :], bank(bank_)[:, 0].rearrange("p (c t) -> p c t", c=2),
                                mixer_hT[0][:, k, :].bitcast(F32), ALU.subtract).then_inc(sem("turn_lo"), 1)

            def conv_half(l, h):
                dve.wait_ge(sem("moved"), 6 * l + h + 1)
                par = lambda k, c: conv_par[:, l * NCP + k * CT + c:l * NCP + k * CT + c + 1]
                for k in range(TAPS):
                    for c in range(4 * h, 4 * h + 4):
                        src = xbc[:, c, k:k + T]
                        if k == 0:
                            ins = v.tensor_scalar(conv[:, c], src, par(0, c), par(TAPS, c), ALU.mult, ALU.add)
                        else:
                            ins = v.scalar_tensor_tensor(out=conv[:, c], in0=src, scalar=par(k, c), in1=conv[:, c],
                                                         op0=ALU.mult, op1=ALU.add)
                    if k < TAPS - 1:
                        link(ins)
                ins.then_inc(sem("convolved"), 1)

            def mixer_dve(l):
                n0, o0 = seg[f"in{l}"], seg[f"out{l}"]
                heads = lambda t: t.rearrange("p (h d) -> p h d", h=HEADS)
                if l == 0:
                    dve.wait_ge(sem("x_landed0"), 16)
                    dve.wait_ge(sem("x_landed1"), 16)
                variance(STAGE(l, "mix"), "mix", D)
                for h in range(2):
                    scale_half(STAGE(l, "mix"), GAINS(l, "mix"), h)
                if l == 0:
                    lo(n0, 1)
                for c in range(4):
                    turn_lo(TURNS(l, "mix") - 4 + c, c, 4 + c)
                    if l == 0 and c == 0:
                        lo(n0 + 1)
                lo(n0 + 2, 2)
                v.memset(xbc[:, :, 0:PAD], 0.0).then_inc(sem("padded"), 1)
                if l == 0:
                    dve.wait_ge(sem("w_dt_hi"), 1)
                    v.tensor_tensor(w_dt[1][:], w_dt_raw[:], w_dt[0][:].bitcast(F32), ALU.subtract
                                    ).then_inc(sem("w_dt_lo"), 1)
                lo(n0 + 4, 4)
                dve.wait_ge(sem("par_out"), 1)
                dve.wait_ge(sem("padded"), l + 1)
                conv_half(l, 0)
                lo(n0 + 8, 4)
                conv_half(l, 1)
                dve.wait_ge(sem("dt_ps"), l + 1)
                bias = dt_par[:, 0, l, :].unsqueeze(1).broadcast_to([P, TB, HEADS])
                v.tensor_tensor(dt_v[:], psum[:, 5, 0:TB * HEADS].rearrange("p (b h) -> p b h", b=TB), bias,
                                ALU.add).then_inc(sem("dt_raw"), 1)
                lo(n0 + 12, 4)
                dve.wait_ge(sem("dt_rest"), l + 1)
                link(v.scalar_tensor_tensor(out=dt_b[:], in0=dt_v[:], scalar=0.0, in1=dt_a[:], op0=ALU.max,
                                            op1=ALU.add))
                dve.wait_ge(sem("exp_a"), 1)
                link(v.scalar_tensor_tensor(out=dA[:], in0=dt_b[:], scalar=-1.0,
                                            in1=dt_par[:, 1, l, :].unsqueeze(1).broadcast_to([P, TB, HEADS]),
                                            op0=ALU.mult, op1=ALU.mult))
                for c in range(TB):
                    v.tensor_tensor(seg_rhs[:, c], tri_le[:].unsqueeze(1).broadcast_to([P, HEADS, P]),
                                    dA[:, c].unsqueeze(2).broadcast_to([P, HEADS, P]), ALU.mult
                                    ).then_inc(sem("seg_rhs"), 1)
                lo(n0 + 16, 2)
                dve.wait_ge(sem("tokened"), l + 1)
                v.tensor_copy(b_tok[:], bank(6)[:, 0, 0:GROUPS * P].rearrange("p (g n) -> p g n", g=GROUPS)
                              ).then_inc(sem("b_tok"), 1)
                dve.wait_ge(sem("cb_ps"), l + 1)
                link(v.tensor_tensor(cb_m[:].rearrange("p c g t -> p (c g) t"),
                                     bank(7)[:, 0].rearrange("p (c t) -> p c t", c=TB * GROUPS),
                                     tri_le[:].unsqueeze(1).broadcast_to([P, TB * GROUPS, P]), ALU.mult))
                dve.wait_ge(sem("x_tok"), l + 1)
                for c in range(TB):
                    ins = v.tensor_tensor(heads(x_dt[:, c]), heads(x_tok[:, c]),
                                          dt_b[:, c].unsqueeze(2).broadcast_to([P, HEADS, HD]), ALU.mult)
                ins.then_inc(sem("x_dt"), 1)
                lo(n0 + 18, 4)
                dve.wait_ge(sem("decay"), TB * l + 1)
                dve.wait_ge(sem("x_dt"), l + 1)
                v.tensor_tensor(heads(x_state[:]), heads(x_dt[:, 0]),
                                decay[:, 0, :, P - 1:P].broadcast_to([P, HEADS, HD]), ALU.mult
                                ).then_inc(sem("x_state"), 1)
                dve.wait_ge(sem("x_state"), l + 1)
                for c in range(TB):
                    dve.wait_ge(sem("decay"), TB * l + c + 1)
                    d4 = decay[:, c].rearrange("p (g r) t -> p g r t", g=GROUPS)
                    v.tensor_tensor(d4, d4, cb_m[:, c].unsqueeze(2).broadcast_to([P, GROUPS, HG, P]), ALU.mult
                                    ).then_inc(sem("masked_decay"), 1)
                lo(n0 + 22, 2)
                for c in range(TB):
                    y = mix[:, c, AW:2 * AW]
                    link(v.tensor_tensor(heads(y), heads(x_tok[:, c]),
                                         dt_par[:, 2, l, :].unsqueeze(2).broadcast_to([P, HEADS, HD]), ALU.mult))
                    dve.wait_ge(sem("y_diag"), TB * l + c + 1)
                    link(v.tensor_tensor(y, y, bank(5 + c)[:, 0], ALU.add))
                    if c == 1:
                        dve.wait_ge(sem("y_off"), l + 1)
                        dve.wait_ge(sem("e_cum"), l + 1)
                        link(v.tensor_tensor(heads(y_off[:]), heads(bank(7)[:, 0]),
                                             e_cum[:].unsqueeze(2).broadcast_to([P, HEADS, HD]), ALU.mult))
                        link(v.tensor_tensor(y, y, y_off[:], ALU.add))
                    dve.wait_ge(sem("moved"), 6 * l + 3)
                    v.tensor_tensor(y, y, z_act[:, c], ALU.mult).then_inc(sem("y_done"), 1)

                def soft_part(p):
                    dve.wait_ge(sem("rest"), 4 * l + p + 1)
                    if p >= 2:
                        dve.wait_ge(sem("cummed"), 4 * l + p - 1)
                    s = soft[p % 2]
                    link(v.scalar_tensor_tensor(out=s[:], in0=bank(ZB[p % 2], 2)[:, :, 0:W3], scalar=0.0,
                                                in1=rest[p % 2][:], op0=ALU.max, op1=ALU.add))
                    for h in range(2):
                        d = diag(s[:, h])
                        ins = v.tensor_tensor(d, d, tri_lt[:].unsqueeze(1).broadcast_to([P, 2, P]), ALU.mult)
                    ins.then_inc(sem("soft"), 1)

                def mask_part(p):
                    dve.wait_ge(sem("prob"), 4 * l + p + 1)
                    for h in range(2):
                        d = diag(prob[p % 2][:, h])
                        ins = v.scalar_tensor_tensor(out=d, in0=d, scalar=2.0,
                                                     in1=tri_lt[:].unsqueeze(1).broadcast_to([P, 2, P]),
                                                     op0=ALU.min, op1=ALU.mult)
                    ins.then_inc(sem("masked"), 1)

                soft_part(0)
                lo(n0 + 24, 2)
                soft_part(1)
                mask_part(0)
                lo(n0 + 26, 2)
                soft_part(2)
                variance(STAGE(l, "ssd"), "ssd", GW)
                mask_part(1)
                scale(STAGE(l, "ssd"), GAINS(l, "ssd"), mix, "ssd", AW, GW)
                soft_part(3)
                mask_part(2)
                for c in range(2):
                    turn_lo(TURNS(l, "ssd") - 2 + c, 2 + c, 2 + c)
                lo(n0 + 28)
                mask_part(3)
                lo(n0 + 29)
                variance(STAGE(l, "attn"), "attn", AW)
                scale(STAGE(l, "attn"), GAINS(l, "attn"), mix, "attn", 0, AW)
                lo(n0 + 30)
                for c in range(2):
                    turn_lo(TURNS(l, "attn") - 2 + c, c, 4 + c)
                lo(n0 + 31)
                dve.wait_ge(used, o0 + 6)
                add_to_x(0, (OUT_BANK[0], OUT_BANK[0] + 1))

            def a_lo(k, src, dst_hi, dst_lo):
                dve.wait_ge(sem("a_hi"), k + 1)
                v.tensor_tensor(dst_lo, src, dst_hi.bitcast(F32), ALU.subtract).then_inc(sem("hidden_split"), 1)

            def add_second_half(l):
                dve.wait_ge(used, seg[f"out{l}"] + 8)
                add_to_x(1, (OUT_BANK[1], OUT_BANK[1] + 1))

            def glu(k, pieces, up):
                dve.wait_ge(sem("silu"), k + 1)
                dve.wait_ge(used, pieces)
                v.tensor_tensor(act_h[:], act_h[:], up, ALU.mult).then_inc(sem("hidden"), 1)

            mixer_dve(0)

            d0 = seg["dense"]

            def turn_gain_lo(c):
                dve.wait_ge(sem("turn_hi"), TURNS(0, "ffn") - 4 + c + 1)
                for k in range(2 * c, 2 * c + 2):
                    ins = v.scalar_tensor_tensor(out=dense_hT[1][:, k, :],
                                                 in0=psum[:, 2 + c, k % 2 * T:k % 2 * T + T], scalar=ffn_gain(0, k),
                                                 in1=dense_hT[0][:, k, :].bitcast(F32), op0=ALU.mult,
                                                 op1=ALU.subtract)
                ins.then_inc(sem("turn_lo"), 1)

            lo(d0, 2)
            turn_gain_lo(0)
            turn_gain_lo(1)
            add_second_half(0)
            turn_gain_lo(2)
            turn_gain_lo(3)
            lo(d0 + 2)
            variance(STAGE(0, "ffn"), "ffn", D)
            lo(d0 + 3)
            dve.wait_ge(sem("rstd"), STAGE(0, "ffn"))

            def dense_glu(j, pieces):
                dve.wait_ge(sem("silu"), j + 1)
                dve.wait_ge(used, pieces)
                for b in range(TB):
                    ins = v.scalar_tensor_tensor(out=dense_h[:, b], in0=psum[:, 1, b * DS:(b + 1) * DS],
                                                 scalar=rstd[:, b:b + 1], in1=dense_h[:, b], op0=ALU.mult,
                                                 op1=ALU.mult)
                ins.then_inc(sem("hidden"), 1)

            two = lambda ap: ap.rearrange("p (b n) -> p b n", b=2)
            for j in range(1, DSTEPS):
                base = d0 + 4 + 6 * (j - 1)
                lo(base, 2)
                dense_glu(j - 1, base - (0 if j == 1 else 2))
                lo(base + 2, 4)
                a_lo(j - 1, two(bank(2)[:, 0]), dense_aT[0][:], dense_aT[1][:])
            lo(d0 + N_DENSE - 2, 2)
            dense_glu(DSTEPS - 1, d0 + N_DENSE - 4)
            a_lo(DSTEPS - 1, two(bank(2)[:, 0]), dense_aT[0][:], dense_aT[1][:])
            lo(seg["in1"], 1)
            dve.wait_ge(sem("dense_half"), 1)
            add_to_x(0, (4, 6))
            dve.wait_ge(used, d0 + N_DENSE)
            add_to_x(1, (5, 7))
            lo(seg["in1"] + 1)
            mixer_dve(1)

            def make_pick(i):
                for b in range(TB):
                    ins = v.tensor_scalar(pick[:, b], slots[:], slot_t[:, b, bass.ds(i, 1)], None, ALU.is_equal)
                ins.then_inc(sem("pick"), 1)

            def gather_lo(k, half):
                dve.wait_ge(sem("gather_hi"), k)
                h = slice(4 * half, 4 * half + 4)
                v.tensor_tensor(g_hT[1][:, h, :], bank(GATHER_BANK[half])[:, 0].rearrange("p (c t) -> p c t", c=4),
                                g_hT[0][:, h, :].bitcast(F32), ALU.subtract).then_inc(sem("gather_lo"), 1)

            dve.wait_ge(sem("router_in"), 16)
            gains = conv_par[:, L * NCP + KT:L * NCP + 2 * KT]
            v.tensor_tensor(router[:], router[:], gains.unsqueeze(2).broadcast_to([P, KT, E]), ALU.mult
                            ).then_inc(sem("router_gain"), 1)
            add_second_half(1)
            lo(M0, 3)
            variance(STAGE(1, "ffn"), "ffn", D)
            dve.wait_ge(sem("consts"), ROUTE_CONSTS)
            dve.wait_ge(sem("logits"), 1)
            wide = [P, TB, E, E]
            link(v.tensor_tensor(logit[:], psum[:, 2, 0:TB * E].rearrange("p (b e) -> p b e", b=TB),
                                 rstd[:, 0:TB].unsqueeze(2).broadcast_to([P, TB, E]), ALU.mult))
            mine, other = logit[:].unsqueeze(3).broadcast_to(wide), logit[:].unsqueeze(2).broadcast_to(wide)
            v.tensor_tensor(cmp_a[:], mine, other, ALU.is_lt)
            link(v.tensor_tensor(cmp_b[:], mine, other, ALU.is_equal))
            link(v.tensor_tensor(cmp_b[:], cmp_b[:], low8[:].unsqueeze(1).broadcast_to(wide), ALU.mult))
            link(v.tensor_tensor(cmp_a[:], cmp_a[:], cmp_b[:], ALU.add))
            link(v.tensor_reduce(rank[:], cmp_a[:], AX.X, ALU.add))
            v.tensor_scalar(chosen[:], rank[:], TOPK - 0.5, None, ALU.is_lt).then_inc(sem("chosen"), 1)
            link(v.tensor_reduce(r_max[:], logit[:], AX.X, ALU.max))
            v.tensor_tensor(logit[:], logit[:], r_max[:].unsqueeze(2).broadcast_to([P, TB, E]), ALU.subtract
                            ).then_inc(sem("logit_rel"), 1)
            v.memset(slot_t[:, :, E:], -1.0)
            v.memset(gate_t[:, :, E:], 0.0)
            scale_half(STAGE(1, "ffn"), GAINS(1, "ffn"), 0)
            dve.wait_ge(sem("chosen"), 1)
            dve.wait_ge(sem("positions"), 1)
            pos = psum[:, 1, 0:TB * E].rearrange("p (b e) -> p b e", b=TB)
            link(v.scalar_tensor_tensor(out=pos1[:], in0=pos, scalar=1.0, in1=chosen[:], op0=ALU.add, op1=ALU.mult))
            v.tensor_scalar(slot_t[:, :, 0:E], pos1[:], -1.0, None, ALU.add)
            link(v.tensor_scalar(over[:], psum[:, 1, TB * E:(TB + 1) * E], float(P), None, ALU.is_gt))
            make_pick(0)
            scale_half(STAGE(1, "ffn"), GAINS(1, "ffn"), 1)
            link(v.tensor_tensor(cmp_a[:, 0], over[:].unsqueeze(1).broadcast_to([P, E, E]), low8[:], ALU.mult))
            link(v.tensor_reduce(o_rank[:], cmp_a[:, 0], AX.X, ALU.add))
            v.tensor_reduce(plan_f[:, 0:1], over[:], AX.X, ALU.add)
            each = [P, MORE, E]
            link(v.tensor_tensor(sel[:], o_rank[:].unsqueeze(1).broadcast_to(each),
                                 e_ids[:, 0:MORE].unsqueeze(2).broadcast_to(each), ALU.is_equal))
            link(v.tensor_tensor(sel[:], sel[:], over[:].unsqueeze(1).broadcast_to(each), ALU.mult))
            link(v.tensor_tensor(tmp_e[:, 0], e_ids[:].unsqueeze(1).broadcast_to(each), sel[:], ALU.mult))
            link(v.tensor_reduce(plan_f[:, 1:1 + MORE], tmp_e[:, 0], AX.X, ALU.add))
            link(v.tensor_scalar(plan_f[:, 0:1], plan_f[:, 0:1], float(E), None, ALU.add))
            v.tensor_copy(plan[:], plan_f[:]).then_inc(sem("planned"), 1)
            lo(M0 + 3)
            gather_lo(1, 0)
            dve.wait_ge(sem("e_gate"), 1)
            link(v.tensor_tensor(e_gate[:], e_gate[:], chosen[:], ALU.mult))
            link(v.tensor_reduce(r_max[:], e_gate[:], AX.X, ALU.add))
            link(v.reciprocal(r_max[:], r_max[:]))
            link(v.tensor_tensor(gate_t[:, :, 0:E], e_gate[:], r_max[:].unsqueeze(2).broadcast_to([P, TB, E]),
                                 ALU.mult))
            link(v.tensor_scalar(pos1[:], pos1[:], -1.0 - P, None, ALU.add))
            each = [P, TB, MORE, E]
            both = sel[:].unsqueeze(1).broadcast_to(each)
            for src, dst in ((pos1[:], slot_t), (gate_t[:, :, 0:E], gate_t)):
                link(v.tensor_tensor(tmp_e[:], src.unsqueeze(2).broadcast_to(each), both, ALU.mult))
                v.tensor_reduce(dst[:, :, E:E + MORE], tmp_e[:], AX.X, ALU.add).then_inc(sem("routed"), 1)
                dve.wait_ge(sem("routed"), 1 + (dst is gate_t))

            gather_lo(2, 1)
            lo(M0 + 4, RING - 4)
            dve.wait_ge(sem("planned"), 1)
            n_items = dve.value_load(plan[0:1, 0:1], min_val=E, max_val=E + MORE)
            KD = DSTEPS
            four = lambda ap: ap.rearrange("p (c t) -> p c t", c=4)
            def y_lo(i):
                for h in range(2):
                    dve.wait_ge(sem("turn_hi"), Y_SPLIT + h - 1 + i * 2)
                    v.scalar_tensor_tensor(out=y[1][:, HALVES[h]], in0=bank(4 + h)[:, 0], scalar=slot_gate[:, 0:1],
                                           in1=y[0][:, HALVES[h]].bitcast(F32), op0=ALU.mult, op1=ALU.subtract
                                           ).then_inc(sem("turn_lo"), 1)

            def add_combined(i):
                for h in range(2):
                    dve.wait_ge(sem("turned"), COMBINED + h - 1 + i * 2)
                    add_to_x(h, (COMBINE[0][h], COMBINE[1][h]))

            with dve.Fori(0, n_items) as i:
                def lo_m(q):
                    n = M0 + q
                    dve.wait_ge(hi_done, n + 1 + i * N_ITEM)
                    v.tensor_tensor(w_lo[q % RING][:], piece_src(n), w_hi[q % RING][:].bitcast(F32), ALU.subtract
                                    ).then_inc(split, 1)

                for q in range(RING, N_ITEM):
                    lo_m(q)
                    if q == RING:
                        with dve.If(i > 0):
                            y_lo(i)
                        with dve.Else():
                            pass
                    if q == 10:
                        with dve.If(i > 0):
                            add_combined(i)
                        with dve.Else():
                            pass
                    if q == 12:
                        glu(KD + i * ESTEPS, M0 + 8 + i * N_ITEM, bank(2)[:, 0])
                    if q == 42:
                        dve.wait_ge(sem("place"), 1 + i)
                        v.tensor_copy(slot_gate[:], psum[:, 7, T:T + ITEMS][:, bass.ds(i, 1)]
                                      ).then_inc(sem("slot_gate"), 1)
                    if q >= 18 and q % 12 == 6:
                        j = (q - 18) // 12 + 1
                        glu(KD + j + i * ESTEPS, M0 + q - 2 + i * N_ITEM, bank(2 + j % 2)[:, 0])
                    if q > 8 and q % 12 == 2 and q < N_ITEM - 8:
                        j = (q - 14) // 12 + 1
                        a_lo(KD + j - 1 + i * ESTEPS, four(bank(6)[:, 0]), aT[0][:], aT[1][:])
                    if q == 60:
                        make_pick(i + 1)
                    if q == N_ITEM - 3:
                        a_lo(KD + ESTEPS - 1 + i * ESTEPS, four(bank(6)[:, 0]), aT[0][:], aT[1][:])
                with dve.If(n_items > i + 1):
                    for half in range(2):
                        gather_lo(3 + half + i * 2, half)
                    for q in range(N_ITEM, N_ITEM + RING):
                        lo_m(q)
                with dve.Else():
                    pass
            y_lo(n_items)
            add_combined(n_items)
            variance(FINAL, "mix", D)
            for h in range(2):
                scale_half(FINAL, GAINS(L, "mix"), h)

        @block.tensor
        def _(pe):
            def turn(k0, tiles, first_bank, src=xn):
                for c in range(tiles // 2):
                    for k in range(2):
                        for b in range(TB):
                            at_ = (k0 + 2 * c + k) * P
                            ins = nc.tensor.transpose(psum[:, first_bank + c, k * T + b * P:k * T + b * P + P],
                                                      src[:, b, at_:at_ + P], ident[:])
                    ins.then_inc(sem("turned"), 1)

            hi_lo = lambda n, c: [w[slot_in(n)][:].rearrange("p (k n) -> p k n", k=c) for w in (w_hi, w_lo)]

            def token_major(n, k0, kts, h, banks_of, first, last, halfway=lambda: None):
                wh, wl = hi_lo(n, kts)
                for kk in range(kts):
                    if kk == kts // 2:
                        halfway()
                    k = k0 + kk
                    for b in range(TB):
                        tok = slice(b * P, b * P + P)
                        ins = mm3(banks_of(b), h[0][:, k, tok], h[1][:, k, tok], wh[:, kk], wl[:, kk],
                                  first(k, b), last(k))
                ins.then_inc(used, 1)

            def mixer_pe(l):
                n0, o0 = seg[f"in{l}"], seg[f"out{l}"]
                if l == 0:
                    pe.wait_ge(sem("consts"), CONSTS)
                pe.wait_ge(sem("half_normed"), l + 1)
                turn(0, KT // 2, 4)
                pe.wait_ge(sem("normed"), NORMED(STAGE(l, "mix")))
                turn(KT // 2, KT // 2, 6)
                hh, hl = mixer_hT

                def project(grp, q):
                    if q == 0 and grp >= 2:
                        pe.wait_ge(sem("moved"), 6 * l + grp - 1)
                    b0, n = 2 * (grp % 2), n0 + 4 * grp + q
                    if grp == 0:
                        pe.wait_ge(sem("turn_lo"), TURNS(l, "mix") - 4 + q + 1)
                    pe.wait_ge(split, n + 1)
                    if grp in (2, 5):
                        token_major(n, 2 * q, 2, mixer_hT, lambda b: psum[:, b0 + b, :],
                                    lambda k, b: k == 0, lambda k: k == KT - 1)
                        return
                    wh, wl = hi_lo(n, 2)
                    for kk in range(2):
                        k = 2 * q + kk
                        for c in range(4):
                            ch = slice(c * P, c * P + P)
                            ins = mm3(psum[:, b0 + c // 2, (c % 2) * T:(c % 2) * T + T], wh[:, kk, ch],
                                      wl[:, kk, ch], hh[:, k], hl[:, k], k == 0 and c % 2 == 0, k == KT - 1)
                    ins.then_inc(used, 1)

                def project_group(grp):
                    for q in range(4):
                        project(grp, q)

                def scores(p):
                    if p == 0:
                        pe.wait_ge(sem("moved"), 6 * l + 5)
                    elif p == 1:
                        pe.wait_ge(sem("y_done"), TB * (l + 1))
                    else:
                        pe.wait_ge(sem("prob"), 4 * l + p - 1)
                    for s in range(2):
                        part = slice(s * HD, (s + 1) * HD)
                        ps = psum[:, ZB[p % 2] + s, :]
                        mm(ps[:, 0:T], kT[part, p, 0:P], qT[part, p, :])
                        ins = mm(ps[:, T:W3], kT[part, p, P:T], qT[part, p, P:T], start=False)
                    ins.then_inc(sem("scores"), 1)

                def cums(p):
                    pe.wait_ge(sem("soft"), 4 * l + p + 1)
                    for s in range(2):
                        ps, sf = psum[:, ZB[p % 2] + s, :], soft[p % 2][:, s]
                        mm(ps[:, 0:T], neg_ge[:], sf[:, 0:T], start=False)
                        mm(ps[:, P:T], neg_one[:], sf[:, T:W3], start=False)
                        ins = mm(ps[:, T:W3], neg_ge[:], sf[:, T:W3], start=False)
                    ins.then_inc(sem("cummed"), 1)

                def values(p):
                    if p == 0:
                        pe.wait_ge(sem("moved"), 6 * l + 6)
                    pe.wait_ge(sem("masked"), 4 * l + p + 1)
                    for s in range(2):
                        h, w = 2 * p + s, prob[p % 2][:, s]
                        col = slice(h * HD, (h + 1) * HD)
                        mm(psum[:, 4, col], w[:, 0:P], v_tok[:, 0, col])
                        mm(psum[:, 5, col], w[:, P:T], v_tok[:, 0, col], stop=False)
                        ins = mm(psum[:, 5, col], w[:, T:W3], v_tok[:, 1, col], start=False)
                    ins.then_inc(sem("pv"), 1)

                def out_piece(m):
                    n, h = o0 + m, m // 2 % 2
                    k0 = (XT if m < 4 else 0) + 2 * (m % 2)
                    pe.wait_ge(split, n + 1)
                    token_major(n, k0, 2, mixer_hT, lambda b: psum[:, OUT_BANK[h] + b, :],
                                lambda k, b: k == XT, lambda k: k == XT - 1)

                for q in range(4):
                    project(0, q)
                    if l == 0 and q == 2:
                        pe.wait_ge(sem("params"), PARAMS)
                        nc.tensor.transpose(psum[:, 5, 0:ROWS], conv_raw[:], ident[0:ROWS, 0:ROWS]
                                            ).then_inc(sem("par_turned"), 1)
                project_group(1)
                pe.wait_ge(sem("w_dt_lo"), 1)
                pe.wait_ge(sem("par_out"), 1)
                for k in range(KT):
                    ins = mm3(psum[0:HEADS, 4, 0:T], w_dt[0][:, l, k], w_dt[1][:, l, k], hh[:, k], hl[:, k],
                              k == 0, k == KT - 1)
                ins.then_inc(sem("dt_mm"), 1)
                project(2, 0)
                pe.wait_ge(sem("dt_t"), l + 1)
                for b in range(TB):
                    ins = nc.tensor.transpose(psum[:, 5, b * HEADS:(b + 1) * HEADS],
                                              dt_t[0:HEADS, b * P:(b + 1) * P], ident[0:HEADS, 0:HEADS])
                ins.then_inc(sem("dt_ps"), 1)
                for q in range(1, 4):
                    project(2, q)
                pe.wait_ge(sem("conv_act"), 2 * l + 2)
                pe.wait_ge(sem("dt_raw"), l + 1)
                for b in range(TB):
                    for c in range(XT):
                        nc.tensor.transpose(psum[:, 4 + b, c * P:c * P + P], conv[:, c, b * P:b * P + P], ident[:])
                for g in range(GROUPS):
                    ins = nc.tensor.transpose(psum[:, 6, g * P:g * P + P], conv[:, XT + g, 0:P], ident[:])
                ins.then_inc(sem("tokened"), 1)
                for c in range(TB):
                    for g in range(GROUPS):
                        at_ = (c * GROUPS + g) * P
                        ins = mm(psum[:, 7, at_:at_ + P], conv[:, XT + g, c * P:c * P + P],
                                 conv[:, XT + GROUPS + g, c * P:c * P + P])
                ins.then_inc(sem("cb_ps"), 1)
                project_group(3)
                pe.wait_ge(sem("x_tok"), l + 1)
                pe.wait_ge(sem("x_dt"), l + 1)
                for c in range(TB):
                    pe.wait_ge(sem("seg_rhs"), TB * l + c + 1)
                    for h in range(2):
                        ins = mm(psum[:, 4 + 2 * c + h, :], tri_gt[:],
                                 seg_rhs[:, c, 4 * h:4 * h + 4, :].rearrange("p h t -> p (h t)"))
                    ins.then_inc(sem("segsum"), 1)
                project_group(4)
                pe.wait_ge(sem("decay"), TB * (l + 1))
                mm(psum[:, 4, 0:HEADS], tri_le[:], dA[:, 1, :])
                pe.wait_ge(sem("b_tok"), l + 1)
                pe.wait_ge(sem("x_state"), l + 1)
                for g in range(GROUPS):
                    ins = mm(psum[:, 7, g * GW:(g + 1) * GW], b_tok[:, g, :], x_state[:, g * GW:(g + 1) * GW])
                ins.then_inc(sem("stated"), 1)
                for c in range(TB):
                    pe.wait_ge(sem("masked_decay"), TB * l + c + 1)
                    for h in range(HEADS):
                        ins = mm(psum[:, 5 + c, h * HD:(h + 1) * HD], decay[:, c, h, :],
                                 x_dt[:, c, h * HD:(h + 1) * HD])
                    ins.then_inc(sem("y_diag"), 1)
                project(5, 0)
                pe.wait_ge(sem("state_out"), l + 1)
                for g in range(GROUPS):
                    ins = mm(psum[:, 7, g * GW:(g + 1) * GW], conv[:, XT + GROUPS + g, P:2 * P],
                             state[:, g * GW:(g + 1) * GW])
                ins.then_inc(sem("y_off"), 1)
                scores(0)
                project(5, 1)
                scores(1)
                cums(0)
                project(5, 2)
                scores(2)
                project(5, 3)
                cums(1)
                values(0)
                scores(3)
                cums(2)
                pe.wait_ge(sem("normed"), NORMED(STAGE(l, "ssd")))
                turn(XT, XT, 2)
                values(1)
                cums(3)
                values(2)
                pe.wait_ge(sem("turn_lo"), TURNS(l, "ssd"))
                pe.wait_ge(sem("prob"), 4 * l + 3)
                out_piece(0)
                values(3)
                out_piece(1)
                out_piece(2)
                pe.wait_ge(sem("normed"), NORMED(STAGE(l, "attn")))
                turn(0, XT, 4)
                out_piece(3)
                for m in range(4, 7):
                    if m < 6:
                        pe.wait_ge(sem("turn_lo"), TURNS(l, "attn") - 2 + m % 2 + 1)
                    out_piece(m)
                pe.wait_ge(sem("x_added"), 8 * l + 2)
                turn(0, XT, 2, x_sb)
                out_piece(7)

            mixer_pe(0)

            d0 = seg["dense"]

            def turn_second_half():
                pe.wait_ge(sem("x_added"), 4)
                turn(XT, XT, 4, x_sb)

            for j in range(DSTEPS + 1):
                base = d0 + (0 if j == 0 else 4 + 6 * (j - 1))
                for up in range(2):
                    if j < DSTEPS:
                        for q in range(2):
                            n = base + 2 * up + q
                            halfway = lambda: None
                            if j == 0 and up == 0 and q == 0:
                                pe.wait_ge(sem("turn_lo"), TURNS(0, "ffn") - 2)
                                halfway = turn_second_half
                            elif j == 0 and up == 0:
                                pe.wait_ge(sem("turn_lo"), TURNS(0, "ffn") - 1)
                                halfway = lambda: pe.wait_ge(sem("turn_lo"), TURNS(0, "ffn"))
                            pe.wait_ge(split, n + 1)
                            ps = psum[:, 1 if up else (0, 3)[j % 2], :]
                            token_major(n, 4 * q, 4, dense_hT, lambda b: ps[:, b * DS:(b + 1) * DS],
                                        lambda k, b: k == 0 and b == 0, lambda k: k == KT - 1, halfway)
                    if up == 0 and j >= 1:
                        pe.wait_ge(sem("hidden"), j)
                        for c in range(2):
                            for b in range(TB):
                                ins = nc.tensor.transpose(
                                    psum[:, 2, c * T + b * P:c * T + b * P + P],
                                    dense_h[:, b].rearrange("p (f c) -> p c f", c=2)[:, c], ident[:])
                        ins.then_inc(sem("hidden_turned"), 1)
                if j >= 1:
                    pe.wait_ge(sem("hidden_split"), j)
                    for c in range(2):
                        n = base + (4 if j < DSTEPS else 0) + c
                        pe.wait_ge(split, n + 1)
                        wh, wl = hi_lo(n, 2)
                        last = j == DSTEPS and c == 1
                        for h in range(2):
                            for b in range(TB):
                                tok = slice(b * P, b * P + P)
                                ins = mm3(psum[:, 4 + 2 * b + h, :], dense_aT[0][:, c, tok], dense_aT[1][:, c, tok],
                                          wh[:, h], wl[:, h], j == 1 and c == 0, last)
                            if last and h == 0:
                                ins.then_inc(sem("dense_half"), 1)
                        ins.then_inc(used, 1)

            mixer_pe(1)

            pe.wait_ge(sem("router_gain"), 1)
            for k in range(KT):
                if k == XT:
                    pe.wait_ge(sem("x_added"), 12)
                    turn(XT, XT, 4, x_sb)
                if k % 2 == 0:
                    pe.wait_ge(sem("router_hT"), k // 2 + 1)
                ins = mm(psum[0:E, 0, 0:T], router[:, k], r_hT[:, k, :], k == 0, k == KT - 1)
            ins.then_inc(sem("logits_t"), 1)
            pe.wait_ge(sem("logit_t"), 1)
            for b in range(TB):
                ins = nc.tensor.transpose(psum[:, 2, b * E:(b + 1) * E], logit_t[0:E, b * P:(b + 1) * P],
                                          ident[0:E, 0:E])
            ins.then_inc(sem("logits"), 1)
            pe.wait_ge(sem("chosen"), 1)
            mm(psum[:, 1, 0:TB * E], tri_lt[:], chosen[:].rearrange("p b e -> p (b e)"), stop=False)
            mm(psum[:, 1, E:3 * E], ones[:], chosen[:, 0:1].broadcast_to([P, 2, E]), start=False, stop=False)
            mm(psum[:, 1, 2 * E:3 * E], ones[:], chosen[:, 1], start=False).then_inc(sem("positions"), 1)

            def gather(half):
                for kk in range(4):
                    k = 4 * half + kk
                    for b in range(TB):
                        ins = mm(psum[:, GATHER_BANK[half], kk * P:kk * P + P], xn[:, b, k * P:k * P + P],
                                 pick[:, b], b == 0, b == TB - 1)
                ins.then_inc(sem("gathered"), 1)

            pe.wait_ge(sem("pick"), 1)
            pe.wait_ge(sem("half_normed"), L + 1)
            gather(0)
            pe.wait_ge(sem("normed"), NORMED(STAGE(L - 1, "ffn")))
            gather(1)
            pe.wait_ge(sem("planned"), 1)
            n_items = pe.value_load(plan[0:1, 0:1], min_val=E, max_val=E + MORE)
            KD = DSTEPS

            def combine(i):
                for h in range(2):
                    pe.wait_ge(sem("turn_lo"), Y_SPLIT + h - 1 + i * 2)
                    for b in range(TB):
                        for part in range(2):
                            ins = mm(bank(COMBINE[b][h])[:, 0], place[:, b * P:b * P + P], y[part][:, HALVES[h]],
                                     part == 0, part == 1)
                    ins.then_inc(sem("turned"), 1)

            with pe.Fori(0, n_items) as i:
                def expert_up(q0, ps):
                    for q in range(4):
                        n = M0 + q0 + q
                        if q0 == 0 and q % 2 == 0:
                            pe.wait_ge(sem("gather_lo"), 1 + q // 2 + i * 2)
                        pe.wait_ge(split, n + 1 + i * N_ITEM)
                        wh, wl = hi_lo(n, 2)
                        for kk in range(2):
                            k = 2 * q + kk
                            ins = mm3(ps, g_hT[0][:, k], g_hT[1][:, k], wh[:, kk], wl[:, kk], k == 0, k == KT - 1)
                        ins.then_inc(used, 1)
                        if q0 + q == 4:
                            with pe.If(i > 0):
                                combine(i)
                            with pe.Else():
                                pass

                def turn_hidden(j):
                    pe.wait_ge(sem("hidden"), KD + j + 1 + i * ESTEPS)
                    for c in range(4):
                        ins = nc.tensor.transpose(psum[:, 6, c * P:c * P + P],
                                                  act_h[:].rearrange("p (f c) -> p c f", c=4)[:, c], ident[:])
                    ins.then_inc(sem("hidden_turned"), 1)

                def expert_down(q0, j):
                    pe.wait_ge(sem("hidden_split"), KD + j + 1 + i * ESTEPS)
                    for c in range(4):
                        n = M0 + q0 + c
                        pe.wait_ge(split, n + 1 + i * N_ITEM)
                        wh, wl = hi_lo(n, 2)
                        for h in range(2):
                            ins = mm3(psum[:, 4 + h, :], aT[0][:, c], aT[1][:, c], wh[:, h], wl[:, h],
                                      j == 0 and c == 0, j == ESTEPS - 1 and c == 3)
                        ins.then_inc(used, 1)

                for j in range(ESTEPS):
                    q0 = 0 if j == 0 else 8 + 12 * (j - 1)
                    if j == 1:
                        pe.wait_ge(sem("x_added"), 10 + i * 4)
                    expert_up(q0, psum[:, j % 2, :])
                    if j >= 1:
                        turn_hidden(j - 1)
                    if j == 1:
                        pe.wait_ge(sem("x_added"), 12 + i * 4)
                    expert_up(q0 + 4, psum[:, 2 + j % 2, :])
                    if j >= 1:
                        expert_down(q0 + 8, j - 1)
                    if j == 2:
                        for b in range(TB):
                            nc.tensor.transpose(psum[:, 7, b * P:b * P + P], pick[:, b], ident[:])
                        for b in range(TB):
                            ins = mm(psum[:, 7, T:T + ITEMS], pick[:, b], gate_t[:, b], b == 0, b == TB - 1)
                        ins.then_inc(sem("place_ps"), 1)
                turn_hidden(ESTEPS - 1)
                pe.wait_ge(sem("slot_gate"), 1 + i)
                pe.wait_ge(sem("pick"), 2 + i)
                with pe.If(n_items > i + 1):
                    gather(0)
                    gather(1)
                with pe.Else():
                    pass
                expert_down(N_ITEM - 4, ESTEPS - 1)
            combine(n_items)
    return nc


_INS = ["x", "mix_norm_g", "w_in", "conv_w", "conv_b", "dt_bias", "a_log", "d_skip", "attn_norm_g", "ssd_norm_g",
        "w_out", "ffn_norm_g", "dense_w_gate", "dense_w_up", "dense_w_down", "router_w", "moe_w_gate",
        "moe_w_up", "moe_w_down", "final_norm_g"]


def kernel(**inputs):
    import numpy as _np
    import concourse.bacc as _bacc
    from concourse import mybir as _mybir
    from concourse.bass_utils import run_bass_kernel_spmd as _run

    nc = _bacc.Bacc("TRN2", target_bir_lowering=False, num_devices=1)
    arrays, args = {}, []
    for name in _INS:
        a = _np.ascontiguousarray(inputs[name])
        arrays[f"in_{name}"] = a
        args.append(nc.dram_tensor(f"in_{name}", a.shape, _mybir.dt.from_np(a.dtype), kind="ExternalInput").ap())
    shape = inputs["x"].shape
    args.append(nc.dram_tensor("out_0", shape, _mybir.dt.float32, kind="ExternalOutput").ap())
    hybrid_trunk(nc, *args)
    r = _run(nc, [arrays], core_ids=[0])
    return r.results[0]["out_0"]
```
